# Optimizing a Trainium2 kernel written in Bass

```python
import jax, jax.numpy as jnp
from jax import lax
import numpy as np
import math
import jax
import jax.numpy as jnp

D_MODEL = 1024
BATCH = 1
SEQ = 256
DEPTH = 2

SC_WIDTH = D_MODEL // 2
SC_KERNEL = 3
MLA_HEADS = 8
MLA_NOPE = 64
MLA_ROPE = 32
MLA_V = 64
MLA_Q_RANK = 384
MLA_KV_RANK = 256
ROPE_BASE = 10000.0
Q_BLOCK = 128
IN_COLS = 3 * SC_WIDTH + MLA_Q_RANK + MLA_KV_RANK + MLA_ROPE
MIX_WIDTH = SC_WIDTH + MLA_HEADS * MLA_V
CONF_KERNEL = 31
CONF_WIDTH = D_MODEL
D_FF = 4 * D_MODEL
N_EVEN = (DEPTH + 1) // 2
N_ODD = DEPTH // 2
EPS = 1e-6


def rms_norm(x, g):
    xf = x.astype(jnp.float32)
    y = xf * lax.rsqrt(jnp.mean(xf * xf, axis=-1, keepdims=True) + EPS)
    return (y * g.astype(jnp.float32)).astype(x.dtype)

def layer_norm(x, g, b):
    xf = x.astype(jnp.float32)
    mu = jnp.mean(xf, axis=-1, keepdims=True)
    var = jnp.mean(jnp.square(xf - mu), axis=-1, keepdims=True)
    y = (xf - mu) * lax.rsqrt(var + EPS)
    return (y * g.astype(jnp.float32) + b.astype(jnp.float32)).astype(x.dtype)

def depthwise_conv(x, w):
    k = w.shape[0]
    return lax.conv_general_dilated(
        x, w[:, None, :].astype(x.dtype), window_strides=(1,),
        padding=[(k // 2, k // 2)], dimension_numbers=('NWC', 'WIO', 'NWC'),
        feature_group_count=x.shape[-1])

def apply_rope(x, cos, sin):
    half = x.shape[-1] // 2
    xf = x.astype(jnp.float32)
    x1, x2 = xf[..., :half], xf[..., half:]
    out = jnp.concatenate([x1 * cos - x2 * sin, x2 * cos + x1 * sin], axis=-1)
    return out.astype(x.dtype)

def block_attention(q, k, v):
    b, s, h, dq = q.shape
    nblk = s // Q_BLOCK
    qb = q.reshape(b, nblk, Q_BLOCK, h, dq).transpose(1, 0, 2, 3, 4)
    kf = k.astype(jnp.float32)
    scale = dq ** -0.5

    def one_block(q_blk):
        sc = jnp.einsum('bqhd,bkhd->bhqk', q_blk.astype(jnp.float32), kf) * scale
        p = jax.nn.softmax(sc, axis=-1)
        return jnp.einsum('bhqk,bkhd->bqhd', p.astype(v.dtype), v)

    o = lax.map(one_block, qb)
    return o.transpose(1, 0, 2, 3, 4).reshape(b, s, h * v.shape[-1])

def parallel_conv_mla(h, positions, w_in, sc_kernel, q_norm, w_uq, kv_norm, w_ukv, w_out):
    b, s, _ = h.shape
    proj = h @ w_in
    cuts = [SC_WIDTH, 2 * SC_WIDTH, 3 * SC_WIDTH,
            3 * SC_WIDTH + MLA_Q_RANK, 3 * SC_WIDTH + MLA_Q_RANK + MLA_KV_RANK]
    gate_b, gate_c, xs, q_lat, kv_lat, k_rope = jnp.split(proj, cuts, axis=-1)

    y_a = gate_b * depthwise_conv(gate_c * xs, sc_kernel)

    q = (rms_norm(q_lat, q_norm) @ w_uq).reshape(b, s, MLA_HEADS, MLA_NOPE + MLA_ROPE)
    q_nope, q_pe = q[..., :MLA_NOPE], q[..., MLA_NOPE:]
    kv = (rms_norm(kv_lat, kv_norm) @ w_ukv).reshape(b, s, MLA_HEADS, MLA_NOPE + MLA_V)
    k_nope, v = kv[..., :MLA_NOPE], kv[..., MLA_NOPE:]
    half = MLA_ROPE // 2
    inv_freq = 1.0 / (ROPE_BASE ** (jnp.arange(half, dtype=jnp.float32) / half))
    ang = positions.astype(jnp.float32)[..., None] * inv_freq
    cos, sin = jnp.cos(ang), jnp.sin(ang)
    q_pe = apply_rope(q_pe, cos[:, :, None, :], sin[:, :, None, :])
    k_pe = apply_rope(k_rope, cos, sin)[:, :, None, :]
    q_full = jnp.concatenate([q_nope, q_pe], axis=-1)
    k_full = jnp.concatenate(
        [k_nope, jnp.broadcast_to(k_pe, (b, s, MLA_HEADS, MLA_ROPE))], axis=-1)
    y_b = block_attention(q_full, k_full, v)

    return jnp.concatenate([y_a, y_b], axis=-1) @ w_out

def conformer_conv(h, w_pw1, b_pw1, w_dw, b_dw, ln_g, ln_b, w_pw2, b_pw2):
    u = h @ w_pw1 + b_pw1
    a, g = jnp.split(u, 2, axis=-1)
    u = a * jax.nn.sigmoid(g)
    u = depthwise_conv(u, w_dw) + b_dw
    u = jax.nn.silu(layer_norm(u, ln_g, ln_b))
    return u @ w_pw2 + b_pw2

def squared_relu_mlp(h, w1, w2):
    return jnp.square(jax.nn.relu(h @ w1)) @ w2

def first_inputs(seed: int = 0) -> dict:
    key = jax.random.key(seed)
    ks = jax.random.split(key, 24)

    def nrm(k, shape, fan_in):
        return jax.random.normal(k, shape, jnp.float32) * (fan_in ** -0.5)

    def gain(k, shape):
        return 1.0 + 0.05 * jax.random.normal(k, shape, jnp.float32)

    def bias(k, shape):
        return 0.02 * jax.random.normal(k, shape, jnp.float32)

    x = jax.random.normal(ks[0], (BATCH, SEQ, D_MODEL), jnp.float32)
    offsets = jax.random.randint(ks[1], (BATCH, 1), 0, SEQ, dtype=jnp.int32)
    positions = jnp.arange(SEQ, dtype=jnp.int32)[None, :] + offsets
    return {
        "x": x,
        "positions": positions,
        "sandwich_gains": gain(ks[2], (DEPTH, 4, D_MODEL)),
        "even_w_in": nrm(ks[3], (N_EVEN, D_MODEL, IN_COLS), D_MODEL),
        "even_sc_kernel": nrm(ks[4], (N_EVEN, SC_KERNEL, SC_WIDTH), SC_KERNEL),
        "even_q_norm": gain(ks[5], (N_EVEN, MLA_Q_RANK)),
        "even_w_uq": nrm(ks[6], (N_EVEN, MLA_Q_RANK, MLA_HEADS * (MLA_NOPE + MLA_ROPE)), MLA_Q_RANK),
        "even_kv_norm": gain(ks[7], (N_EVEN, MLA_KV_RANK)),
        "even_w_ukv": nrm(ks[8], (N_EVEN, MLA_KV_RANK, MLA_HEADS * (MLA_NOPE + MLA_V)), MLA_KV_RANK),
        "even_w_out": nrm(ks[9], (N_EVEN, MIX_WIDTH, D_MODEL), MIX_WIDTH),
        "odd_w_pw1": nrm(ks[10], (N_ODD, D_MODEL, 2 * CONF_WIDTH), D_MODEL),
        "odd_b_pw1": bias(ks[11], (N_ODD, 2 * CONF_WIDTH)),
        "odd_w_dw": nrm(ks[12], (N_ODD, CONF_KERNEL, CONF_WIDTH), CONF_KERNEL),
        "odd_b_dw": bias(ks[13], (N_ODD, CONF_WIDTH)),
        "odd_ln_g": gain(ks[14], (N_ODD, CONF_WIDTH)),
        "odd_ln_b": bias(ks[15], (N_ODD, CONF_WIDTH)),
        "odd_w_pw2": nrm(ks[16], (N_ODD, CONF_WIDTH, D_MODEL), CONF_WIDTH),
        "odd_b_pw2": bias(ks[17], (N_ODD, D_MODEL)),
        "mlp_w1": nrm(ks[18], (DEPTH, D_MODEL, D_FF), D_MODEL),
        "mlp_w2": nrm(ks[19], (DEPTH, D_FF, D_MODEL), D_FF),
    }

def first_block(x, positions, sandwich_gains, even_w_in, even_sc_kernel, even_q_norm,
              even_w_uq, even_kv_norm, even_w_ukv, even_w_out, odd_w_pw1, odd_b_pw1,
              odd_w_dw, odd_b_dw, odd_ln_g, odd_ln_b, odd_w_pw2, odd_b_pw2,
              mlp_w1, mlp_w2):
    for i in range(DEPTH):
        g = sandwich_gains[i]
        j = i // 2
        h = rms_norm(x, g[0])
        if i % 2 == 0:
            m = parallel_conv_mla(h, positions, even_w_in[j], even_sc_kernel[j],
                                  even_q_norm[j], even_w_uq[j], even_kv_norm[j],
                                  even_w_ukv[j], even_w_out[j])
        else:
            m = conformer_conv(h, odd_w_pw1[j], odd_b_pw1[j], odd_w_dw[j], odd_b_dw[j],
                               odd_ln_g[j], odd_ln_b[j], odd_w_pw2[j], odd_b_pw2[j])
        x = x + rms_norm(m, g[1])
        h = rms_norm(x, g[2])
        x = x + rms_norm(squared_relu_mlp(h, mlp_w1[i], mlp_w2[i]), g[3])
    return x


DEPTH_2 = 1

HEAD_DIM = 64
ROPE_THETA = 10000.0
NORM_EPS = 1e-6
NEG_INF = -1e30

DIFF_HEADS = 4
DIFF_V_DIM = 2 * HEAD_DIM
DIFF_WIDTH = DIFF_HEADS * DIFF_V_DIM

NSA_HEADS = 8
NSA_KV_GROUPS = 2
NSA_HEADS_PER_GROUP = NSA_HEADS // NSA_KV_GROUPS
NSA_WIDTH = NSA_HEADS * HEAD_DIM
KV_COLS = NSA_KV_GROUPS * HEAD_DIM
CMP_BLOCK = 32
CMP_STRIDE = 16
CMP_HIDDEN = 4 * HEAD_DIM
SLC_BLOCK = 64
SLC_TOPK = 16
WINDOW = 512
NSA_Q_BLOCK = 64
N_BRANCHES = 3

MIX_WIDTH_2 = DIFF_WIDTH + NSA_WIDTH
IN_COLS_2 = 2 * DIFF_HEADS * 2 * HEAD_DIM + DIFF_WIDTH + NSA_WIDTH + 6 * KV_COLS + NSA_HEADS * N_BRANCHES
D_FF_2 = ((8 * D_MODEL + 3 * 256 - 1) // (3 * 256)) * 256


def rms_norm_2(x, g):
    xf = x.astype(jnp.float32)
    y = xf * lax.rsqrt(jnp.mean(xf * xf, axis=-1, keepdims=True) + NORM_EPS)
    return (y * g.astype(jnp.float32)).astype(x.dtype)

def rope_tables(S):
    inv = 1.0 / (ROPE_THETA ** (jnp.arange(0, HEAD_DIM, 2, dtype=jnp.float32) / HEAD_DIM))
    ang = jnp.arange(S, dtype=jnp.float32)[:, None] * inv[None, :]
    return jnp.cos(ang), jnp.sin(ang)

def apply_rope_2(x, cos, sin):
    x1, x2 = jnp.split(x, 2, axis=-1)
    c = cos.astype(x.dtype)
    s = sin.astype(x.dtype)
    return jnp.concatenate([x1 * c - x2 * s, x1 * s + x2 * c], axis=-1)

def masked_softmax(s, mask):
    p = jax.nn.softmax(jnp.where(mask, s, NEG_INF), axis=-1)
    return jnp.where(mask, p, 0.0)

def diff_attention(q, k, v, lam):
    B, H, _, S, d = q.shape
    scale = d ** -0.5
    kpos = jnp.arange(S)

    def block(i):
        s0 = i * Q_BLOCK
        qb = lax.dynamic_slice_in_dim(q, s0, Q_BLOCK, axis=3)
        s = jnp.einsum('bhmqd,bhmkd->bhmqk', qb, k).astype(jnp.float32) * scale
        qpos = s0 + jnp.arange(Q_BLOCK)
        mask = kpos[None, :] <= qpos[:, None]
        p = jax.nn.softmax(jnp.where(mask, s, NEG_INF), axis=-1)
        a = p[:, :, 0] - lam * p[:, :, 1]
        return jnp.einsum('bhqk,bhke->bhqe', a.astype(v.dtype), v)

    o = lax.map(block, jnp.arange(S // Q_BLOCK))
    return o.transpose(1, 0, 3, 2, 4).reshape(B, S, H, v.shape[-1])

def compress_tokens(t, tok_idx, pos, w1, w2):
    blocks = t[:, :, tok_idx] + pos.astype(t.dtype)
    flat = blocks.reshape(blocks.shape[0], blocks.shape[1], blocks.shape[2], -1)
    return jax.nn.silu(flat @ w1) @ w2

def selection_overlap(n_cmp, n_sel):
    c0 = np.arange(n_cmp)[:, None] * CMP_STRIDE
    s0 = np.arange(n_sel)[None, :] * SLC_BLOCK
    ov = np.clip(np.minimum(c0 + CMP_BLOCK, s0 + SLC_BLOCK) - np.maximum(c0, s0), 0, None)
    return (ov / CMP_BLOCK).astype(np.float32)

def nsa_attention(q, kc_tok, vc_tok, ks, vs, kw, vw, gates,
                  k_pos, k_w1, k_w2, v_pos, v_w1, v_w2):
    B, G, Hg, S, d = q.shape
    dt = q.dtype
    scale = d ** -0.5
    QB = NSA_Q_BLOCK
    n_cmp = (S - CMP_BLOCK) // CMP_STRIDE + 1
    n_sel = S // SLC_BLOCK
    top_n = min(SLC_TOPK, n_sel)

    tok_idx = np.arange(n_cmp)[:, None] * CMP_STRIDE + np.arange(CMP_BLOCK)[None, :]
    kc = compress_tokens(kc_tok, tok_idx, k_pos, k_w1, k_w2)
    vc = compress_tokens(vc_tok, tok_idx, v_pos, v_w1, v_w2)
    cmp_end = jnp.asarray(tok_idx[:, -1])
    overlap = jnp.asarray(selection_overlap(n_cmp, n_sel))

    ks_blk = ks.reshape(B, G, n_sel, SLC_BLOCK, d)
    vs_blk = vs.reshape(B, G, n_sel, SLC_BLOCK, d)
    kw_pad = jnp.pad(kw, ((0, 0), (0, 0), (WINDOW, 0), (0, 0)))
    vw_pad = jnp.pad(vw, ((0, 0), (0, 0), (WINDOW, 0), (0, 0)))
    gather_blocks = jax.vmap(jax.vmap(lambda t, i: t[i]))
    blk = jnp.arange(n_sel)

    def block(i):
        s0 = i * QB
        qb = lax.dynamic_slice_in_dim(q, s0, QB, axis=3)
        gb = lax.dynamic_slice_in_dim(gates, s0, QB, axis=3)
        qpos = s0 + jnp.arange(QB)

        sc = jnp.einsum('bghqd,bgnd->bghqn', qb, kc).astype(jnp.float32) * scale
        pc = masked_softmax(sc, cmp_end[None, :] <= qpos[:, None])
        o_cmp = jnp.einsum('bghqn,bgnd->bghqd', pc.astype(dt), vc)

        imp = jnp.einsum('bghqn,nj->bgqj', pc, overlap)
        cur = qpos // SLC_BLOCK
        valid = blk[None, :] * SLC_BLOCK <= qpos[:, None]
        forced = (blk[None, :] == 0) | (blk[None, :] == cur[:, None]) | (blk[None, :] == cur[:, None] - 1)
        imp = jnp.where(forced, jnp.inf, jnp.where(valid, imp, -jnp.inf))
        _, sel = lax.top_k(imp, top_n)
        kg = gather_blocks(ks_blk, sel)
        vg = gather_blocks(vs_blk, sel)
        tpos = sel[..., None] * SLC_BLOCK + jnp.arange(SLC_BLOCK)
        smask = (tpos <= qpos[:, None, None]).reshape(B, G, 1, QB, top_n * SLC_BLOCK)
        ss = jnp.einsum('bghqd,bgqnld->bghqnl', qb, kg).astype(jnp.float32) * scale
        ps = masked_softmax(ss.reshape(B, G, Hg, QB, top_n * SLC_BLOCK), smask)
        o_slc = jnp.einsum('bghqm,bgqmd->bghqd', ps.astype(dt),
                           vg.reshape(B, G, QB, top_n * SLC_BLOCK, d))

        kwb = lax.dynamic_slice_in_dim(kw_pad, s0, WINDOW + QB, axis=2)
        vwb = lax.dynamic_slice_in_dim(vw_pad, s0, WINDOW + QB, axis=2)
        wpos = s0 - WINDOW + jnp.arange(WINDOW + QB)
        wmask = (wpos[None, :] <= qpos[:, None]) & (wpos[None, :] > qpos[:, None] - WINDOW) & (wpos[None, :] >= 0)
        sw = jnp.einsum('bghqd,bgkd->bghqk', qb, kwb).astype(jnp.float32) * scale
        pw = masked_softmax(sw, wmask)
        o_win = jnp.einsum('bghqk,bgkd->bghqd', pw.astype(dt), vwb)

        return gb[..., 0:1] * o_cmp + gb[..., 1:2] * o_slc + gb[..., 2:3] * o_win

    o = lax.map(block, jnp.arange(S // QB))
    return o.transpose(1, 0, 4, 2, 3, 5).reshape(B, S, G * Hg * d)

def hybrid_mixer(h, layer, w_in, lambda_q1, lambda_k1, lambda_q2, lambda_k2, diff_subln,
                 k_cmp_pos, k_cmp_w1, k_cmp_w2, v_cmp_pos, v_cmp_w1, v_cmp_w2, w_out):
    B, S, _ = h.shape
    cos, sin = rope_tables(S)
    proj = h @ w_in
    sizes = [DIFF_HEADS * 2 * HEAD_DIM, DIFF_HEADS * 2 * HEAD_DIM, DIFF_WIDTH, NSA_WIDTH,
             KV_COLS, KV_COLS, KV_COLS, KV_COLS, KV_COLS, KV_COLS, NSA_HEADS * N_BRANCHES]
    dq, dk, dv, nq, kc, vc, ks, vs, kw, vw, gt = jnp.split(
        proj, np.cumsum(sizes)[:-1].tolist(), axis=-1)

    dq = apply_rope_2(dq.reshape(B, S, DIFF_HEADS, 2, HEAD_DIM).transpose(0, 2, 3, 1, 4), cos, sin)
    dk = apply_rope_2(dk.reshape(B, S, DIFF_HEADS, 2, HEAD_DIM).transpose(0, 2, 3, 1, 4), cos, sin)
    dv = dv.reshape(B, S, DIFF_HEADS, DIFF_V_DIM).transpose(0, 2, 1, 3)
    lam_init = 0.8 - 0.6 * math.exp(-0.3 * layer)
    f32 = jnp.float32
    lam = (jnp.exp(jnp.sum(lambda_q1.astype(f32) * lambda_k1.astype(f32)))
           - jnp.exp(jnp.sum(lambda_q2.astype(f32) * lambda_k2.astype(f32))) + lam_init)
    o_diff = diff_attention(dq, dk, dv, lam)
    o_diff = (rms_norm_2(o_diff, diff_subln) * (1.0 - lam_init)).reshape(B, S, DIFF_WIDTH)

    def q_heads(t):
        return t.reshape(B, S, NSA_KV_GROUPS, NSA_HEADS_PER_GROUP, HEAD_DIM).transpose(0, 2, 3, 1, 4)

    def kv_heads(t):
        return t.reshape(B, S, NSA_KV_GROUPS, HEAD_DIM).transpose(0, 2, 1, 3)

    nq = apply_rope_2(q_heads(nq), cos, sin)
    kc = apply_rope_2(kv_heads(kc), cos, sin)
    ks = apply_rope_2(kv_heads(ks), cos, sin)
    kw = apply_rope_2(kv_heads(kw), cos, sin)
    gates = jax.nn.sigmoid(gt.reshape(B, S, NSA_KV_GROUPS, NSA_HEADS_PER_GROUP, N_BRANCHES)
                           .transpose(0, 2, 3, 1, 4))
    o_nsa = nsa_attention(nq, kc, kv_heads(vc), ks, kv_heads(vs), kw, kv_heads(vw), gates,
                          k_cmp_pos, k_cmp_w1, k_cmp_w2, v_cmp_pos, v_cmp_w1, v_cmp_w2)

    return jnp.concatenate([o_diff, o_nsa], axis=-1) @ w_out

def second_inputs(seed: int = 0) -> dict:
    key = jax.random.key(seed)
    k = jax.random.split(key, 24)
    L = DEPTH_2

    def nrm(kk, shape, scale):
        return jax.random.normal(kk, shape, jnp.float32) * scale

    def gain(kk, n):
        return 1.0 + 0.05 * jax.random.normal(kk, (L, n), jnp.float32)

    cmp_in = CMP_BLOCK * HEAD_DIM
    return {
        'x': nrm(k[0], (BATCH, SEQ, D_MODEL), 1.0),
        'attn_pre_norm': gain(k[1], D_MODEL),
        'w_in': nrm(k[2], (L, D_MODEL, IN_COLS_2), D_MODEL ** -0.5),
        'lambda_q1': nrm(k[3], (L, HEAD_DIM), 0.1),
        'lambda_k1': nrm(k[4], (L, HEAD_DIM), 0.1),
        'lambda_q2': nrm(k[5], (L, HEAD_DIM), 0.1),
        'lambda_k2': nrm(k[6], (L, HEAD_DIM), 0.1),
        'diff_subln': gain(k[7], DIFF_V_DIM),
        'k_cmp_pos': nrm(k[8], (L, CMP_BLOCK, HEAD_DIM), 0.1),
        'k_cmp_w1': nrm(k[9], (L, cmp_in, CMP_HIDDEN), cmp_in ** -0.5),
        'k_cmp_w2': nrm(k[10], (L, CMP_HIDDEN, HEAD_DIM), CMP_HIDDEN ** -0.5),
        'v_cmp_pos': nrm(k[11], (L, CMP_BLOCK, HEAD_DIM), 0.1),
        'v_cmp_w1': nrm(k[12], (L, cmp_in, CMP_HIDDEN), cmp_in ** -0.5),
        'v_cmp_w2': nrm(k[13], (L, CMP_HIDDEN, HEAD_DIM), CMP_HIDDEN ** -0.5),
        'w_out': nrm(k[14], (L, MIX_WIDTH_2, D_MODEL), MIX_WIDTH_2 ** -0.5),
        'attn_post_norm': gain(k[15], D_MODEL),
        'ffn_pre_norm': gain(k[16], D_MODEL),
        'w_gate': nrm(k[17], (L, D_MODEL, D_FF_2), D_MODEL ** -0.5),
        'w_up': nrm(k[18], (L, D_MODEL, D_FF_2), D_MODEL ** -0.5),
        'w_down': nrm(k[19], (L, D_FF_2, D_MODEL), D_FF_2 ** -0.5),
        'ffn_post_norm': gain(k[20], D_MODEL),
    }

def second_block(x, attn_pre_norm, w_in, lambda_q1, lambda_k1, lambda_q2, lambda_k2, diff_subln,
              k_cmp_pos, k_cmp_w1, k_cmp_w2, v_cmp_pos, v_cmp_w1, v_cmp_w2, w_out,
              attn_post_norm, ffn_pre_norm, w_gate, w_up, w_down, ffn_post_norm):
    for l in range(DEPTH_2):
        h = rms_norm_2(x, attn_pre_norm[l])
        mix = hybrid_mixer(h, l, w_in[l], lambda_q1[l], lambda_k1[l], lambda_q2[l], lambda_k2[l],
                           diff_subln[l], k_cmp_pos[l], k_cmp_w1[l], k_cmp_w2[l],
                           v_cmp_pos[l], v_cmp_w1[l], v_cmp_w2[l], w_out[l])
        x = x + rms_norm_2(mix, attn_post_norm[l])
        h = rms_norm_2(x, ffn_pre_norm[l])
        f = (jax.nn.silu(h @ w_gate[l]) * (h @ w_up[l])) @ w_down[l]
        x = x + rms_norm_2(f, ffn_post_norm[l])
    return x


def setup_inputs(seed=0):
    out = dict(first_inputs(seed))
    for name, value in second_inputs(seed + 1).items():
        if name != "x":
            out[name + "_2"] = value
    return out


def reference(
    x, positions, sandwich_gains, even_w_in, even_sc_kernel, even_q_norm, even_w_uq,
    even_kv_norm, even_w_ukv, even_w_out, odd_w_pw1, odd_b_pw1, odd_w_dw, odd_b_dw, odd_ln_g,
    odd_ln_b, odd_w_pw2, odd_b_pw2, mlp_w1, mlp_w2, attn_pre_norm_2, w_in_2, lambda_q1_2,
    lambda_k1_2, lambda_q2_2, lambda_k2_2, diff_subln_2, k_cmp_pos_2, k_cmp_w1_2, k_cmp_w2_2,
    v_cmp_pos_2, v_cmp_w1_2, v_cmp_w2_2, w_out_2, attn_post_norm_2, ffn_pre_norm_2, w_gate_2,
    w_up_2, w_down_2, ffn_post_norm_2,
):
    x = first_block(
        x, positions, sandwich_gains, even_w_in, even_sc_kernel, even_q_norm, even_w_uq,
        even_kv_norm, even_w_ukv, even_w_out, odd_w_pw1, odd_b_pw1, odd_w_dw, odd_b_dw,
        odd_ln_g, odd_ln_b, odd_w_pw2, odd_b_pw2, mlp_w1, mlp_w2,
    )
    return second_block(
        x, attn_pre_norm_2, w_in_2, lambda_q1_2, lambda_k1_2, lambda_q2_2, lambda_k2_2,
        diff_subln_2, k_cmp_pos_2, k_cmp_w1_2, k_cmp_w2_2, v_cmp_pos_2, v_cmp_w1_2, v_cmp_w2_2,
        w_out_2, attn_post_norm_2, ffn_pre_norm_2, w_gate_2, w_up_2, w_down_2, ffn_post_norm_2,
    )


_drawn_inputs = setup_inputs


def setup_inputs(seed=0):
    import zlib

    import numpy as np

    out = dict(_drawn_inputs(seed))
    spreads = {}
    factors = {'even_q_norm': 8.0,
     'even_kv_norm': 7.534,
     'odd_b_pw1': 3.904,
     'odd_ln_b': 4.138,
     'lambda_q1_2': 200.0,
     'lambda_q2_2': 8.0,
     'lambda_k2_2': 8.0,
     'diff_subln_2': 3.244,
     'k_cmp_pos_2': 64.0,
     'v_cmp_pos_2': 4.585,
     'ffn_post_norm_2': 3.014,
     'lambda_k1_2': 8.0,
     'k_cmp_w1_2': 5.223,
     'k_cmp_w2_2': 5.025}
    for name, (base, spread) in spreads.items():
        noise = np.random.default_rng([zlib.crc32(name.encode()), seed]).standard_normal(out[name].shape)
        drawn = base * np.exp(spread * noise) if base else spread * noise
        out[name] = jnp.asarray(drawn.astype(out[name].dtype))
    for name, factor in factors.items():
        out[name] = (out[name] * factor).astype(out[name].dtype)
    return out
```

```python
from contextlib import ExitStack

import numpy as np

import concourse.bass as bass
from concourse import mybir

F32 = mybir.dt.float32
F32R = mybir.dt.float32r
I32 = mybir.dt.int32
ALU = mybir.AluOpType
ACT = mybir.ActivationFunctionType
AX = mybir.AxisListType.X
ds = bass.ds

P = 128
T = 256
M = T // P
D = 1024
KD = D // P
EPS = 1e-6
NEG = -1e30

SCW = 512
QR, KVR, ROPE = 384, 256, 32
NOPE, VD, NH = 64, 64, 8
QKD = NOPE + ROPE
A_COLS = QR + KVR + ROPE
MLP_BLOCKS = 4096 // 512
TAPS = 31
CONV_PAD = TAPS // 2
PE_TILES = (4, 5, 6, 7)
DVE_TILES = (0, 1, 2, 3)
DIAGS = 6

HD = 64
DH = 4
LAM_INIT = 0.8 - 0.6 * float(np.exp(-0.3 * 0))
N_CMP = (T - 32) // 16 + 1
FF = 2816
FF_BLOCKS = FF // 256

PIECE = 2048
RING = 4
FF_RING = 3

C_ID, C_CAUSAL = 0, 128
C_COS, C_SIN = 256, 384
C_CNEG, C_CONE = 512, 544
C_BLK, C_FREQ = 576, 584
C_END = 600

TWO_PI = (6.28125, 0.0019350051879882812, 2 * float(np.pi) - 6.28125 - 0.0019350051879882812)
ROUND = 1.5 * 2.0 ** 23


def shape_constants():
    c = np.zeros((P, C_END), np.float32)
    c[:, C_ID:C_ID + P] = np.eye(P)
    q = np.arange(P)
    c[:, C_CAUSAL:C_CAUSAL + P] = np.where(q[None, :] <= q[:, None], 0.0, NEG)
    inv = (1.0 / (np.float32(10000.0) ** (np.arange(0, HD, 2, dtype=np.float32) / np.float32(HD)))).astype(np.float32)
    for m in range(M):
        tok = np.arange(m * P, (m + 1) * P)
        ang = tok.astype(np.float32)[:, None] * inv[None, :]
        cos, sin = np.cos(ang), np.sin(ang)
        c[:, C_COS + 64 * m:C_COS + 64 * m + 64] = np.concatenate([cos, cos], 1)
        c[:, C_SIN + 64 * m:C_SIN + 64 * m + 64] = np.concatenate([-sin, sin], 1)
        seen = (np.arange(16) * 16 + 31)[None, :] <= tok[:, None]
        c[:, C_CNEG + 16 * m:C_CNEG + 16 * m + 16] = np.where(seen, 0.0, NEG)
        c[:, C_CONE + 16 * m:C_CONE + 16 * m + 16] = seen
    c[:, C_BLK:C_BLK + 8] = (q[:, None] // 16 == np.arange(8)[None, :])
    c[:, C_FREQ:C_FREQ + 16] = 1.0 / (np.float32(10000.0) ** (np.arange(16, dtype=np.float32) / np.float32(16)))
    return c


STAGES = [("w_in_wide", 6), ("w_in_tall", 3), ("w_uq", 2), ("w_ukv", 1), ("w_out", 4),
          ("mlp0", 4 * MLP_BLOCKS), ("pw1", 8), ("pw2", 4), ("mlp1", 4 * MLP_BLOCKS),
          ("w_in_2", 12), ("cmp", 4), ("w_out_2", 4), ("ffn", 3 * FF_BLOCKS)]
FIRST = {}
_n = 0
for _name, _count in STAGES:
    FIRST[_name] = _n
    _n += _count
N_PIECES = _n
assert FIRST["ffn"] % RING == 0


class Steps:

    def __init__(self, eng, sem):
        self.eng, self.sem, self.count, self.turn, self.per = eng, sem, 0, None, 0

    def link(self, ins):
        self.count += 1
        ins.then_inc(self.sem, 1)
        self.eng.wait_ge(self.sem, self.count if self.turn is None else self.turn * self.per + self.count)

    def enter(self, turn, per):
        self.turn, self.per, self.at = turn, per, self.count

    def leave(self, turns):
        assert self.count - self.at == self.per, (self.count - self.at, self.per)
        self.count = self.at + turns * self.per
        self.turn = None


def two_blocks(nc, a, out):
    with ExitStack() as ctx:
        def sb(name, shape, dt=F32):
            return ctx.enter_context(nc.sbuf_tensor(name, shape, dt))

        sems = {}

        def S(name):
            if name not in sems:
                sems[name] = ctx.enter_context(nc.semaphore(name))
            return sems[name]

        raw = [sb(f"raw{i}", [P, PIECE]) for i in range(RING)]
        w_hi = [sb(f"w_hi{i}", [P, PIECE], F32R) for i in range(RING)]
        w_lo = [sb(f"w_lo{i}", [P, PIECE], F32R) for i in range(RING)]
        x = sb("x_res", [P, M, D])
        act_hl = sb("act_hl", [P, KD, 2 * T], F32R)
        hl2 = sb("hl2", [P, 5, 2 * T], F32R)
        nrm = sb("nrm", [P, M, D])
        gain = [sb(f"gain{i}", [P, D]) for i in range(4)]
        cst = sb("cst", [P, C_END])
        col = sb("col", [P, 3, P])
        bc = sb("bc", [P, 1024])
        ones = sb("ones", [1, P])
        st = sb("st", [P, 192])
        arena = sb("arena", [P, 10752])
        brow = arena[0:1, 9712:9712 + D]

        ident = cst[:, C_ID:C_ID + P]
        causal = cst[:, C_CAUSAL:C_CAUSAL + P]

        def AR(at, *dims, p=P, p0=0):
            n = int(np.prod(dims))
            v = arena[p0:p0 + p, at:at + n]
            if len(dims) == 2:
                return v.rearrange("p (a b) -> p a b", a=dims[0])
            if len(dims) == 3:
                return v.rearrange("p (a b c) -> p a b c", a=dims[0], b=dims[1])
            if len(dims) == 4:
                return v.rearrange("p (a b c d) -> p a b c d", a=dims[0], b=dims[1], c=dims[2])
            return v

        hb = AR(0, 4, T)
        htmp = AR(1024, 4, T)
        gsum, usum = AR(2048, 2, T), AR(2560, 2, T)
        esum = AR(3072, 2, T)
        gate_b, gate_c = AR(0, 4, T), AR(1024, 4, T)
        cx = AR(2048, 4, T + 2)
        ctmp = AR(3080, 4, T)
        qT, kT1 = AR(0, NH, T), AR(2048, NH, T)
        lat = AR(4104, M, QR + KVR)
        prob = [AR(4104 + 512 * i, M, T) for i in range(2)]
        probT = [AR(5128 + 512 * i, M, T) for i in range(2)]
        qf, kf = AR(6152, M, NH, QKD), AR(7688, M, NH, QKD)
        v1 = AR(9224, M, NH, VD)
        rows = AR(9224, 3, P)
        rt = AR(10248, NH, ROPE)
        rt2 = AR(10504, M, ROPE)
        UW = T + 2 * CONV_PAD
        upad = AR(0, 8, UW)
        cv = AR(2288, 8, T)
        ag = AR(4336, 4, T)
        ptmp = AR(5360, 4, T)
        diag = AR(6384, DIAGS, P)
        zb = AR(0, 8, T)
        eb = AR(7152, 8, T)
        eg = AR(9200, 2, T)
        tok2 = AR(0, 2048)
        nqt = AR(2048, M, 8 * HD)
        p2 = [AR(768 * i, 2, 384) for i in range(2)]
        pt2 = [AR(1536 + 768 * i, 2, 384) for i in range(2)]
        dqkT = AR(3072, 8, T)
        nqT = AR(5120, 4, T)
        kT2 = AR(6144, 4, 2, T)
        dv = AR(8192, M, 512)
        vsw = AR(9216, M, 2, 128)
        od = AR(9728, 8, P)
        t1, t2 = nrm[:, 0, :], nrm[:, 1, :]
        flat = nrm[:, 0, 0:960].rearrange("p (a j n) -> p a j n", a=2, j=16)
        vsel = nrm[:, 1, 0:512].rearrange("p (h d) -> p h d", h=8)
        pcT = nrm[:, 1, 512:768]
        pcm = nrm[:, 1, 768:1024].rearrange("p (m h n) -> p m h n", m=2, h=8)
        pc = nrm[:, 0, 0:256].rearrange("p (a h m n) -> p a h m n", a=2, h=4, m=2)
        hidrep = nrm[:, 0, 256:512].rearrange("p (c h n) -> p c h n", c=2, h=8)
        hidc = nrm[:, 0, 512:632].rearrange("p (a c n) -> p a c n", a=2, c=2)
        hctmp = nrm[:, 0, 640:760].rearrange("p (a c n) -> p a c n", a=2, c=2)
        hce = nrm[:, 0, 768:888].rearrange("p (a c n) -> p a c n", a=2, c=2)
        kcT = nrm[:, 0, 896:926]
        w2k = sb("w2k", [P, 2, 2, HD])
        w2v = sb("w2v", [P, 2, HD])
        gates = sb("gates", [P, M, 24])
        cs1 = sb("cs1", [P, 2, M, ROPE])
        posi = sb("posi", [P, M], I32)
        lamn = sb("lamn", [P, 1])

        ss = st[:, 0:2]
        rstd = st[:, 2:4]
        mhalf = st[:, 4:12]
        ss4, rs4 = st[:, 12:16], st[:, 16:20]
        mv = st[:, 20:24].rearrange("p (m c) -> p m c", m=2)
        bns = st[:, 24:48].rearrange("p (m h c) -> p m h c", m=2, h=2)
        ss8, rs8 = st[:, 48:56], st[:, 56:64]
        mx = [st[:, 64 + 4 * i:68 + 4 * i] for i in range(2)]
        nmx = [st[:, 72 + 4 * i:76 + 4 * i] for i in range(2)]
        rsum = [st[:, 80 + 4 * i:84 + 4 * i] for i in range(2)]
        rinv = [st[:, 88 + 4 * i:92 + 4 * i] for i in range(2)]
        cf = [st[:, 96 + 4 * i:100 + 4 * i] for i in range(2)]
        pf = st[:, 104:106]
        lam4 = st[:, 106:110]
        cmx = st[:, 112:128]
        crs = st[:, 128:144]

        VC = {}
        r = 0
        for name, n in (("b_pw1", 16), ("b_dw", 8), ("ln_g", 8), ("ln_b", 8), ("sc", 12), ("kpos", 16), ("vpos", 16)):
            VC[name] = r
            r += n
        VROWS = r
        DROWS = 4 * TAPS

        def vcol(name, i, n=1):
            return col[:, 0, VC[name] + i:VC[name] + i + n]

        def dwcol(t, c):
            r = t * 8 + c
            return col[:, 1 + r // DROWS, r % DROWS:r % DROWS + 1]

        ps = ctx.enter_context(nc.psum_tensor("ps", [P, 8, 512], F32))
        ACC, UP = 0, 4
        TURN_BANK = (ACC, ACC, ACC, ACC, UP, ACC)

        def tall_out(bank, m, width=1024):
            return ps[:, bank + 2 * m:bank + 2 * m + 2, :].rearrange("p b n -> p (b n)")[:, 0:width]

        def turned(bank, k0, n):
            v = ps[:, bank:bank + 4, :].rearrange("p b (h t) -> p (b h) t", h=2)
            return v[:, k0:k0 + n, :]

        def view_k(w):
            return w.rearrange("(k p) n -> p k n", p=P)

        w_in = view_k(a["even_w_in"][0])
        w_uq, w_ukv = view_k(a["even_w_uq"][0]), view_k(a["even_w_ukv"][0])
        w_out = view_k(a["even_w_out"][0])
        pw1 = a["odd_w_pw1"][0].rearrange("(k p) (h n) -> p k h n", p=P, h=2)
        pw2 = view_k(a["odd_w_pw2"][0])
        mlp1 = [view_k(a["mlp_w1"][i]) for i in range(2)]
        mlp2 = [view_k(a["mlp_w2"][i]) for i in range(2)]
        w_in_2, w_out_2 = view_k(a["w_in_2"][0]), view_k(a["w_out_2"][0])
        cmp1 = [view_k(a["k_cmp_w1_2"][0]), view_k(a["v_cmp_w1_2"][0])]
        w_gate, w_up, w_down = view_k(a["w_gate_2"][0]), view_k(a["w_up_2"][0]), view_k(a["w_down_2"][0])

        piece = {}
        for b in range(3):
            for h in range(2):
                piece[FIRST["w_in_wide"] + 2 * b + h] = (4, 512, [w_in[:, 4 * h:4 * h + 4, 512 * b:512 * b + 512]])
        TALL_K = [(0, 3), (3, 3), (6, 2)]
        for j, (k, n) in enumerate(TALL_K):
            piece[FIRST["w_in_tall"] + j] = (n, A_COLS, [w_in[:, k:k + n, 3 * SCW:3 * SCW + A_COLS]])
        UQ_K = [(0, 2), (2, 1)]
        for j, (k, n) in enumerate(UQ_K):
            piece[FIRST["w_uq"] + j] = (n, NH * QKD, [w_uq[:, k:k + n, :]])
        piece[FIRST["w_ukv"]] = (2, 1024, [w_ukv])
        for name, w in (("w_out", w_out), ("pw2", pw2), ("w_out_2", w_out_2)):
            for j in range(4):
                piece[FIRST[name] + j] = (2, 1024, [w[:, 2 * j:2 * j + 2, :]])
        for b in range(4):
            for h in range(2):
                piece[FIRST["pw1"] + 2 * b + h] = (4, 512, [
                    pw1[:, 4 * h:4 * h + 4, g, 256 * b:256 * b + 256] for g in range(2)])
        W2C = [(0, 1024), (1024, 1024), (2048, 792)]
        for c, (n0, n) in enumerate(W2C):
            for j in range(4):
                piece[FIRST["w_in_2"] + 4 * c + j] = (2, n, [w_in_2[:, 2 * j:2 * j + 2, n0:n0 + n]])
        for a_ in range(2):
            for h in range(2):
                piece[FIRST["cmp"] + 2 * a_ + h] = (8, 256, [cmp1[a_][:, 8 * h:8 * h + 8, :]])

        def in_loop(n):
            return n not in piece

        def slot_of(n):
            return n % RING if n < FIRST["ffn"] else (n - FIRST["ffn"]) % FF_RING

        def back(n):
            return RING if n < FIRST["ffn"] else FF_RING

        def width_of(n):
            return piece[n][0] * piece[n][1] if n in piece else PIECE

        def parts_of(n):
            if n in piece:
                return len(piece[n][2])
            if n < FIRST["ffn"]:
                return 1
            q = n - FIRST["ffn"]
            return 2 if q < 2 or (q < 2 + 3 * (FF_BLOCKS - 1) and (q - 2) % 3 < 2) else 1

        def landed_at(n):
            return 16 * sum(parts_of(q) for q in range(n + 1) if slot_of(q) == slot_of(n))

        def pv(tile, n):
            k, w = piece[n][0:2]
            return tile[slot_of(n)][:, 0:k * w].rearrange("p (k n) -> p k n", k=k)

        with nc.Block() as block:
            @block.sync
            def _(sp):
                def load(n):
                    k, w, srcs = piece[n]
                    if n >= back(n):
                        sp.wait_ge(S("w_split"), n - back(n) + 1)
                    dst = pv(raw, n)
                    for i, src in enumerate(srcs):
                        part = w // len(srcs)
                        sp.dma_start(dst[:, :, i * part:(i + 1) * part], src).then_inc(S(f"landed{slot_of(n)}"), 16)

                def load_gain(s, src):
                    if s >= 4:
                        sp.wait_ge(S("gain_used"), s - 3)
                    sp.dma_start(gain[s % 4][:, :], src.partition_broadcast(P)).then_inc(S(f"gain{s % 4}"), 16)

                gains = [a["sandwich_gains"][i, j, :] for i in range(2) for j in range(4)] + [
                    a["attn_pre_norm_2"][0, :], a["attn_post_norm_2"][0, :],
                    a["ffn_pre_norm_2"][0, :], a["ffn_post_norm_2"][0, :]]

                for m in range(M):
                    sp.dma_start(x[:, m, :], a["x"][0, m * P:(m + 1) * P, :]).then_inc(S(f"x_in{m}"), 16)
                load_gain(0, gains[0])
                for n in range(4):
                    load(n)
                for s in range(1, 4):
                    load_gain(s, gains[s])
                for n in range(4, FIRST["mlp0"]):
                    load(n)
                load_gain(4, gains[4])

                def load_in_loop(n, i, per, src, cols=None):
                    slot = n % RING if per == 4 else (n - FIRST["ffn"]) % FF_RING
                    sp.wait_ge(S("w_split"), i * per + (n - (RING if per == 4 else FF_RING) + 1))
                    dst = raw[slot][:, :].rearrange("p (k n) -> p k n", k=src.shape[1])
                    if cols is not None:
                        dst = dst[:, :, cols[0]:cols[1]]
                    sp.dma_start(dst, src).then_inc(S(f"landed{slot}"), 16)

                def load_mlp(layer, n0):
                    def up(n, i, turn):
                        for h in range(2):
                            load_in_loop(n + h, turn, 4, mlp1[layer][:, 4 * h:4 * h + 4, ds(i * 512, 512)])

                    def down(n, i, turn):
                        for h in range(2):
                            load_in_loop(n + h, turn, 4, mlp2[layer][:, ds(i * 4 + 2 * h, 2), :])

                    up(n0, 0, 0)
                    with sp.Fori(1, MLP_BLOCKS) as i:
                        up(n0 + 2 - 4, i, i)
                        down(n0 + 4 - 4, i - 1, i)
                    down(n0 + 4 * MLP_BLOCKS - 2, MLP_BLOCKS - 1, 0)

                load_mlp(0, FIRST["mlp0"])
                sp.dma_start(brow, a["odd_b_pw2"]).then_inc(S("b_pw2"), 16)
                load_gain(5, gains[5])
                load_gain(6, gains[6])
                for n in range(FIRST["pw1"], FIRST["mlp1"]):
                    load(n)
                load_gain(7, gains[7])
                load_gain(8, gains[8])
                load_mlp(1, FIRST["mlp1"])
                load_gain(9, gains[9])
                load_gain(10, gains[10])
                for n in range(FIRST["w_in_2"], FIRST["ffn"]):
                    load(n)
                load_gain(11, gains[11])

                f0 = FIRST["ffn"]

                def gate_up(n, i, turn):
                    for h in range(2):
                        for g, w in enumerate((w_gate, w_up)):
                            load_in_loop(n + h, turn, 3, w[:, 4 * h:4 * h + 4, ds(i * 256, 256)], (256 * g, 256 * g + 256))

                gate_up(f0, 0, 0)
                with sp.Fori(1, FF_BLOCKS) as i:
                    gate_up(f0 - 1, i, i)
                    load_in_loop(f0 + 1, i, 3, w_down[:, ds((i - 1) * 2, 2), :])
                n = N_PIECES - 1
                sp.wait_ge(S("w_split"), n - FF_RING + 1)
                sp.dma_start(raw[slot_of(n)][:, :].rearrange("p (k n) -> p k n", k=2),
                             w_down[:, 2 * FF_BLOCKS - 2:2 * FF_BLOCKS, :]).then_inc(S(f"landed{slot_of(n)}"), 16)
                for m in range(M):
                    sp.wait_ge(S("x_new"), 2 * 5 + m + 1)
                    sp.dma_start(out[0, m * P:(m + 1) * P, :], x[:, m, :]).then_inc(S("stored"), 16)
                sp.wait_ge(S("stored"), 16 * M)

            @block.gpsimd
            def _(gp):
                me = Steps(gp, S("pool_step"))
                cursor = [0]

                def hi(n):
                    gp.wait_ge(S(f"landed{slot_of(n)}"), landed_at(n))
                    if n >= back(n):
                        gp.wait_ge(S("pe_piece"), n - back(n) + 1)
                    w = width_of(n)
                    gp.tensor_scalar(w_hi[slot_of(n)][:, 0:w], raw[slot_of(n)][:, 0:w], 1.0, 0.0,
                                     ALU.mult, ALU.add).then_inc(S("w_hi"), 1)

                def hi_until(n):
                    while cursor[0] <= min(n, N_PIECES - 1):
                        hi(cursor[0])
                        cursor[0] += 1

                def hi_in_loop(n, turn, per):
                    each = landed_at(n + per) - landed_at(n)
                    gp.wait_ge(S(f"landed{slot_of(n)}"), turn * each + landed_at(n))
                    gp.wait_ge(S("pe_piece"), turn * per + (n - back(n) + 1))
                    gp.sem_inc(S("pool_turn"), 1)
                    gp.tensor_scalar(w_hi[slot_of(n)][:, :], raw[slot_of(n)][:, :], 1.0, 0.0,
                                     ALU.mult, ALU.add).then_inc(S("w_hi"), 1)

                def rsqrt(dst, src, parts, sem):
                    for c0, c1, scale in parts:
                        me.link(gp.tensor_scalar(src[:, c0:c1], src[:, c0:c1], scale, EPS, ALU.mult, ALU.add))
                    n = parts[-1][1]
                    gp.tensor_tensor(dst[:, 0:n], src[:, 0:n], mhalf[:, 0:n], ALU.pow).then_inc(sem, 1)

                me.link(gp.memset(mhalf, -0.5))
                gp.memset(ones[:, :], 1.0).then_inc(S("ones"), 1)
                normed = [0]

                def norm(after):
                    hi_until(after)
                    normed[0] += 1
                    gp.wait_ge(S("ssq"), 2 * normed[0])
                    rsqrt(rstd, ss, [(0, 2, 1.0 / D)], S("rstd"))

                norm(-1)
                hi_until(FIRST["w_uq"] + 3)
                gp.wait_ge(S("lat_ssq"), 4)
                rsqrt(rs4, ss4, [(0, 2, 1.0 / QR), (2, 4, 1.0 / KVR)], S("lat_rstd"))

                def mlp(n0):
                    hi_until(n0 + 3)
                    with gp.Fori(0, MLP_BLOCKS - 1) as i:
                        for j in range(4):
                            hi_in_loop(n0 + 4 + j, i, 4)
                    cursor[0] = n0 + 4 * MLP_BLOCKS
                    norm(n0 + 4 * MLP_BLOCKS + 3)
                    norm(0)

                norm(FIRST["mlp0"] + 3)
                norm(0)
                mlp(FIRST["mlp0"])
                hi_until(FIRST["pw2"] + 3)
                gp.wait_ge(S("ln_stats"), 2)
                me.link(gp.tensor_scalar(ss, mv[:, :, 1], 1.0, EPS, ALU.mult, ALU.add))
                gp.tensor_tensor(rstd, ss, mhalf[:, 0:2], ALU.pow).then_inc(S("ln_rstd"), 1)
                norm(FIRST["mlp1"] + 3)
                norm(0)
                mlp(FIRST["mlp1"])
                hi_until(FIRST["w_out_2"] + 3)
                gp.wait_ge(S("diff_ssq"), 1)
                rsqrt(rs8, ss8, [(0, 8, 1.0 / P)], S("diff_rstd"))
                f0 = FIRST["ffn"]
                norm(f0 + 2)
                norm(0)
                with gp.Fori(0, FF_BLOCKS - 2) as i:
                    for j in range(3):
                        q = f0 + 3 + j
                        base = landed_at(q)
                        each = 32 if (q - f0 - 2) % 3 < 2 else 16
                        gp.wait_ge(S(f"landed{slot_of(q)}"), i * each + base)
                        gp.wait_ge(S("pe_piece"), i * 3 + (q - FF_RING + 1))
                        gp.sem_inc(S("pool_turn"), 1)
                        gp.tensor_scalar(w_hi[slot_of(q)][:, :], raw[slot_of(q)][:, :], 1.0, 0.0,
                                         ALU.mult, ALU.add).then_inc(S("w_hi"), 1)
                cursor[0] = f0 + 3 * (FF_BLOCKS - 1)
                norm(N_PIECES)

            @block.vector
            def _(dve):
                me = Steps(dve, S("dve_step"))
                link = me.link
                tt, stt, tsc = dve.tensor_tensor, dve.scalar_tensor_tensor, dve.tensor_scalar
                cursor = [0]

                def lo(n, turn=0, per=0):
                    w = width_of(n)
                    dve.wait_ge(S("w_hi"), turn * per + n + 1)
                    tt(w_lo[slot_of(n)][:, 0:w], raw[slot_of(n)][:, 0:w],
                       w_hi[slot_of(n)][:, 0:w].bitcast(F32), ALU.subtract).then_inc(S("w_split"), 1)

                def lo_until(n):
                    while cursor[0] <= min(n, N_PIECES - 1):
                        lo(cursor[0])
                        cursor[0] += 1

                def piece_done(n, turn=0, per=0):
                    dve.wait_ge(S("pe_piece"), turn * per + n + 1)

                def act_lo(src, k0, n, count, scale=1.0):
                    dve.wait_ge(S("act_hi"), count)
                    dst, high = act_hl[:, k0:k0 + n, T:2 * T], act_hl[:, k0:k0 + n, 0:T].bitcast(F32)
                    if scale == 1.0:
                        tt(dst, src, high, ALU.subtract).then_inc(S("act_lo"), 1)
                    else:
                        stt(dst, src, scale, high, ALU.mult, ALU.subtract).then_inc(S("act_lo"), 1)

                norms = [0]
                his = [0]

                def norm_turn(s):
                    g = norms[0]
                    norms[0] += 1
                    dve.wait_ge(S("rstd"), g + 1)
                    dve.wait_ge(S(f"gain{g % 4}"), 16 * (g // 4 + 1))
                    for m in range(M):
                        stt(nrm[:, m, :], x[:, m, :], rstd[:, m:m + 1], gain[g % 4][:, :], ALU.mult, ALU.mult)\
                            .then_inc(S("normed"), 1)
                    for k in range(0, KD, 2):
                        his[0] += 1
                        act_lo(turned(TURN_BANK[s], k, 2), k, 2, his[0])
                    dve.sem_inc(S("gain_used"), 1)

                def post_norm(p):
                    g = norms[0]
                    norms[0] += 1
                    dve.wait_ge(S("rstd"), g + 1)
                    dve.wait_ge(S(f"gain{g % 4}"), 16 * (g // 4 + 1))
                    for m in range(M):
                        link(stt(nrm[:, m, :], tall_out(ACC, m), rstd[:, m:m + 1], gain[g % 4][:, :],
                                 ALU.mult, ALU.mult))
                        tt(x[:, m, :], x[:, m, :], nrm[:, m, :], ALU.add).then_inc(S("x_new"), 1)
                    dve.sem_inc(S("gain_used"), 1)

                def rope(dst, src, cos, sin, ta, tb, half):
                    idx = (slice(None),) * (len(dst.shape) - 1)
                    first, second = idx + (slice(0, half),), idx + (slice(half, 2 * half),)
                    link(tt(ta, src, cos, ALU.mult))
                    link(tt(tb[first], src[second], sin[first], ALU.mult))
                    link(tt(tb[second], src[first], sin[second], ALU.mult))
                    return tt(dst, ta, tb, ALU.add)

                for i in range(3):
                    dve.wait_ge(S("cols"), i + 1)
                    n = VROWS if i == 0 else DROWS
                    link(tsc(col[:, i, 0:n], ps[:, UP + i, 0:n], 1.0 if i == 0 else 0.5, None, ALU.mult))
                norm_turn(0)
                lo_until(3)
                dve.wait_ge(S("small"), 16 * 11)
                posf, ang = rt[:, 0, 0:2], rt[:, 1:2, 0:32].rearrange("p o (m f) -> p (o m) f", m=2)
                link(dve.tensor_copy(posf, posi[:, :]))
                for m in range(M):
                    link(tsc(ang[:, m, :], cst[:, C_FREQ:C_FREQ + 16], posf[:, m:m + 1], None, ALU.mult))
                for i, quarter in enumerate((0.25, 0.0)):
                    turns = rt[:, 2 + i:3 + i, 0:32].rearrange("p o (m f) -> p (o m) f", m=2)
                    red = rt[:, 4 + i:5 + i, 0:32].rearrange("p o (m f) -> p (o m) f", m=2)
                    link(tsc(turns, ang, 1.0 / (2 * float(np.pi)), quarter, ALU.mult, ALU.add))
                    link(tsc(turns, turns, ROUND, -ROUND, ALU.add, ALU.add))
                    link(stt(red, turns, -TWO_PI[0], ang, ALU.mult, ALU.add))
                    link(stt(red, turns, -TWO_PI[1], red, ALU.mult, ALU.add))
                    link(stt(red, turns, -TWO_PI[2], red, ALU.mult, ALU.add))
                    link(tsc(red, red, float(np.pi) / 2 if i == 0 else 0.0, 3.1415925, ALU.add, ALU.min))
                    tsc(red, red, -3.1415925, None, ALU.max).then_inc(S("angles"), 1)
                dve.wait_ge(S("sines"), 2)
                link(dve.tensor_copy(cs1[:, 0, :, 16:32], cs1[:, 0, :, 0:16]))
                link(tsc(cs1[:, 1, :, 0:16], cs1[:, 1, :, 16:32], -1.0, None, ALU.mult))
                link(stt(rt[:, 6:8, :].rearrange("p a b -> p (a b)"), bc[:, 768:832], 1.0, bc[:, 832:896],
                         ALU.mult, ALU.mult, accum_out=lam4[:, 0:1]))
                stt(rt[:, 6:8, :].rearrange("p a b -> p (a b)"), bc[:, 896:960], 1.0, bc[:, 960:1024],
                    ALU.mult, ALU.mult, accum_out=lam4[:, 1:2]).then_inc(S("lam_sums"), 1)
                dve.wait_ge(S("lam_exp"), 1)
                link(tt(lamn[:, :], lam4[:, 3:4], lam4[:, 2:3], ALU.subtract))
                link(tsc(lamn[:, :], lamn[:, :], -LAM_INIT, None, ALU.add))
                link(dve.memset(cx[:, :, 0:1], 0.0))
                link(dve.memset(cx[:, :, T + 1:T + 2], 0.0))

                def halves(bank):
                    return ps[:, bank:bank + 4, 0:T]

                for b, dst in enumerate((gate_b, gate_c, None)):
                    n = FIRST["w_in_wide"] + 2 * b + 1
                    lo_until(n + 3)
                    dve.wait_ge(S("half_copied"), b + 1)
                    bank = (UP, ACC, UP)[b]
                    if b < 2:
                        tt(dst, halves(bank), ctmp, ALU.add).then_inc(S("wide_read"), 1)
                    else:
                        dve.wait_ge(S("wide_read"), 2)
                        link(tt(cx[:, :, 1:T + 1], halves(bank), ctmp, ALU.add))
                        link(tt(cx[:, :, 1:T + 1], cx[:, :, 1:T + 1], gate_c, ALU.mult))
                        dve.sem_inc(S("wide_read"), 1)
                for t in range(3):
                    for c in range(4):
                        w = vcol("sc", 4 * t + c)
                        if t == 0:
                            ins = tsc(gate_c[:, c, :], cx[:, c, 0:T], w, None, ALU.mult)
                        else:
                            ins = stt(gate_c[:, c, :], cx[:, c, t:t + T], w, gate_c[:, c, :], ALU.mult, ALU.add)
                    link(ins)
                tt(gate_b, gate_b, gate_c, ALU.mult).then_inc(S("ya"), 1)
                lo_until(FIRST["w_uq"] - 1 + 3)
                dve.wait_ge(S("lat_rstd"), 1)
                for m in range(M):
                    tall = tall_out(ACC, m)
                    stt(lat[:, m, 0:QR], tall[:, 0:QR], rs4[:, m:m + 1], bc[:, 0:QR], ALU.mult, ALU.mult)
                    stt(lat[:, m, QR:QR + KVR], tall[:, QR:QR + KVR], rs4[:, 2 + m:3 + m],
                        bc[:, QR:QR + KVR], ALU.mult, ALU.mult).then_inc(S("lat_normed"), 1)
                kr = ps[:, ACC:ACC + 4, :].rearrange("p (m b) n -> p m (b n)", m=2)[:, :, QR + KVR:A_COLS]
                link(rope(rt2, kr, cs1[:, 0], cs1[:, 1], rt[:, 0:2, :], rt[:, 2:4, :], ROPE // 2))
                for m in range(M):
                    ins = dve.tensor_copy(kf[:, m, :, NOPE:QKD], rt2[:, m, :].unsqueeze(1).to_broadcast([P, NH, ROPE]))
                ins.then_inc(S("kpe"), 1)
                for i, (k, n) in enumerate(((0, 2), (2, 2), (4, 1))):
                    dve.wait_ge(S("lat_hi"), i + 1)
                    tt(hl2[:, k:k + n, T:2 * T], turned(UP, k, n), hl2[:, k:k + n, 0:T].bitcast(F32),
                       ALU.subtract).then_inc(S("lat_lo"), 1)
                his[0] += 1
                act_lo(gate_b, 0, 4, his[0])
                lo_until(FIRST["w_uq"] + 1 + 3)
                piece_done(FIRST["w_uq"] + 1)
                for m in range(M):
                    src = tall_out(ACC, m, NH * QKD).rearrange("p (h d) -> p h d", h=NH)[:, :, NOPE:QKD]
                    cos, sin = (cs1[:, i, m, :].unsqueeze(1).to_broadcast([P, NH, ROPE]) for i in range(2))
                    ta = AR(4104, NH, ROPE)
                    tb = AR(4360, NH, ROPE)
                    dve.wait_ge(S("q_nope"), m + 1)
                    rope(qf[:, m, :, NOPE:QKD], src, cos, sin, ta, tb, ROPE // 2).then_inc(S("q_rope"), 1)
                    dve.wait_ge(S("q_rope"), m + 1)
                lo_until(FIRST["w_out"] - 1 + 3)
                for j in range(4):
                    dve.wait_ge(S("k_turned"), j + 1)
                    dve.tensor_copy(kT1[0:QKD, 2 * j:2 * j + 2, :],
                                    ps[0:QKD, UP + j, :].rearrange("p (h t) -> p h t", h=2)).then_inc(S("kT"), 1)
                lo_until(FIRST["w_out"] + 3)
                for t in range(NH + 2):
                    if t < NH:
                        b = t % 2
                        dve.wait_ge(S("scores"), t + 1)
                        if t >= 2:
                            dve.wait_ge(S("probs_exp"), t - 1)
                        dve.tensor_reduce(nmx[b][:, 0:2], ps[:, b, :].rearrange("p (m t) -> p m t", m=2), AX, ALU.max,
                                          negate=True).then_inc(S("row_max"), 1)
                    if 1 <= t <= NH:
                        h = t - 1
                        b = h % 2
                        dve.wait_ge(S("probs_exp"), h + 1)
                        link(dve.reciprocal(rinv[b][:, 0:2], rsum[b][:, 0:2]))
                        for m in range(M):
                            tsc(prob[b][:, m, :], prob[b][:, m, :], rinv[b][:, m:m + 1], None, ALU.mult)\
                                .then_inc(S("probs"), 1)
                    if t >= 2:
                        h = t - 2
                        b = h % 2
                        dve.wait_ge(S("probs_turned"), h + 1)
                        if h >= 2:
                            dve.wait_ge(S("pv"), h - 1)
                        dve.tensor_copy(probT[b], ps[:, 2 + b, :].rearrange("p (k t) -> p k t", k=2))\
                            .then_inc(S("probT"), 1)
                        if h % 2 == 0 and h >= 2:
                            his[0] += 1
                            act_lo(ps[:, 4 + (h // 2 - 1) % 2, 0:T].unsqueeze(1), 4 + h // 2 - 1, 1, his[0])
                his[0] += 1
                act_lo(ps[:, 4 + 1, 0:T].unsqueeze(1), 7, 1, his[0])
                lo_until(FIRST["w_out"] + 6)
                post_norm(0)
                norm_turn(1)

                def mlp(n0, s):
                    done = 8 * s
                    blocks = MLP_BLOCKS * s

                    def square(i, ahead):
                        for j in range(2):
                            dve.wait_ge(S("half_copied"), 3 + 2 * blocks + 2 * i + j + 1)
                            c = slice(2 * j, 2 * j + 2)
                            link(tt(htmp[:, c, :], ps[:, UP + 2 * j:UP + 2 * j + 2, 0:T], htmp[:, c, :], ALU.add))
                            stt(hb[:, c, :], htmp[:, c, :], 0.0, htmp[:, c, :], ALU.max, ALU.mult)\
                                .then_inc(S("hidden"), 1)

                    def hidden_lo(i):
                        dve.wait_ge(S("hid_hi"), blocks + i + 1)
                        tt(hl2[:, 0:4, T:2 * T], hb, hl2[:, 0:4, 0:T].bitcast(F32), ALU.subtract)\
                            .then_inc(S("hid_lo"), 1)

                    lo_until(n0 + 3)
                    square(0, 0)
                    hidden_lo(0)
                    with dve.Fori(0, MLP_BLOCKS - 1) as i:
                        me.enter(i, 2)
                        lo(n0 + 4, i, 4)
                        lo(n0 + 5, i, 4)
                        square(i + 1, 0)
                        lo(n0 + 6, i, 4)
                        lo(n0 + 7, i, 4)
                        hidden_lo(i + 1)
                    me.leave(MLP_BLOCKS - 1)
                    cursor[0] = n0 + 4 * MLP_BLOCKS
                    lo_until(n0 + 4 * MLP_BLOCKS - 1 + 3)

                mlp(FIRST["mlp0"], 0)
                post_norm(1)
                norm_turn(2)

                link(dve.memset(upad[:, :, 0:CONV_PAD], 0.0))
                link(dve.memset(upad[:, :, CONV_PAD + T:UW], 0.0))
                for b in range(4):
                    n = FIRST["pw1"] + 2 * b + 1
                    lo_until(n + 3)
                    bank = (UP, ACC)[b % 2]
                    dve.wait_ge(S("pw_half"), b + 1)
                    for c in range(4):
                        bias = vcol("b_pw1", 2 * b + c if c < 2 else 8 + 2 * b + c - 2)
                        stt(ag[:, c, :], ps[:, bank + c, 0:T], bias, ptmp[:, c, :], ALU.add, ALU.add)\
                            .then_inc(S("ag"), 1)
                    dve.wait_ge(S("gate_tanh"), b + 1)
                    stt(upad[:, 2 * b:2 * b + 2, CONV_PAD:CONV_PAD + T], eg, 1.0, ag[:, 0:2, :], ALU.add, ALU.mult)\
                        .then_inc(S("u"), 1)
                    dve.wait_ge(S("u"), b + 1)
                for t in range(TAPS):
                    for c in DVE_TILES:
                        if t == 0:
                            ins = tsc(cv[:, c, :], upad[:, c, t:t + T], dwcol(t, c), vcol("b_dw", c), ALU.mult, ALU.add)
                        else:
                            ins = stt(cv[:, c, :], upad[:, c, t:t + T], dwcol(t, c), cv[:, c, :], ALU.mult, ALU.add)
                    if t < TAPS - 1:
                        link(ins)
                ins.then_inc(S("conv_dve"), 1)
                lo_until(FIRST["pw2"] + 3)
                for m in range(M):
                    dve.wait_ge(S("cv_turned"), m + 1)
                    for h in range(2):
                        ins = dve.bn_stats(bns[:, m, h, :], ps[:, ACC + 2 * m + h, :])
                    link(ins)
                    dve.bn_aggr(mv[:, m, :], bns[:, m, :, :]).then_inc(S("ln_stats"), 1)
                dve.wait_ge(S("ln_rstd"), 1)
                for m in range(M):
                    tsc(nrm[:, m, :], tall_out(ACC, m), mv[:, m, 0:1], rstd[:, m:m + 1], ALU.subtract, ALU.mult)\
                        .then_inc(S("normed"), 1)
                for j in range(4):
                    dve.wait_ge(S("z_tanh"), j + 1)
                    c = slice(2 * j, 2 * j + 2)
                    stt(zb[:, c, :], eb[:, c, :], 1.0, zb[:, c, :], ALU.add, ALU.mult).then_inc(S("silu"), 1)
                    his[0] += 1
                    act_lo(zb[:, c, :], 2 * j, 2, his[0], 0.5)
                lo_until(FIRST["mlp1"] - 1 + 3)
                post_norm(2)
                norm_turn(3)
                mlp(FIRST["mlp1"], 1)
                post_norm(3)
                norm_turn(4)

                def tab(c, m, *shape):
                    v = cst[:, c + 64 * m:c + 64 * m + 64]
                    for _ in shape:
                        v = v.unsqueeze(1)
                    return v.to_broadcast([P, *shape, 64])

                n = FIRST["w_in_2"]
                for c, (bank, h0, heads) in enumerate(((ACC, 0, 16), (UP, 8, 8))):
                    lo_until(n + 4 * c + 3 + 3)
                    piece_done(n + 4 * c + 3)
                    for m in range(M):
                        src = tall_out(bank, m).rearrange("p (h d) -> p h d", d=HD)[:, h0:h0 + heads, :]
                        dst = tok2.rearrange("p (m h d) -> p m h d", m=2, h=16)[:, m] if c == 0 else \
                            nqt[:, m, :].rearrange("p (h d) -> p h d", d=HD)
                        ta, tb = (t[:, 0:heads * HD].rearrange("p (h d) -> p h d", d=HD) for t in (t1, t2))
                        link(rope(dst, src, tab(C_COS, m, heads), tab(C_SIN, m, heads), ta, tb, HD // 2))
                    dve.sem_inc(S("roped"), 1)
                lo_until(n + 8 + 3 + 3)
                piece_done(n + 11)
                dve.wait_ge(S("dqk_turned"), 1)
                kd = tok2.rearrange("p (m a g u d) -> p m a g u d", m=2, a=4, g=2, u=2)
                for m in range(M):
                    src = tall_out(ACC, m, 768).rearrange("p (a v g d) -> p a v g d", a=3, v=2, g=2)[:, :, 0]
                    ta, tb = (t[:, 0:384].rearrange("p (a g d) -> p a g d", a=3, g=2) for t in (t1, t2))
                    link(rope(kd[:, m, 0:3, :, 0, :], src, tab(C_COS, m, 3, 2), tab(C_SIN, m, 3, 2), ta, tb, HD // 2))
                    ins = tt(kd[:, m, 0:3, :, 1, :], ta, tb, ALU.add)
                    link(ins)
                dve.sem_inc(S("roped"), 1)
                dve.wait_ge(S("gate_e"), 1)
                link(tsc(gates[:, :, :], gates[:, :, :], 1.0, 0.5, ALU.add, ALU.mult))
                dve.wait_ge(S("dqk_turned"), 1)
                for j in range(4):
                    dve.wait_ge(S("kd_turned"), j + 1)
                    dve.tensor_copy(kT2[:, j, :, :], ps[:, ACC + j, :].rearrange("p (g t) -> p g t", g=2))\
                        .then_inc(S("kT2"), 1)
                dve.wait_ge(S("kT2"), 4)
                for a_, kind in enumerate((0, 3)):
                    for par in range(2):
                        p0 = 64 * par
                        for g in range(2):
                            src = kT2[p0:p0 + 64, kind, g, :]
                            pos = vcol("kpos" if a_ == 0 else "vpos", 0, 16)[p0:p0 + 64, :]
                            win = src[:, 0:16 * 15].rearrange("p (n j q) -> p j n q", j=8, q=2)[:, :, :, par]
                            win2 = src[:, 16:256].rearrange("p (n j q) -> p j n q", j=8, q=2)[:, :, :, par]
                            for hh, wv in enumerate((win, win2)):
                                ins = tt(flat[p0:p0 + 64, a_, 8 * hh:8 * hh + 8, 15 * g:15 * g + 15], wv,
                                         pos[:, 8 * hh:8 * hh + 8].unsqueeze(2).to_broadcast([64, 8, 15]), ALU.add)
                link(ins)
                dve.sem_inc(S("flat"), 1)
                f2 = hl2[:, :, :].rearrange("p a b -> p (a b)")[:, 0:1920].rearrange("p (j n) -> p j n", j=32)
                dve.wait_ge(S("flat_hi"), 1)
                tt(f2[:, :, 30:60], flat.rearrange("p a j n -> p (a j) n"), f2[:, :, 0:30].bitcast(F32), ALU.subtract)\
                    .then_inc(S("flat_lo"), 1)
                lo_until(FIRST["w_out_2"] - 1 + 3)

                dve.wait_ge(S("hc_half"), 1)
                for a_ in range(2):
                    ins = tt(hidc[:, a_], ps[:, UP + 2 * a_:UP + 2 * a_ + 2, 0:30], hctmp[:, a_], ALU.add)
                ins.then_inc(S("hc"), 1)
                dve.wait_ge(S("hc_tanh"), 1)
                link(stt(hidc, hce, 1.0, hidc, ALU.add, ALU.mult))
                link(dve.memset(hidrep, 0.0))
                for c in range(2):
                    ins = dve.tensor_copy(
                        hidrep[:, c].rearrange("p (g r) n -> p g r n", g=2)[:, :, :, 0:15],
                        hidc[:, 1, c, :].rearrange("p (g n) -> p g n", g=2).unsqueeze(2).to_broadcast([P, 2, 4, 15]))
                ins.then_inc(S("hidc"), 1)
                for t in range(DH + 2):
                    if t < DH:
                        b = t % 2
                        dve.wait_ge(S("dscores"), t + 1)
                        if t >= 2:
                            dve.wait_ge(S("dexp"), t - 1)
                        dve.tensor_reduce(nmx[b][:, 0:2], ps[:, 2 * b:2 * b + 2, 0:128], AX, ALU.max, negate=True)
                        dve.tensor_reduce(nmx[b][:, 2:4], ps[:, 2 * b:2 * b + 2, 128:384], AX, ALU.max, negate=True)\
                            .then_inc(S("dmax"), 1)
                    if 1 <= t <= DH:
                        h = t - 1
                        b = h % 2
                        dve.wait_ge(S("dexp"), h + 1)
                        link(dve.reciprocal(rinv[b], rsum[b]))
                        for m in range(M):
                            ins = tt(cf[b][:, m:m + 1], rinv[b][:, 2 * m + 1:2 * m + 2], lamn[:, :], ALU.mult)
                        link(ins)
                        for m, c in enumerate((slice(0, 128), slice(128, 384))):
                            link(tsc(p2[b][:, 1, c], p2[b][:, 1, c], cf[b][:, m:m + 1], None, ALU.mult))
                            ins = stt(p2[b][:, 0, c], p2[b][:, 0, c], rinv[b][:, 2 * m:2 * m + 1], p2[b][:, 1, c],
                                      ALU.mult, ALU.add)
                        ins.then_inc(S("dprobs"), 1)
                    if t >= 2:
                        h = t - 2
                        dve.wait_ge(S("dpv"), h + 1)
                        dve.tensor_copy(od[:, 2 * h:2 * h + 2, :],
                                        ps[:, 6 + h % 2, 0:256].rearrange("p (m e) -> p m e", m=2)).then_inc(S("od"), 1)
                dve.wait_ge(S("od"), 4)
                sq = nrm[:, 1, :].rearrange("p (a e) -> p a e", a=8)
                link(tt(sq, od, od, ALU.mult))
                dve.tensor_reduce(ss8, sq, AX, ALU.add).then_inc(S("diff_ssq"), 1)
                dve.wait_ge(S("diff_rstd"), 1)
                link(tt(od, od, rs8.unsqueeze(2).to_broadcast([P, 8, P]), ALU.mult))
                stt(od, od, 1.0 - LAM_INIT, bc[:, 640:768].unsqueeze(1).to_broadcast([P, 8, P]), ALU.mult, ALU.mult)\
                    .then_inc(S("o_normed"), 1)
                for j in range(2):
                    his[0] += 1
                    act_lo(turned(ACC, 2 * j, 2), 2 * j, 2, his[0])

                dve.wait_ge(S("cmp_kv"), 1)
                tsc(kcT, ps[:, UP, 0:30], 0.5, None, ALU.mult).then_inc(S("kcT"), 1)
                stt(vsel, ps[:, UP + 1, 0:64].unsqueeze(1).to_broadcast([P, 8, 64]), 0.5,
                    cst[:, C_BLK:C_BLK + 8].unsqueeze(2).to_broadcast([P, 8, 64]), ALU.mult, ALU.mult)\
                    .then_inc(S("vsel"), 1)
                dve.wait_ge(S("cscores"), 1)
                for par in range(2):
                    neg = cst[:, C_CNEG:C_CNEG + 32].rearrange("p (m n) -> p m n", m=2)[:, :, 0:15]
                    ins = tt(pc[:, par, :, :, 0:15],
                             ps[:, UP + 2 + par, 0:128].rearrange("p (h m n) -> p h m n", h=4, m=2)[:, :, :, 0:15],
                             neg.unsqueeze(1).to_broadcast([P, 4, 2, 15]), ALU.add)
                link(ins)
                pcv = nrm[:, 0, 0:256].rearrange("p (r n) -> p r n", n=16)[:, :, 0:15]
                link(dve.tensor_reduce(cmx, pcv, AX, ALU.max))
                tt(pcv, pcv, cmx.unsqueeze(2).to_broadcast([P, 16, 15]), ALU.subtract).then_inc(S("cshift"), 1)
                dve.wait_ge(S("cexp"), 1)
                link(dve.tensor_reduce(crs, pcv, AX, ALU.add))
                link(dve.reciprocal(crs, crs))
                crv = crs.rearrange("p (a h m) -> p a h m", a=2, h=4)
                gv = gates[:, :, :].rearrange("p m (h a b) -> p a h m b", a=2, b=3)
                for par in range(2):
                    ins = tt(crv[:, par], crv[:, par], gv[:, par, :, :, 0], ALU.mult)
                link(ins)
                link(tt(pcv, pcv, crs.unsqueeze(2).to_broadcast([P, 16, 15]), ALU.mult))
                link(dve.memset(pcm, 0.0))
                pmv = pcm.rearrange("p m (h a) n -> p a h m n", a=2)
                one = cst[:, C_CONE:C_CONE + 32].rearrange("p (m n) -> p m n", m=2)[:, :, 0:15]
                for par in range(2):
                    ins = tt(pmv[:, par, :, :, 0:15], pc[:, par, :, :, 0:15], one.unsqueeze(1).to_broadcast([P, 4, 2, 15]),
                             ALU.mult)
                ins.then_inc(S("pcm"), 1)
                dve.wait_ge(S("pcm_turned"), 1)
                dve.tensor_copy(pcT, ps[:, UP, 0:256]).then_inc(S("pcT"), 1)

                for t in range(NH + 2):
                    if t < NH:
                        b = t % 2
                        dve.wait_ge(S("nscores"), t + 1)
                        if t >= 2:
                            dve.wait_ge(S("nexp"), t - 1)
                        dve.tensor_reduce(nmx[b][:, 0:2], ps[:, 2 * b:2 * b + 2, 0:128], AX, ALU.max, negate=True)
                        dve.tensor_reduce(nmx[b][:, 2:4], ps[:, 2 * b:2 * b + 2, 128:384], AX, ALU.max, negate=True)\
                            .then_inc(S("nmax"), 1)
                    if 1 <= t <= NH:
                        h = t - 1
                        b = h % 2
                        dve.wait_ge(S("nexp"), h + 1)
                        link(dve.reciprocal(rinv[b], rsum[b]))
                        gt = gates[:, :, 3 * h + 1:3 * h + 3]
                        link(tt(cf[b].rearrange("p (m a) -> p m a", m=2), rinv[b].rearrange("p (m a) -> p m a", m=2),
                                gt, ALU.mult))
                        for m, c in enumerate((slice(0, 128), slice(128, 384))):
                            for a_ in range(2):
                                ins = tsc(p2[b][:, a_, c], p2[b][:, a_, c], cf[b][:, 2 * m + a_:2 * m + a_ + 1], None,
                                          ALU.mult)
                        ins.then_inc(S("nprobs"), 1)
                    if t >= 3 and t % 2 == 1:
                        h = t - 2
                        his[0] += 1
                        act_lo(ps[:, 6 + (h // 2) % 2, 0:T].unsqueeze(1), 4 + h // 2, 1, his[0])
                lo_until(FIRST["ffn"] - 1 + 3)
                post_norm(4)
                norm_turn(5)

                f0 = FIRST["ffn"]

                def silu_gate(i):
                    for j in range(2):
                        dve.wait_ge(S("ff_half"), 2 * i + j + 1)
                        dst = (gsum, usum)[j]
                        tt(dst, ps[:, UP + 2 * j:UP + 2 * j + 2, 0:T], htmp[:, 2 * j:2 * j + 2, :], ALU.add)\
                            .then_inc(S("ff_sum"), 1)
                    dve.wait_ge(S("ff_tanh"), i + 1)
                    link(stt(gsum, esum, 1.0, gsum, ALU.add, ALU.mult))
                    tt(hb[:, 0:2, :], gsum, usum, ALU.mult).then_inc(S("ff_hidden"), 1)

                def ff_lo(i):
                    dve.wait_ge(S("ff_hi"), i + 1)
                    stt(hl2[:, 0:2, T:2 * T], hb[:, 0:2, :], 0.5, hl2[:, 0:2, 0:T].bitcast(F32), ALU.mult, ALU.subtract)\
                        .then_inc(S("ff_lo"), 1)

                lo_until(f0 + 2)
                silu_gate(0)
                lo_until(f0 + 3)
                ff_lo(0)
                with dve.Fori(0, FF_BLOCKS - 2) as i:
                    me.enter(i, 1)
                    lo(f0 + 4, i, 3)
                    lo(f0 + 5, i, 3)
                    silu_gate(i + 1)
                    lo(f0 + 6, i, 3)
                    ff_lo(i + 1)
                me.leave(FF_BLOCKS - 2)
                cursor[0] = f0 + 4 + 3 * (FF_BLOCKS - 2)
                lo_until(N_PIECES)
                silu_gate(FF_BLOCKS - 1)
                ff_lo(FF_BLOCKS - 1)
                post_norm(5)

            @block.scalar
            def _(act):
                me = Steps(act, S("act_step"))
                link = me.link
                f = act.activation

                def small(dst, src, sem="small"):
                    act.dma_start(dst, src).then_inc(S(sem), 16)

                small(cst[:, :], a["shape_constants"], "rows_in")
                for name, src in (("b_pw1", a["odd_b_pw1"][0]), ("b_dw", a["odd_b_dw"][0]), ("ln_g", a["odd_ln_g"][0]),
                                  ("ln_b", a["odd_ln_b"][0])):
                    n = src.shape[0] // P
                    small(rows[VC[name]:VC[name] + n, 0, :], src.rearrange("(k p) -> k p", p=P), "rows_in")
                small(rows[VC["sc"]:VC["sc"] + 12, 0, :], a["even_sc_kernel"][0].rearrange("t (c p) -> (t c) p", p=P),
                      "rows_in")
                for name, src in (("kpos", a["k_cmp_pos_2"][0]), ("vpos", a["v_cmp_pos_2"][0])):
                    small(rows[VC[name]:VC[name] + 16, 0, :], src.rearrange("(j q) d -> j (q d)", q=2), "rows_in")
                dw = a["odd_w_dw"][0].rearrange("t (c p) -> (t c) p", p=P)
                for i in range(2):
                    small(rows[0:DROWS, 1 + i, :], dw[DROWS * i:DROWS * (i + 1), :], "rows_in")
                act.dma_start(posi[:, :], a["positions"][0].rearrange("(m p) -> p m", p=P),
                              allow_slow_non_contiguous=True).then_inc(S("small"), 16)
                at = 0
                for src in (a["even_q_norm"][0], a["even_kv_norm"][0], a["diff_subln_2"][0], a["lambda_q1_2"][0],
                            a["lambda_k1_2"][0], a["lambda_q2_2"][0], a["lambda_k2_2"][0]):
                    n = src.shape[0]
                    small(bc[:, at:at + n], src.partition_broadcast(P))
                    at += n
                for u in range(2):
                    small(w2k[:, :, u, :], view_k(a["k_cmp_w2_2"][0]))
                small(w2v[:, :, :], view_k(a["v_cmp_w2_2"][0]))

                his = [0]

                def piece_done(n, turn=0, per=0):
                    act.wait_ge(S("pe_piece"), turn * per + n + 1)

                def sum_squares(m, src):
                    f(nrm[:, m, :], src, ACT.Square, accum_out=ss[:, m:m + 1]).then_inc(S("ssq"), 1)

                def act_high(src, k0, n, scale=1.0):
                    f(act_hl[:, k0:k0 + n, 0:T], src, ACT.Copy, scale=scale).then_inc(S("act_hi"), 1)

                turns = [0]

                def norm_turn(s):
                    for m in range(M):
                        if s == 0:
                            act.wait_ge(S(f"x_in{m}"), 16)
                        else:
                            act.wait_ge(S("x_new"), 2 * (s - 1) + m + 1)
                        sum_squares(m, x[:, m, :])
                    high_of_turned(TURN_BANK[s], 4)

                def high_of_turned(bank, pairs):
                    for j in range(pairs):
                        turns[0] += 1
                        act.wait_ge(S("turned"), turns[0])
                        act_high(turned(bank, 2 * j, 2), 2 * j, 2)

                def post_norm(n):
                    piece_done(n)
                    for m in range(M):
                        sum_squares(m, tall_out(ACC, m))

                norm_turn(0)
                for i in range(2):
                    act.wait_ge(S("angles"), i + 1)
                    red = rt[:, 4 + i:5 + i, 0:32].rearrange("p o (m f) -> p (o m) f", m=2)
                    f(cs1[:, i, :, 16 * i:16 * i + 16], red, ACT.Sin).then_inc(S("sines"), 1)
                act.wait_ge(S("lam_sums"), 1)
                act.wait_ge(S("dve_step"), 1)
                f(lam4[:, 2:4], lam4[:, 0:2], ACT.Exp).then_inc(S("lam_exp"), 1)
                for b in range(3):
                    piece_done(FIRST["w_in_wide"] + 2 * b + 1)
                    if b:
                        act.wait_ge(S("wide_read"), b)
                    bank = (UP, ACC, UP)[b]
                    f(ctmp, ps[:, bank:bank + 4, T:2 * T], ACT.Copy).then_inc(S("half_copied"), 1)
                piece_done(FIRST["w_uq"] - 1)
                for c0, c1, i in ((0, QR, 0), (QR, QR + KVR, 2)):
                    for m in range(M):
                        f(lat[:, m, c0:c1], tall_out(ACC, m)[:, c0:c1], ACT.Square, accum_out=ss4[:, i + m:i + m + 1])\
                            .then_inc(S("lat_ssq"), 1)
                for i, (k, n) in enumerate(((0, 2), (2, 2), (4, 1))):
                    act.wait_ge(S("lat_turned"), i + 1)
                    f(hl2[:, k:k + n, 0:T], turned(UP, k, n), ACT.Copy).then_inc(S("lat_hi"), 1)
                act.wait_ge(S("ya"), 1)
                act_high(gate_b, 0, 4)
                piece_done(FIRST["w_uq"] + 1)
                for m in range(M):
                    src = tall_out(ACC, m, NH * QKD).rearrange("p (h d) -> p h d", h=NH)[:, :, 0:NOPE]
                    f(qf[:, m, :, 0:NOPE], src, ACT.Copy).then_inc(S("q_nope"), 1)
                piece_done(FIRST["w_ukv"])
                for m in range(M):
                    src = tall_out(UP, m).rearrange("p (h d) -> p h d", h=NH)
                    f(kf[:, m, :, 0:NOPE], src[:, :, 0:NOPE], ACT.Copy)
                    f(v1[:, m, :, :], src[:, :, NOPE:NOPE + VD], ACT.Copy).then_inc(S("kv_nope"), 1)
                act.wait_ge(S("act_lo"), 5)
                for j in range(4):
                    act.wait_ge(S("q_turned"), j + 1)
                    f(qT[0:QKD, 2 * j:2 * j + 2, :], ps[0:QKD, ACC + j, :].rearrange("p (h t) -> p h t", h=2),
                      ACT.Copy, scale=float(QKD) ** -0.5).then_inc(S("qT"), 1)

                def pair_out(h, sem, bank, k0):
                    act.wait_ge(S(sem), h + 1)
                    act_high(ps[:, bank, 0:T].unsqueeze(1), k0, 1)

                for h in range(NH):
                    b = h % 2
                    act.wait_ge(S("row_max"), h + 1)
                    if h >= 2:
                        act.wait_ge(S("probs_turned"), h - 1)
                    for m in range(M):
                        ins = f(prob[b][:, m, :], ps[:, b, m * T:(m + 1) * T], ACT.Exp, bias=nmx[b][:, m:m + 1],
                                accum_out=rsum[b][:, m:m + 1])
                    ins.then_inc(S("probs_exp"), 1)
                    if h % 2 == 0 and h >= 4:
                        pair_out(h - 3, "pv", 4 + (h // 2 - 2) % 2, 4 + h // 2 - 2)
                pair_out(5, "pv", 4, 6)
                pair_out(7, "pv", 5, 7)
                post_norm(FIRST["mlp0"] - 1)
                norm_turn(1)

                def mlp(n0, s):
                    blocks = MLP_BLOCKS * s

                    def half_copy(i, turn):
                        piece_done(n0 + 1 if turn is None else n0 + 3, 0 if turn is None else turn, 4)
                        for j in range(2):
                            if turn is not None:
                                act.wait_ge(S("hidden"), 2 * blocks + 2 * i - 1 + j)
                            f(htmp[:, 2 * j:2 * j + 2, :], ps[:, UP + 2 * j:UP + 2 * j + 2, T:2 * T], ACT.Copy)\
                                .then_inc(S("half_copied"), 1)

                    def hidden_hi(i):
                        act.wait_ge(S("hidden"), 2 * blocks + 2 * i + 2)
                        f(hl2[:, 0:4, 0:T], hb, ACT.Copy).then_inc(S("hid_hi"), 1)

                    half_copy(0, None)
                    hidden_hi(0)
                    with act.Fori(0, MLP_BLOCKS - 1) as i:
                        half_copy(i + 1, i)
                        piece_done(n0 + 5, i, 4)
                        hidden_hi(i + 1)
                    post_norm(n0 + 4 * MLP_BLOCKS - 1)

                mlp(FIRST["mlp0"], 0)
                norm_turn(2)

                for b in range(4):
                    piece_done(FIRST["pw1"] + 2 * b + 1)
                    if b:
                        act.wait_ge(S("ag"), 4 * b)
                    bank = (UP, ACC)[b % 2]
                    f(ptmp, ps[:, bank:bank + 4, T:2 * T], ACT.Copy).then_inc(S("pw_half"), 1)
                    act.wait_ge(S("ag"), 4 * b + 4)
                    if b:
                        act.wait_ge(S("u"), b)
                    f(eg, ag[:, 2:4, :], ACT.Tanh, scale=0.5).then_inc(S("gate_tanh"), 1)
                i = 0
                for q, c in enumerate(PE_TILES):
                    for t in range(TAPS):
                        if i >= DIAGS:
                            act.wait_ge(S("diag_used"), i - DIAGS + 1)
                        f(diag[:, i % DIAGS, :], ident, ACT.Copy, scale=dwcol(t, c)).then_inc(S("diag"), 1)
                        i += 1
                    act.wait_ge(S("diag_used"), i)
                    f(cv[:, c, :], ps[:, UP + q, 0:T], ACT.Identity, bias=vcol("b_dw", c)).then_inc(S("conv_act"), 1)
                for k in range(KD):
                    act.wait_ge(S("turned"), turns[0] + k // 2 + 1)
                    f(zb[:, k, :], turned(UP, k, 1)[:, 0, :], ACT.Identity, bias=vcol("ln_b", k), scale=vcol("ln_g", k))\
                        .then_inc(S("z"), 1)
                    if k % 2:
                        act.wait_ge(S("z"), k + 1)
                        f(eb[:, k - 1:k + 1, :], zb[:, k - 1:k + 1, :], ACT.Tanh, scale=0.5).then_inc(S("z_tanh"), 1)
                turns[0] += 4
                for j in range(4):
                    act.wait_ge(S("silu"), j + 1)
                    act_high(zb[:, 2 * j:2 * j + 2, :], 2 * j, 2, 0.5)
                post_norm(FIRST["mlp1"] - 1)
                norm_turn(3)
                mlp(FIRST["mlp1"], 1)
                norm_turn(4)

                n = FIRST["w_in_2"]
                piece_done(n + 7)
                for m in range(M):
                    ins = f(dv[:, m, :], tall_out(UP, m)[:, 0:512], ACT.Copy)
                ins.then_inc(S("dv"), 1)
                for j in range(4):
                    act.wait_ge(S("dqk_turned4"), j + 1)
                    f(dqkT[:, 2 * j:2 * j + 2, :], ps[:, UP + j, :].rearrange("p (h t) -> p h t", h=2), ACT.Copy,
                      scale=HD ** -0.5 if j < 2 else 1.0).then_inc(S("dqkT"), 1)
                act.wait_ge(S("roped"), 3)
                for m in range(M):
                    src = tall_out(ACC, m)[:, 0:792]
                    f(vsw[:, m, :, :], src[:, 256:768].rearrange("p (a v n) -> p a v n", a=2, v=2)[:, :, 1, :], ACT.Copy)
                    f(gates[:, m, :], src[:, 768:792], ACT.Tanh, scale=0.5)
                    kd = tok2.rearrange("p (m a g u d) -> p m a g u d", m=2, a=4, g=2, u=2)
                    for u in range(2):
                        ins = f(kd[:, m, 3, :, u, :], src[:, 128:256].rearrange("p (g d) -> p g d", g=2), ACT.Copy)
                ins.then_inc(S("gate_e"), 1)
                for j in range(2):
                    act.wait_ge(S("nq_turned"), j + 1)
                    f(nqT[:, 2 * j:2 * j + 2, :], ps[:, UP + j, :].rearrange("p (h t) -> p h t", h=2), ACT.Copy,
                      scale=HD ** -0.5).then_inc(S("nqT"), 1)
                f2 = hl2[:, :, :].rearrange("p a b -> p (a b)")[:, 0:1920].rearrange("p (j n) -> p j n", j=32)
                act.wait_ge(S("flat"), 1)
                f(f2[:, :, 0:30], flat.rearrange("p a j n -> p (a j) n"), ACT.Copy).then_inc(S("flat_hi"), 1)
                piece_done(FIRST["w_out_2"] - 1)
                for a_ in range(2):
                    ins = f(hctmp[:, a_], ps[:, UP + 2 * a_:UP + 2 * a_ + 2, 30:60], ACT.Copy)
                ins.then_inc(S("hc_half"), 1)
                act.wait_ge(S("hc"), 1)
                f(hce, hidc, ACT.Tanh, scale=0.5).then_inc(S("hc_tanh"), 1)

                for t in range(DH + 1):
                    if t < DH:
                        b = t % 2
                        act.wait_ge(S("dmax"), t + 1)
                        if t >= 2:
                            act.wait_ge(S("daT"), t - 1)
                        for m, c in enumerate((slice(0, 128), slice(128, 384))):
                            for j in range(2):
                                k = 2 * m + j
                                ins = f(p2[b][:, j, c], ps[:, 2 * b + j, c], ACT.Exp, bias=nmx[b][:, k:k + 1],
                                        accum_out=rsum[b][:, k:k + 1])
                        ins.then_inc(S("dexp"), 1)
                    if t >= 1:
                        h = t - 1
                        act.wait_ge(S("daT"), h + 1)
                        if h >= 2:
                            act.wait_ge(S("dpv"), h - 1)
                        f(pt2[h % 2][:, 0, :], ps[:, 4 + h % 2, 0:384], ACT.Copy).then_inc(S("dpT"), 1)
                high_of_turned(ACC, 2)
                act.wait_ge(S("cshift"), 1)
                pcv = nrm[:, 0, 0:256].rearrange("p (r n) -> p r n", n=16)[:, :, 0:15]
                f(pcv, pcv, ACT.Exp).then_inc(S("cexp"), 1)
                for t in range(NH + 2):
                    if t < NH:
                        b = t % 2
                        act.wait_ge(S("nmax"), t + 1)
                        if t >= 2:
                            act.wait_ge(S("naT"), t - 1)
                        for m, c in enumerate((slice(0, 128), slice(128, 384))):
                            for j in range(2):
                                k = 2 * m + j
                                ins = f(p2[b][:, j, c], ps[:, 2 * b + j, c], ACT.Exp, bias=nmx[b][:, k:k + 1],
                                        accum_out=rsum[b][:, k:k + 1])
                        ins.then_inc(S("nexp"), 1)
                    if 1 <= t <= NH:
                        h = t - 1
                        act.wait_ge(S("naT"), h + 1)
                        if h >= 2:
                            act.wait_ge(S("npv"), h - 1)
                        f(pt2[h % 2], ps[:, 4:6, 0:384], ACT.Copy).then_inc(S("npT"), 1)
                    if t >= 3 and t % 2 == 1:
                        h = t - 2
                        pair_out(h, "npv", 6 + (h // 2) % 2, 4 + h // 2)
                post_norm(FIRST["ffn"] - 1)
                norm_turn(5)
                f0 = FIRST["ffn"]

                def gate_half(i, turn):
                    piece_done(f0 + 1 if turn is None else f0 + 3, 0 if turn is None else turn, 3)
                    for j in range(2):
                        if turn is not None:
                            act.wait_ge(S("ff_sum"), 2 * i - 1 + j)
                        f(htmp[:, 2 * j:2 * j + 2, :], ps[:, UP + 2 * j:UP + 2 * j + 2, T:2 * T], ACT.Copy)\
                            .then_inc(S("ff_half"), 1)
                    act.wait_ge(S("ff_sum"), 2 * i + 1)
                    if turn is not None:
                        act.wait_ge(S("ff_hidden"), i)
                    f(esum, gsum, ACT.Tanh, scale=0.5).then_inc(S("ff_tanh"), 1)

                def ff_hi(i):
                    act.wait_ge(S("ff_hidden"), i + 1)
                    f(hl2[:, 0:2, 0:T], hb[:, 0:2, :], ACT.Copy, scale=0.5).then_inc(S("ff_hi"), 1)

                gate_half(0, None)
                ff_hi(0)
                with act.Fori(0, FF_BLOCKS - 1) as i:
                    gate_half(i + 1, i)
                    piece_done(f0 + 4, i, 3)
                    ff_hi(i + 1)
                post_norm(N_PIECES - 1)

            @block.tensor
            def _(pe):
                def mm(o, l, r, start, stop):
                    return pe.matmul(o, l, r, start=start, stop=stop, skip_group_check=True)

                def turn(o, src):
                    return pe.transpose(o, src, ident[0:src.shape[0], 0:src.shape[0]])

                def arrived(n, turn_=0, per=0):
                    pe.wait_ge(S("w_split"), turn_ * per + n + 1)

                def wide(n, bank, lhs_k0, moving, first, last, k, cols, turn_=0, per=0):
                    arrived(n, turn_, per)
                    wh = w_hi[slot_of(n)][:, 0:k * cols].rearrange("p (k n) -> p k n", k=k)
                    wl = w_lo[slot_of(n)][:, 0:k * cols].rearrange("p (k n) -> p k n", k=k)
                    width = moving.shape[2]
                    for kk in range(k):
                        for c in range(cols // P):
                            act_k = moving[:, lhs_k0 + kk, :]
                            s = slice(c * P, (c + 1) * P)
                            mm(ps[:, bank + c, 0:width], wh[:, kk, s], act_k, first and kk == 0, False)
                            ins = mm(ps[:, bank + c, 0:width // 2], wl[:, kk, s], act_k[:, 0:width // 2],
                                     False, last and kk == k - 1)
                    ins.then_inc(S("pe_piece"), 1)

                def tall(n, bank, lhs, lhs_k0, first, last, k, cols, turn_=0, per=0):
                    arrived(n, turn_, per)
                    wh = w_hi[slot_of(n)][:, 0:k * cols].rearrange("p (k n) -> p k n", k=k)
                    wl = w_lo[slot_of(n)][:, 0:k * cols].rearrange("p (k n) -> p k n", k=k)
                    for kk in range(k):
                        for m in range(M):
                            h = lhs[:, lhs_k0 + kk, m * P:(m + 1) * P]
                            l = lhs[:, lhs_k0 + kk, T + m * P:T + (m + 1) * P]
                            for part, (lt, w) in enumerate(((h, wh), (h, wl), (l, wh))):
                                for j, c0 in enumerate(range(0, cols, 512)):
                                    c1 = min(cols, c0 + 512)
                                    ins = mm(ps[:, bank + 2 * m + j, 0:c1 - c0], lt, w[:, kk, c0:c1],
                                             first and kk == 0 and part == 0, last and kk == k - 1 and part == 2)
                    ins.then_inc(S("pe_piece"), 1)

                normed, lows = [0], [0]

                def turn_normed(bank=ACC):
                    for k in range(KD):
                        for m in range(M):
                            pe.wait_ge(S("normed"), normed[0] + m + 1)
                            ins = turn(turned(bank, k, 1)[:, 0, m * P:(m + 1) * P], nrm[:, m, k * P:(k + 1) * P])
                        if k % 2:
                            ins.then_inc(S("turned"), 1)
                    normed[0] += 2

                def need_lows(n):
                    pe.wait_ge(S("act_lo"), n)

                pe.wait_ge(S("rows_in"), 16 * 10)
                for i in range(3):
                    n = VROWS if i == 0 else DROWS
                    turn(ps[:, UP + i, 0:n], rows[0:n, i, :]).then_inc(S("cols"), 1)
                turn_normed()
                n = FIRST["w_in_wide"]
                for b in range(3):
                    if b == 2:
                        pe.wait_ge(S("wide_read"), 1)
                    for h in range(2):
                        need_lows(2 * h + 2 if b == 0 else 4)
                        wide(n + 2 * b + h, (UP, ACC, UP)[b], 4 * h, act_hl, h == 0, h == 1, 4, 512)
                pe.wait_ge(S("wide_read"), 2)
                for j, (k, kn) in enumerate(TALL_K):
                    tall(FIRST["w_in_tall"] + j, ACC, act_hl, k, j == 0, j == 2, kn, A_COLS)
                pe.wait_ge(S("wide_read"), 3)
                for i, (k, kn) in enumerate(((0, 2), (2, 2), (4, 1))):
                    for kk in range(k, k + kn):
                        for m in range(M):
                            pe.wait_ge(S("lat_normed"), m + 1)
                            ins = turn(turned(UP, kk, 1)[:, 0, m * P:(m + 1) * P], lat[:, m, kk * P:(kk + 1) * P])
                    ins.then_inc(S("lat_turned"), 1)
                pe.wait_ge(S("kpe"), 1)
                for j, (k, kn) in enumerate(UQ_K):
                    pe.wait_ge(S("lat_lo"), (1, 2)[j])
                    tall(FIRST["w_uq"] + j, ACC, hl2, k, j == 0, j == 1, kn, NH * QKD)
                pe.wait_ge(S("lat_lo"), 3)
                tall(FIRST["w_ukv"], UP, hl2, 3, True, True, 2, 1024)
                pe.wait_ge(S("q_nope"), 2)
                pe.wait_ge(S("q_rope"), 2)
                for h in range(NH):
                    for m in range(M):
                        ins = turn(ps[0:QKD, ACC + h // 2, (h % 2) * T + m * P:(h % 2) * T + (m + 1) * P], qf[:, m, h, :])
                    if h % 2:
                        ins.then_inc(S("q_turned"), 1)
                pe.wait_ge(S("kv_nope"), 2)
                for h in range(NH):
                    for m in range(M):
                        ins = turn(ps[0:QKD, UP + h // 2, (h % 2) * T + m * P:(h % 2) * T + (m + 1) * P], kf[:, m, h, :])
                    if h % 2:
                        ins.then_inc(S("k_turned"), 1)
                pe.wait_ge(S("qT"), 4)
                for t in range(NH + 2):
                    if t < NH:
                        if t % 2 == 0:
                            pe.wait_ge(S("kT"), t // 2 + 1)
                        if t >= 2:
                            pe.wait_ge(S("probs_exp"), t - 1)
                        for m in range(M):
                            ins = mm(ps[:, t % 2, m * T:(m + 1) * T], qT[0:QKD, t, m * P:(m + 1) * P], kT1[0:QKD, t, :],
                                     True, True)
                        ins.then_inc(S("scores"), 1)
                    if 1 <= t <= NH:
                        h = t - 1
                        if h >= 2:
                            pe.wait_ge(S("probT"), h - 1)
                        for m in range(M):
                            pe.wait_ge(S("probs"), 2 * h + m + 1)
                            for k in range(M):
                                ins = turn(ps[:, 2 + h % 2, k * T + m * P:k * T + (m + 1) * P],
                                           prob[h % 2][:, m, k * P:(k + 1) * P])
                        ins.then_inc(S("probs_turned"), 1)
                    if t >= 2:
                        h = t - 2
                        if h == 0:
                            pe.wait_ge(S("kT"), 4)
                        pe.wait_ge(S("probT"), h + 1)
                        if h % 2 == 0 and h >= 4:
                            need_lows(5 + h // 2 - 1)
                        r = 64 * (h % 2)
                        for k in range(M):
                            ins = mm(ps[r:r + 64, 4 + (h // 2) % 2, 0:T], v1[:, k, h, :], probT[h % 2][:, k, :],
                                     k == 0, k == 1)
                        ins.then_inc(S("pv"), 1)
                need_lows(9)
                for j in range(4):
                    tall(FIRST["w_out"] + j, ACC, act_hl, 2 * j, j == 0, j == 3, 2, 1024)
                turn_normed()
                lows[0] = 9

                def mlp(n0, s):
                    blocks = MLP_BLOCKS * s
                    for h in range(2):
                        need_lows(lows[0] + 2 * h + 2)
                        wide(n0 + h, UP, 4 * h, act_hl, h == 0, h == 1, 4, 512)
                    def up(n, i, per):
                        for h in range(2):
                            wide(n + h, UP, 4 * h, act_hl, h == 0, h == 1, 4, 512, i, per)

                    def down(n, i, per, first):
                        for h in range(2):
                            tall(n + h, ACC, hl2, 2 * h, first and h == 0, False, 2, 1024, i, per)

                    pe.wait_ge(S("hidden"), 2 * blocks + 2)
                    up(n0 + 2, 0, 0)
                    pe.wait_ge(S("hid_lo"), blocks + 1)
                    down(n0 + 4, 0, 0, True)
                    with pe.Fori(1, MLP_BLOCKS - 1) as i:
                        pe.wait_ge(S("hidden"), 2 * i + 2 * blocks + 2)
                        up(n0 + 2, i, 4)
                        pe.wait_ge(S("hid_lo"), i + blocks + 1)
                        down(n0 + 4, i, 4, False)
                    pe.wait_ge(S("hid_lo"), blocks + MLP_BLOCKS)
                    down(n0 + 4 * MLP_BLOCKS - 2, 0, 0, False)
                    turn_normed(TURN_BANK[2 * s + 2])
                    lows[0] += 4

                mlp(FIRST["mlp0"], 0)
                for b in range(4):
                    if b >= 2:
                        pe.wait_ge(S("ag"), 4 * (b - 1))
                    for h in range(2):
                        need_lows(lows[0] + (2 * h + 2 if b == 0 else 4))
                        wide(FIRST["pw1"] + 2 * b + h, (UP, ACC)[b % 2], 4 * h, act_hl, h == 0, h == 1, 4, 512)
                lows[0] += 4
                i = 0
                pe.wait_ge(S("ag"), 12)
                for q, c in enumerate(PE_TILES):
                    pe.wait_ge(S("u"), c // 2 + 1)
                    for t in range(TAPS):
                        pe.wait_ge(S("diag"), i + 1)
                        mm(ps[:, UP + q, 0:T], diag[:, i % DIAGS, :], upad[:, c, t:t + T], t == 0, t == TAPS - 1)\
                            .then_inc(S("diag_used"), 1)
                        i += 1
                pe.wait_ge(S("ag"), 16)
                pe.wait_ge(S("conv_act"), len(PE_TILES))
                pe.wait_ge(S("conv_dve"), 1)
                for m in range(M):
                    for c in range(KD):
                        ins = turn(tall_out(ACC, m)[:, c * P:(c + 1) * P], cv[:, c, m * P:(m + 1) * P])
                    ins.then_inc(S("cv_turned"), 1)
                turn_normed(UP)
                for j in range(4):
                    need_lows(lows[0] + j + 1)
                    if j == 0:
                        pe.wait_ge(S("ones"), 1)
                        pe.wait_ge(S("b_pw2"), 16)
                        for m in range(M):
                            for h in range(2):
                                mm(ps[:, ACC + 2 * m + h, :], ones[:, :], brow[0:1, 512 * h:512 * h + 512],
                                   True, False)
                    tall(FIRST["pw2"] + j, ACC, act_hl, 2 * j, False, j == 3, 2, 1024)
                lows[0] += 4
                turn_normed()
                mlp(FIRST["mlp1"], 1)

                n = FIRST["w_in_2"]
                for c, (bank, cols) in enumerate(((ACC, 1024), (UP, 1024), (ACC, 792))):
                    if c == 1:
                        need_lows(lows[0] + 4)
                    if c == 2:
                        pe.wait_ge(S("roped"), 1)
                    for j in range(4):
                        need_lows(lows[0] + (j + 1 if c == 0 else 4))
                        tall(n + 4 * c + j, bank, act_hl, 2 * j, j == 0, j == 3, 2, cols)
                lows[0] += 4
                pe.wait_ge(S("roped"), 2)
                pe.wait_ge(S("dv"), 1)
                tk = tok2.rearrange("p (m h d) -> p m h d", m=2, h=8)
                for h in range(8):
                    for m in range(M):
                        ins = turn(ps[:, UP + h // 2, (h % 2) * T + m * P:(h % 2) * T + (m + 1) * P], tk[:, m, h, :])
                    if h % 2:
                        ins.then_inc(S("dqk_turned4"), 1)
                pe.nop().then_inc(S("dqk_turned"), 1) if False else None
                for h in range(4):
                    if h % 2 == 0:
                        pe.wait_ge(S("dqkT"), h // 2 + 1)
                    for m in range(M):
                        ins = turn(ps[:, UP + h // 2, (h % 2) * T + m * P:(h % 2) * T + (m + 1) * P],
                                   nqt[:, m, h * P:(h + 1) * P])
                    if h == 0:
                        ins.then_inc(S("dqk_turned"), 1)
                    elif h % 2:
                        ins.then_inc(S("nq_turned"), 1)
                pe.wait_ge(S("roped"), 3)
                pe.wait_ge(S("gate_e"), 1)
                kd = tok2.rearrange("p (m a n) -> p m a n", m=2, a=8)
                for q in range(8):
                    for m in range(M):
                        ins = turn(ps[:, ACC + q // 2, (q % 2) * T + m * P:(q % 2) * T + (m + 1) * P], kd[:, m, q, :])
                    if q % 2:
                        ins.then_inc(S("kd_turned"), 1)
                f2 = hl2[:, :, :].rearrange("p a b -> p (a b)")[:, 0:1920].rearrange("p (j n) -> p j n", j=32)
                pe.wait_ge(S("flat_lo"), 1)
                pe.wait_ge(S("dqkT"), 4)
                pe.wait_ge(S("nqT"), 2)
                for a_ in range(2):
                    for h in range(2):
                        wide(FIRST["cmp"] + 2 * a_ + h, UP + 2 * a_, 16 * a_ + 8 * h, f2, h == 0, h == 1, 8, 256)

                pe.wait_ge(S("hidc"), 1)
                pe.wait_ge(S("small"), 16 * 11)

                spans = ((0, 128), (128, 256))

                def scores(bank, q, key):
                    for m, (c0, w) in enumerate(spans):
                        mm(ps[:, bank, c0:c0 + w], q[:, m * P:(m + 1) * P], key[:, 0:w], True, False)
                        ins = mm(ps[:, bank, c0 + w - P:c0 + w], ident, causal, False, True)
                    return ins

                def turn_probs(bank, p):
                    turn(ps[:, bank, 0:128], p[:, 0:128])
                    turn(ps[:, bank, 128:256], p[:, 128:256])
                    return turn(ps[:, bank, 256:384], p[:, 256:384])

                for t in range(DH + 2):
                    if t < DH:
                        if t >= 2:
                            pe.wait_ge(S("dexp"), t - 1)
                        if t == 0:
                            pe.wait_ge(S("kT2"), 4)
                        for j in range(2):
                            ins = scores(2 * (t % 2) + j, dqkT[64 * j:64 * j + 64, t, :], dqkT[64 * j:64 * j + 64, 4 + t, :])
                        ins.then_inc(S("dscores"), 1)
                    if 1 <= t <= DH:
                        h = t - 1
                        pe.wait_ge(S("dprobs"), h + 1)
                        if h >= 2:
                            pe.wait_ge(S("dpT"), h - 1)
                        turn_probs(4 + h % 2, p2[h % 2][:, 0, :]).then_inc(S("daT"), 1)
                    if t >= 2:
                        h = t - 2
                        pe.wait_ge(S("dpT"), h + 1)
                        if h >= 2:
                            pe.wait_ge(S("od"), h - 1)
                        pt = pt2[h % 2][:, 0, :]
                        o = ps[:, 6 + h % 2, :]
                        mm(o[:, 0:128], pt[:, 0:128], dv[:, 0, h * P:(h + 1) * P], True, True)
                        mm(o[:, 128:256], pt[:, 128:256], dv[:, 0, h * P:(h + 1) * P], True, False)
                        mm(o[:, 128:256], pt[:, 256:384], dv[:, 1, h * P:(h + 1) * P], False, True)\
                            .then_inc(S("dpv"), 1)
                for c in range(2):
                    mm(ps[:, UP, 0:30], w2k[:, c, :, :].rearrange("p u d -> p (u d)"), hidc[:, 0, c, :], c == 0, c == 1)
                for c in range(2):
                    ins = mm(ps[:, UP + 1, 0:64], hidrep[:, c].rearrange("p h n -> p (h n)"), w2v[:, c, :], c == 0, c == 1)
                ins.then_inc(S("cmp_kv"), 1)
                pe.wait_ge(S("o_normed"), 1)
                for h in range(DH):
                    for m in range(M):
                        ins = turn(turned(ACC, h, 1)[:, 0, m * P:(m + 1) * P], od[:, 2 * h + m, :])
                    if h % 2:
                        ins.then_inc(S("turned"), 1)
                pe.wait_ge(S("kcT"), 1)
                pe.wait_ge(S("od"), 4)
                for h in range(NH):
                    r, g = 64 * (h % 2), h // 4
                    for m in range(M):
                        c = (h // 2) * 32 + m * 16
                        ins = mm(ps[:, UP + 2 + h % 2, c:c + 15], nqT[r:r + 64, h // 2, m * P:(m + 1) * P],
                                 kcT[r:r + 64, 15 * g:15 * g + 15], True, True)
                ins.then_inc(S("cscores"), 1)
                pe.wait_ge(S("pcm"), 1)
                for m in range(M):
                    ins = turn(ps[:, UP, m * P:(m + 1) * P], pcm[:, m].rearrange("p h n -> p (h n)"))
                ins.then_inc(S("pcm_turned"), 1)
                need_lows(lows[0] + 2)
                for t in range(NH + 2):
                    if t < NH:
                        if t >= 2:
                            pe.wait_ge(S("nexp"), t - 1)
                        r = 64 * (t % 2)
                        for j in range(2):
                            ins = scores(2 * (t % 2) + j, nqT[r:r + 64, t // 2, :], kT2[r:r + 64, 1 + j, t // 4, :])
                        ins.then_inc(S("nscores"), 1)
                    if 1 <= t <= NH:
                        h = t - 1
                        pe.wait_ge(S("nprobs"), h + 1)
                        if h == 0:
                            pe.wait_ge(S("pcT"), 1)
                        if h >= 1:
                            pe.wait_ge(S("npT"), h)
                        for j in range(2):
                            ins = turn_probs(4 + j, p2[h % 2][:, j, :])
                        ins.then_inc(S("naT"), 1)
                    if t >= 2:
                        h = t - 2
                        pe.wait_ge(S("npT"), h + 1)
                        if h % 2 == 0 and h >= 4:
                            need_lows(lows[0] + 2 + h // 2 - 1)
                        r, g = 64 * (h % 2), h // 4
                        o = ps[r:r + 64, 6 + (h // 2) % 2, :]
                        mm(o[:, 0:T], vsel[:, h, :], pcT, True, False)
                        for j in range(2):
                            pt = pt2[h % 2][:, j, :]
                            mm(o[:, 0:T], vsw[:, 0, j, 64 * g:64 * g + 64], pt[:, 0:256], False, False)
                            ins = mm(o[:, P:T], vsw[:, 1, j, 64 * g:64 * g + 64], pt[:, 256:384], False, j == 1)
                        ins.then_inc(S("npv"), 1)
                lows[0] += 6
                need_lows(lows[0])
                for j in range(4):
                    tall(FIRST["w_out_2"] + j, ACC, act_hl, 2 * j, j == 0, j == 3, 2, 1024)
                turn_normed()

                f0 = FIRST["ffn"]

                def gate_up(n, i, per):
                    for h in range(2):
                        wide(n + h, UP, 4 * h, act_hl, h == 0, h == 1, 4, 512, i, per)

                for h in range(2):
                    need_lows(lows[0] + 2 * h + 2)
                    wide(f0 + h, UP, 4 * h, act_hl, h == 0, h == 1, 4, 512)
                pe.wait_ge(S("ff_sum"), 2)
                gate_up(f0 + 2, 0, 0)
                pe.wait_ge(S("ff_lo"), 1)
                tall(f0 + 4, ACC, hl2, 0, True, False, 2, 1024)
                with pe.Fori(1, FF_BLOCKS - 1) as i:
                    pe.wait_ge(S("ff_sum"), 2 * i + 2)
                    gate_up(f0 + 2, i, 3)
                    pe.wait_ge(S("ff_lo"), i + 1)
                    tall(f0 + 4, ACC, hl2, 0, False, False, 2, 1024, i, 3)
                pe.wait_ge(S("ff_lo"), FF_BLOCKS)
                tall(N_PIECES - 1, ACC, hl2, 0, False, True, 2, 1024)


def kernel(**inputs):
    import numpy as _np
    import concourse.bacc as _bacc
    from concourse import mybir as _mybir
    from concourse.bass_utils import run_bass_kernel_spmd as _run

    nc = _bacc.Bacc("TRN2", target_bir_lowering=False, num_devices=1)
    arrays = {name: _np.ascontiguousarray(v) for name, v in inputs.items()}
    arrays["shape_constants"] = shape_constants()
    aps = {name: nc.dram_tensor(f"in_{name}", v.shape, _mybir.dt.from_np(v.dtype), kind="ExternalInput").ap()
           for name, v in arrays.items()}
    result = nc.dram_tensor("result", (1, T, D), _mybir.dt.float32, kind="ExternalOutput").ap()
    two_blocks(nc, aps, result)
    r = _run(nc, [{f"in_{name}": v for name, v in arrays.items()}], core_ids=[0])
    return r.results[0]["result"]
```

```python
from contextlib import ExitStack

import numpy as np

import concourse.bass as bass
from concourse import mybir

F32 = mybir.dt.float32
F32R = mybir.dt.float32r
I32 = mybir.dt.int32
ALU = mybir.AluOpType
ACT = mybir.ActivationFunctionType
AX = mybir.AxisListType.X
ds = bass.ds

P = 128
T = 256
M = T // P
D = 1024
KD = D // P
EPS = 1e-6
NEG = -1e30

SCW = 512
QR, KVR, ROPE = 384, 256, 32
NOPE, VD, NH = 64, 64, 8
QKD = NOPE + ROPE
A_COLS = QR + KVR + ROPE
MLP_BLOCKS = 4096 // 512
TAPS = 31
CONV_PAD = TAPS // 2
POOL_TILE = 0
DVE_TILES = (1, 2, 3, 4)
SHARED_TAPS = 10
PE_TAPS = [(4, t) for t in range(SHARED_TAPS)] + [(c, t) for c in (5, 6, 7) for t in range(31)]
DIAGS = 6

HD = 64
DH = 4
LAM_INIT = 0.8 - 0.6 * float(np.exp(-0.3 * 0))
N_CMP = (T - 32) // 16 + 1
FF = 2816
FF_BLOCKS = FF // 256

PIECE = 2048
RING = 4
FF_RING = 3

C_ID, C_CAUSAL = 0, 128
C_COS, C_SIN = 256, 384
C_CNEG, C_CONE = 512, 544
C_BLK, C_FREQ = 576, 584
C_END = 600

TWO_PI = (6.28125, 0.0019350051879882812, 2 * float(np.pi) - 6.28125 - 0.0019350051879882812)
ROUND = 1.5 * 2.0 ** 23


def shape_constants():
    c = np.zeros((P, C_END), np.float32)
    c[:, C_ID:C_ID + P] = np.eye(P)
    q = np.arange(P)
    c[:, C_CAUSAL:C_CAUSAL + P] = np.where(q[None, :] <= q[:, None], 0.0, NEG)
    inv = (1.0 / (np.float32(10000.0) ** (np.arange(0, HD, 2, dtype=np.float32) / np.float32(HD)))).astype(np.float32)
    for m in range(M):
        tok = np.arange(m * P, (m + 1) * P)
        ang = tok.astype(np.float32)[:, None] * inv[None, :]
        cos, sin = np.cos(ang), np.sin(ang)
        c[:, C_COS + 64 * m:C_COS + 64 * m + 64] = np.concatenate([cos, cos], 1)
        c[:, C_SIN + 64 * m:C_SIN + 64 * m + 64] = np.concatenate([-sin, sin], 1)
        seen = (np.arange(16) * 16 + 31)[None, :] <= tok[:, None]
        c[:, C_CNEG + 16 * m:C_CNEG + 16 * m + 16] = np.where(seen, 0.0, NEG)
        c[:, C_CONE + 16 * m:C_CONE + 16 * m + 16] = seen
    c[:, C_BLK:C_BLK + 8] = (q[:, None] // 16 == np.arange(8)[None, :])
    c[:, C_FREQ:C_FREQ + 16] = 1.0 / (np.float32(10000.0) ** (np.arange(16, dtype=np.float32) / np.float32(16)))
    return c


STAGES = [("w_in_wide", 6), ("w_in_tall", 3), ("w_uq", 2), ("w_ukv", 1), ("w_out", 4),
          ("mlp0", 4 * MLP_BLOCKS), ("pw1", 8), ("pw2", 4), ("mlp1", 4 * MLP_BLOCKS),
          ("w_in_2", 12), ("cmp", 4), ("w_out_2", 4), ("ffn", 3 * FF_BLOCKS)]
FIRST = {}
_n = 0
for _name, _count in STAGES:
    FIRST[_name] = _n
    _n += _count
N_PIECES = _n
assert FIRST["ffn"] % RING == 0


class Steps:

    def __init__(self, eng, sem):
        self.eng, self.sem, self.count, self.turn, self.per = eng, sem, 0, None, 0

    def link(self, ins):
        self.count += 1
        ins.then_inc(self.sem, 1)
        self.eng.wait_ge(self.sem, self.count if self.turn is None else self.turn * self.per + self.count)

    def enter(self, turn, per):
        self.turn, self.per, self.at = turn, per, self.count

    def leave(self, turns):
        assert self.count - self.at == self.per, (self.count - self.at, self.per)
        self.count = self.at + turns * self.per
        self.turn = None


def two_blocks(nc, a, out):
    with ExitStack() as ctx:
        def sb(name, shape, dt=F32):
            return ctx.enter_context(nc.sbuf_tensor(name, shape, dt))

        sems = {}

        def S(name):
            if name not in sems:
                sems[name] = ctx.enter_context(nc.semaphore(name))
            return sems[name]

        raw = [sb(f"raw{i}", [P, PIECE]) for i in range(RING)]
        w_hi = [sb(f"w_hi{i}", [P, PIECE], F32R) for i in range(RING)]
        w_lo = [sb(f"w_lo{i}", [P, PIECE], F32R) for i in range(RING)]
        x = sb("x_res", [P, M, D])
        act_hl = sb("act_hl", [P, KD, 2 * T], F32R)
        hl2 = sb("hl2", [P, 5, 2 * T], F32R)
        nrm = sb("nrm", [P, M, D])
        gain = [sb(f"gain{i}", [P, D]) for i in range(4)]
        cst = sb("cst", [P, C_END])
        col = sb("col", [P, 3, P])
        bc = sb("bc", [P, 1024])
        ones = sb("ones", [1, P])
        st = sb("st", [P, 192])
        arena = sb("arena", [P, 10752])
        brow = arena[0:1, 9712:9712 + D]

        ident = cst[:, C_ID:C_ID + P]
        causal = cst[:, C_CAUSAL:C_CAUSAL + P]

        def AR(at, *dims, p=P, p0=0):
            n = int(np.prod(dims))
            v = arena[p0:p0 + p, at:at + n]
            if len(dims) == 2:
                return v.rearrange("p (a b) -> p a b", a=dims[0])
            if len(dims) == 3:
                return v.rearrange("p (a b c) -> p a b c", a=dims[0], b=dims[1])
            if len(dims) == 4:
                return v.rearrange("p (a b c d) -> p a b c d", a=dims[0], b=dims[1], c=dims[2])
            return v

        hb = AR(0, 4, T)
        htmp = AR(1024, 4, T)
        gsum, usum = AR(2048, 2, T), AR(2560, 2, T)
        esum = AR(3072, 2, T)
        gate_b, gate_c = AR(0, 4, T), AR(1024, 4, T)
        cx = AR(2048, 4, T + 2)
        ctmp = AR(3080, 4, T)
        qT, kT1 = AR(0, NH, T), AR(2048, NH, T)
        lat = AR(4104, M, QR + KVR)
        prob = [AR(4104 + 512 * i, M, T) for i in range(2)]
        probT = [AR(5128 + 512 * i, M, T) for i in range(2)]
        qf, kf = AR(6152, M, NH, QKD), AR(7688, M, NH, QKD)
        v1 = AR(9224, M, NH, VD)
        rows = AR(9224, 3, P)
        rt = AR(10248, NH, ROPE)
        rt2 = AR(10504, M, ROPE)
        UW = T + 2 * CONV_PAD
        upad = AR(0, 8, UW)
        cv = AR(2288, 8, T)
        ag = AR(4336, 4, T)
        ptmp = AR(5360, 4, T)
        diag = AR(6384, DIAGS, P)
        tap = AR(8944, T)
        zb = AR(0, 8, T)
        eb = AR(7152, 8, T)
        eg = AR(9200, 2, T)
        tok2 = AR(0, 2048)
        nqt = AR(2048, M, 8 * HD)
        p2 = [AR(768 * i, 2, 384) for i in range(2)]
        pt2 = [AR(1536 + 768 * i, 2, 384) for i in range(2)]
        dqkT = AR(3072, 8, T)
        nqT = AR(5120, 4, T)
        kT2 = AR(6144, 4, 2, T)
        dv = AR(8192, M, 512)
        vsw = AR(9216, M, 2, 128)
        od = AR(9728, 8, P)
        t1, t2 = nrm[:, 0, :], nrm[:, 1, :]
        flat = nrm[:, 0, 0:960].rearrange("p (a j n) -> p a j n", a=2, j=16)
        vsel = nrm[:, 1, 0:512].rearrange("p (h d) -> p h d", h=8)
        pcT = nrm[:, 1, 512:768]
        pcm = nrm[:, 1, 768:1024].rearrange("p (m h n) -> p m h n", m=2, h=8)
        pc = nrm[:, 0, 0:256].rearrange("p (a h m n) -> p a h m n", a=2, h=4, m=2)
        hidrep = nrm[:, 0, 256:512].rearrange("p (c h n) -> p c h n", c=2, h=8)
        hidc = nrm[:, 0, 512:632].rearrange("p (a c n) -> p a c n", a=2, c=2)
        hctmp = nrm[:, 0, 640:760].rearrange("p (a c n) -> p a c n", a=2, c=2)
        hce = nrm[:, 0, 768:888].rearrange("p (a c n) -> p a c n", a=2, c=2)
        kcT = nrm[:, 0, 896:926]
        w2k = sb("w2k", [P, 2, 2, HD])
        w2v = sb("w2v", [P, 2, HD])
        gates = sb("gates", [P, M, 24])
        cs1 = sb("cs1", [P, 2, M, ROPE])
        posi = sb("posi", [P, M], I32)
        lamn = sb("lamn", [P, 1])

        ssh = st[:, 144:148]
        ssx = st[:, 148:150]
        rs_post, rs_pre = st[:, 150:152], st[:, 152:154]
        junk = AR(0, M, D)
        ss = st[:, 0:2]
        rstd = st[:, 2:4]
        mhalf = st[:, 4:12]
        ss4, rs4 = st[:, 12:16], st[:, 16:20]
        mv = st[:, 20:24].rearrange("p (m c) -> p m c", m=2)
        bns = st[:, 24:48].rearrange("p (m h c) -> p m h c", m=2, h=2)
        ss8, rs8 = st[:, 48:56], st[:, 56:64]
        mx = [st[:, 64 + 4 * i:68 + 4 * i] for i in range(2)]
        nmx = [st[:, 72 + 4 * i:76 + 4 * i] for i in range(2)]
        rsum = [st[:, 80 + 4 * i:84 + 4 * i] for i in range(2)]
        rinv = [st[:, 88 + 4 * i:92 + 4 * i] for i in range(2)]
        cf = [st[:, 96 + 4 * i:100 + 4 * i] for i in range(2)]
        pf = st[:, 104:106]
        lam4 = st[:, 106:110]
        cmx = st[:, 112:128]
        crs = st[:, 128:144]

        VC = {}
        r = 0
        for name, n in (("b_pw1", 16), ("b_dw", 8), ("ln_g", 8), ("ln_b", 8), ("sc", 12), ("kpos", 16), ("vpos", 16)):
            VC[name] = r
            r += n
        VROWS = r
        DROWS = 4 * TAPS

        def vcol(name, i, n=1):
            return col[:, 0, VC[name] + i:VC[name] + i + n]

        def dwcol(t, c):
            r = t * 8 + c
            return col[:, 1 + r // DROWS, r % DROWS:r % DROWS + 1]

        ps = ctx.enter_context(nc.psum_tensor("ps", [P, 8, 512], F32))
        ACC, UP = 0, 4
        TURN_BANK = (ACC, ACC, ACC, ACC, UP, ACC)

        def tall_out(bank, m, width=1024):
            return ps[:, bank + 2 * m:bank + 2 * m + 2, :].rearrange("p b n -> p (b n)")[:, 0:width]

        def turned(bank, k0, n):
            v = ps[:, bank:bank + 4, :].rearrange("p b (h t) -> p (b h) t", h=2)
            return v[:, k0:k0 + n, :]

        def turned_tile(bank, m, j):
            return ps[:, bank + 2 * m + j, :].rearrange("p (k t) -> p k t", k=4)

        def view_k(w):
            return w.rearrange("(k p) n -> p k n", p=P)

        w_in = view_k(a["even_w_in"][0])
        w_uq, w_ukv = view_k(a["even_w_uq"][0]), view_k(a["even_w_ukv"][0])
        w_out = view_k(a["even_w_out"][0])
        pw1 = a["odd_w_pw1"][0].rearrange("(k p) (h n) -> p k h n", p=P, h=2)
        pw2 = view_k(a["odd_w_pw2"][0])
        mlp1 = [view_k(a["mlp_w1"][i]) for i in range(2)]
        mlp2 = [view_k(a["mlp_w2"][i]) for i in range(2)]
        w_in_2, w_out_2 = view_k(a["w_in_2"][0]), view_k(a["w_out_2"][0])
        cmp1 = [view_k(a["k_cmp_w1_2"][0]), view_k(a["v_cmp_w1_2"][0])]
        w_gate, w_up, w_down = view_k(a["w_gate_2"][0]), view_k(a["w_up_2"][0]), view_k(a["w_down_2"][0])

        piece = {}
        for b in range(3):
            for h in range(2):
                piece[FIRST["w_in_wide"] + 2 * b + h] = (4, 512, [w_in[:, 4 * h:4 * h + 4, 512 * b:512 * b + 512]])
        TALL_K = [(0, 3), (3, 3), (6, 2)]
        for j, (k, n) in enumerate(TALL_K):
            piece[FIRST["w_in_tall"] + j] = (n, A_COLS, [w_in[:, k:k + n, 3 * SCW:3 * SCW + A_COLS]])
        UQ_K = [(0, 2), (2, 1)]
        for j, (k, n) in enumerate(UQ_K):
            piece[FIRST["w_uq"] + j] = (n, NH * QKD, [w_uq[:, k:k + n, :]])
        piece[FIRST["w_ukv"]] = (2, 1024, [w_ukv])
        for name, w in (("w_out", w_out), ("pw2", pw2), ("w_out_2", w_out_2)):
            for j in range(4):
                piece[FIRST[name] + j] = (2, 1024, [w[:, 2 * j:2 * j + 2, :]])
        for b in range(4):
            for h in range(2):
                piece[FIRST["pw1"] + 2 * b + h] = (4, 512, [
                    pw1[:, 4 * h:4 * h + 4, g, 256 * b:256 * b + 256] for g in range(2)])
        W2C = [(0, 1024), (1024, 1024), (2048, 792)]
        for c, (n0, n) in enumerate(W2C):
            for j in range(4):
                piece[FIRST["w_in_2"] + 4 * c + j] = (2, n, [w_in_2[:, 2 * j:2 * j + 2, n0:n0 + n]])
        for a_ in range(2):
            for h in range(2):
                piece[FIRST["cmp"] + 2 * a_ + h] = (8, 256, [cmp1[a_][:, 8 * h:8 * h + 8, :]])

        def in_loop(n):
            return n not in piece

        def slot_of(n):
            return n % RING if n < FIRST["ffn"] else (n - FIRST["ffn"]) % FF_RING

        def back(n):
            return RING if n < FIRST["ffn"] + FF_RING else FF_RING

        def width_of(n):
            return piece[n][0] * piece[n][1] if n in piece else PIECE

        def parts_of(n):
            if n in piece:
                return len(piece[n][2])
            if n < FIRST["ffn"]:
                return 1
            q = n - FIRST["ffn"]
            return 2 if q < 2 or (q < 2 + 3 * (FF_BLOCKS - 1) and (q - 2) % 3 < 2) else 1

        def landed_at(n):
            return 16 * sum(parts_of(q) for q in range(n + 1) if slot_of(q) == slot_of(n))

        def pv(tile, n):
            k, w = piece[n][0:2]
            return tile[slot_of(n)][:, 0:k * w].rearrange("p (k n) -> p k n", k=k)

        with nc.Block() as block:
            @block.sync
            def _(sp):
                def load(n):
                    k, w, srcs = piece[n]
                    if n >= back(n):
                        sp.wait_ge(S("w_split"), n - back(n) + 1)
                    dst = pv(raw, n)
                    for i, src in enumerate(srcs):
                        part = w // len(srcs)
                        sp.dma_start(dst[:, :, i * part:(i + 1) * part], src).then_inc(S(f"landed{slot_of(n)}"), 16)

                def load_gain(s, src):
                    if s >= 4:
                        sp.wait_ge(S("gain_used"), s - 3)
                    sp.dma_start(gain[s % 4][:, :], src.partition_broadcast(P)).then_inc(S(f"gain{s % 4}"), 16)

                gains = [a["sandwich_gains"][i, j, :] for i in range(2) for j in range(4)] + [
                    a["attn_pre_norm_2"][0, :], a["attn_post_norm_2"][0, :],
                    a["ffn_pre_norm_2"][0, :], a["ffn_post_norm_2"][0, :]]

                for m in range(M):
                    sp.dma_start(x[:, m, :], a["x"][0, m * P:(m + 1) * P, :]).then_inc(S(f"x_in{m}"), 16)
                for n in range(4):
                    load(n)

                def small(dst, src, sem="small"):
                    sp.dma_start(dst, src).then_inc(S(sem), 16)

                for name, src in (("b_pw1", a["odd_b_pw1"][0]), ("b_dw", a["odd_b_dw"][0]), ("ln_g", a["odd_ln_g"][0]),
                                  ("ln_b", a["odd_ln_b"][0])):
                    n = src.shape[0] // P
                    small(rows[VC[name]:VC[name] + n, 0, :], src.rearrange("(k p) -> k p", p=P), "rows_in")
                small(rows[VC["sc"]:VC["sc"] + 12, 0, :], a["even_sc_kernel"][0].rearrange("t (c p) -> (t c) p", p=P),
                      "rows_in")
                for name, src in (("kpos", a["k_cmp_pos_2"][0]), ("vpos", a["v_cmp_pos_2"][0])):
                    small(rows[VC[name]:VC[name] + 16, 0, :], src.rearrange("(j q) d -> j (q d)", q=2), "rows_in")
                dw = a["odd_w_dw"][0].rearrange("t (c p) -> (t c) p", p=P)
                for i in range(2):
                    small(rows[0:DROWS, 1 + i, :], dw[DROWS * i:DROWS * (i + 1), :], "rows_in")
                sp.dma_start(posi[:, :], a["positions"][0].rearrange("(m p) -> p m", p=P),
                              allow_slow_non_contiguous=True).then_inc(S("small"), 16)
                at = 0
                for src in (a["even_q_norm"][0], a["even_kv_norm"][0], a["diff_subln_2"][0], a["lambda_q1_2"][0],
                            a["lambda_k1_2"][0], a["lambda_q2_2"][0], a["lambda_k2_2"][0]):
                    n = src.shape[0]
                    small(bc[:, at:at + n], src.partition_broadcast(P))
                    at += n
                for u in range(2):
                    small(w2k[:, :, u, :], view_k(a["k_cmp_w2_2"][0]))
                small(w2v[:, :, :], view_k(a["v_cmp_w2_2"][0]))
                for s in range(1, 4):
                    load_gain(s, gains[s])
                for n in range(4, FIRST["mlp0"]):
                    load(n)
                load_gain(4, gains[4])

                def load_in_loop(n, i, per, src, cols=None):
                    slot = n % RING if per == 4 else (n - FIRST["ffn"]) % FF_RING
                    sp.wait_ge(S("w_split"), i * per + (n - (RING if per == 4 else FF_RING) + 1))
                    dst = raw[slot][:, :].rearrange("p (k n) -> p k n", k=src.shape[1])
                    if cols is not None:
                        dst = dst[:, :, cols[0]:cols[1]]
                    sp.dma_start(dst, src).then_inc(S(f"landed{slot}"), 16)

                def load_mlp(layer, n0):
                    def up(n, i, turn):
                        for h in range(2):
                            load_in_loop(n + h, turn, 4, mlp1[layer][:, 4 * h:4 * h + 4, ds(i * 512, 512)])

                    def down(n, i, turn):
                        for h in range(2):
                            load_in_loop(n + h, turn, 4, mlp2[layer][:, ds(i * 4 + 2 * h, 2), :])

                    up(n0, 0, 0)
                    with sp.Fori(1, MLP_BLOCKS) as i:
                        up(n0 + 2 - 4, i, i)
                        down(n0 + 4 - 4, i - 1, i)
                    down(n0 + 4 * MLP_BLOCKS - 2, MLP_BLOCKS - 1, 0)

                load_mlp(0, FIRST["mlp0"])
                sp.dma_start(brow, a["odd_b_pw2"]).then_inc(S("b_pw2"), 16)
                load_gain(5, gains[5])
                load_gain(6, gains[6])
                for n in range(FIRST["pw1"], FIRST["mlp1"]):
                    load(n)
                load_gain(7, gains[7])
                load_gain(8, gains[8])
                load_mlp(1, FIRST["mlp1"])
                load_gain(9, gains[9])
                load_gain(10, gains[10])
                for n in range(FIRST["w_in_2"], FIRST["ffn"]):
                    load(n)
                load_gain(11, gains[11])

                f0 = FIRST["ffn"]

                def gate_up(n, i, turn):
                    for h in range(2):
                        for g, w in enumerate((w_gate, w_up)):
                            load_in_loop(n + h, turn, 3, w[:, 4 * h:4 * h + 4, ds(i * 256, 256)], (256 * g, 256 * g + 256))

                gate_up(f0, 0, 0)
                with sp.Fori(1, FF_BLOCKS) as i:
                    gate_up(f0 - 1, i, i)
                    load_in_loop(f0 + 1, i, 3, w_down[:, ds((i - 1) * 2, 2), :])
                n = N_PIECES - 1
                sp.wait_ge(S("w_split"), n - FF_RING + 1)
                sp.dma_start(raw[slot_of(n)][:, :].rearrange("p (k n) -> p k n", k=2),
                             w_down[:, 2 * FF_BLOCKS - 2:2 * FF_BLOCKS, :]).then_inc(S(f"landed{slot_of(n)}"), 16)
                for m in range(M):
                    sp.wait_ge(S("x_new"), 2 * 5 + m + 1)
                    sp.dma_start(out[0, m * P:(m + 1) * P, :], x[:, m, :]).then_inc(S("stored"), 16)
                sp.wait_ge(S("stored"), 16 * M)

            @block.gpsimd
            def _(gp):
                me = Steps(gp, S("pool_step"))
                cursor = [0]

                def hi(n):
                    gp.wait_ge(S(f"landed{slot_of(n)}"), landed_at(n))
                    if n >= back(n):
                        gp.wait_ge(S("pe_piece"), n - back(n) + 1)
                    w = width_of(n)
                    gp.tensor_scalar(w_hi[slot_of(n)][:, 0:w], raw[slot_of(n)][:, 0:w], 1.0, 0.0,
                                     ALU.mult, ALU.add).then_inc(S("w_hi"), 1)

                def hi_until(n):
                    while cursor[0] <= min(n, N_PIECES - 1):
                        hi(cursor[0])
                        cursor[0] += 1

                def hi_in_loop(n, turn, per):
                    each = landed_at(n + per) - landed_at(n)
                    gp.wait_ge(S(f"landed{slot_of(n)}"), turn * each + landed_at(n))
                    gp.wait_ge(S("pe_piece"), turn * per + (n - back(n) + 1))
                    gp.sem_inc(S("pool_turn"), 1)
                    gp.tensor_scalar(w_hi[slot_of(n)][:, :], raw[slot_of(n)][:, :], 1.0, 0.0,
                                     ALU.mult, ALU.add).then_inc(S("w_hi"), 1)

                def rsqrt(dst, src, parts, sem):
                    for c0, c1, scale in parts:
                        me.link(gp.tensor_scalar(src[:, c0:c1], src[:, c0:c1], scale, EPS, ALU.mult, ALU.add))
                    n = parts[-1][1]
                    gp.tensor_tensor(dst[:, 0:n], src[:, 0:n], mhalf[:, 0:n], ALU.pow).then_inc(sem, 1)

                me.link(gp.memset(mhalf, -0.5))
                gp.memset(ones[:, :], 1.0).then_inc(S("ones"), 1)
                squares = [0]

                def post_rsqrt(m):
                    squares[0] += 2
                    gp.wait_ge(S("ssq"), squares[0])
                    h = ssh[:, 2 * m:2 * m + 1]
                    me.link(gp.tensor_scalar(h, h, ssh[:, 2 * m + 1:2 * m + 2], EPS, ALU.add, ALU.add))
                    gp.tensor_tensor(rs_post[:, m:m + 1], h, mhalf[:, 0:1], ALU.pow).then_inc(S("rstd"), 1)

                def pre_rsqrt(m):
                    squares[0] += 1
                    gp.wait_ge(S("ssq"), squares[0])
                    h = ssx[:, m:m + 1]
                    me.link(gp.tensor_scalar(h, h, EPS, None, ALU.add))
                    gp.tensor_tensor(rs_pre[:, m:m + 1], h, mhalf[:, 0:1], ALU.pow).then_inc(S("rstd"), 1)

                def boundary(last):
                    hi_until(last + 2)
                    post_rsqrt(0)
                    pre_rsqrt(0)
                    post_rsqrt(1)
                    hi_until(last + 3)
                    pre_rsqrt(1)
                    hi_until(min(last + 4, FIRST["ffn"] + 2))

                pre_rsqrt(0)
                pre_rsqrt(1)
                hi_until(FIRST["w_uq"] + 3)
                gp.wait_ge(S("lat_ssq"), 4)
                rsqrt(rs4, ss4, [(0, 2, 1.0 / QR), (2, 4, 1.0 / KVR)], S("lat_rstd"))

                def mlp(n0):
                    hi_until(n0 + 3)
                    with gp.Fori(0, MLP_BLOCKS - 1) as i:
                        for j in range(4):
                            hi_in_loop(n0 + 4 + j, i, 4)
                    cursor[0] = n0 + 4 * MLP_BLOCKS
                    boundary(n0 + 4 * MLP_BLOCKS - 1)

                boundary(FIRST["mlp0"] - 1)
                mlp(FIRST["mlp0"])
                taps = [0]

                def convolve(n):
                    for t in range(taps[0], min(taps[0] + n, TAPS)):
                        src, w = upad[:, POOL_TILE, t:t + T], dwcol(t, POOL_TILE)
                        if t == 0:
                            gp.wait_ge(S("u"), POOL_TILE // 2 + 1)
                            me.link(gp.tensor_scalar(cv[:, POOL_TILE, :], src, w, vcol("b_dw", POOL_TILE),
                                                     ALU.mult, ALU.add))
                        else:
                            me.link(gp.tensor_scalar(tap, src, w, None, ALU.mult))
                            me.link(gp.tensor_tensor(cv[:, POOL_TILE, :], cv[:, POOL_TILE, :], tap, ALU.add))
                    taps[0] = min(taps[0] + n, TAPS)

                hi_until(FIRST["pw1"] + 6)
                for n in range(FIRST["pw1"] + 7, FIRST["pw2"] + 4):
                    convolve(2)
                    hi_until(n)
                convolve(TAPS)
                gp.sem_inc(S("conv_pool"), 1)
                for m in range(M):
                    gp.wait_ge(S("ln_stats"), m + 1)
                    me.link(gp.tensor_scalar(ss[:, m:m + 1], mv[:, m, 1:2], EPS, None, ALU.add))
                    gp.tensor_tensor(rstd[:, m:m + 1], ss[:, m:m + 1], mhalf[:, 0:1], ALU.pow)\
                        .then_inc(S("ln_rstd"), 1)
                boundary(FIRST["mlp1"] - 1)
                mlp(FIRST["mlp1"])
                hi_until(FIRST["w_out_2"] + 3)
                gp.wait_ge(S("diff_ssq"), 1)
                rsqrt(rs8, ss8, [(0, 8, 1.0 / P)], S("diff_rstd"))
                f0 = FIRST["ffn"]
                boundary(f0 - 1)
                with gp.Fori(0, FF_BLOCKS - 2) as i:
                    for j in range(3):
                        q = f0 + 3 + j
                        base = landed_at(q)
                        each = 32 if (q - f0 - 2) % 3 < 2 else 16
                        gp.wait_ge(S(f"landed{slot_of(q)}"), i * each + base)
                        gp.wait_ge(S("pe_piece"), i * 3 + (q - FF_RING + 1))
                        gp.sem_inc(S("pool_turn"), 1)
                        gp.tensor_scalar(w_hi[slot_of(q)][:, :], raw[slot_of(q)][:, :], 1.0, 0.0,
                                         ALU.mult, ALU.add).then_inc(S("w_hi"), 1)
                cursor[0] = f0 + 3 * (FF_BLOCKS - 1)
                hi_until(N_PIECES)
                post_rsqrt(0)
                post_rsqrt(1)

            @block.vector
            def _(dve):
                me = Steps(dve, S("dve_step"))
                link = me.link
                tt, stt, tsc = dve.tensor_tensor, dve.scalar_tensor_tensor, dve.tensor_scalar
                cursor = [0]

                def lo(n, turn=0, per=0):
                    w = width_of(n)
                    dve.wait_ge(S("w_hi"), turn * per + n + 1)
                    tt(w_lo[slot_of(n)][:, 0:w], raw[slot_of(n)][:, 0:w],
                       w_hi[slot_of(n)][:, 0:w].bitcast(F32), ALU.subtract).then_inc(S("w_split"), 1)

                def lo_until(n):
                    while cursor[0] <= min(n, N_PIECES - 1):
                        lo(cursor[0])
                        cursor[0] += 1

                def piece_done(n, turn=0, per=0):
                    dve.wait_ge(S("pe_piece"), turn * per + n + 1)

                def act_lo(src, k0, n, count, scale=1.0):
                    dve.wait_ge(S("act_hi"), count)
                    dst, high = act_hl[:, k0:k0 + n, T:2 * T], act_hl[:, k0:k0 + n, 0:T].bitcast(F32)
                    if scale == 1.0:
                        tt(dst, src, high, ALU.subtract).then_inc(S("act_lo"), 1)
                    else:
                        stt(dst, src, scale, high, ALU.mult, ALU.subtract).then_inc(S("act_lo"), 1)

                norms, rsts, outs, ssqs = [0], [0], [0], [0]
                his = [0]

                def next_rstd():
                    rsts[0] += 1
                    dve.wait_ge(S("rstd"), rsts[0])

                def post_tile(m, last):
                    g = norms[0]
                    y, gn = tall_out(ACC, m), gain[g % 4][:, :]
                    if m == 0:
                        dve.wait_ge(S("tile_out"), outs[0] + 1)
                        dve.wait_ge(S(f"gain{g % 4}"), 16 * (g // 4 + 1))
                        outs[0] += 1
                    else:
                        piece_done(last)
                    tt(nrm[:, m, 512:D], y[:, 512:D], gn[:, 512:D], ALU.mult).then_inc(S("gained"), 1)
                    dve.wait_ge(S("ssq"), ssqs[0] + 1)
                    ssqs[0] += 3
                    link(tt(nrm[:, m, 0:512], y[:, 0:512], gn[:, 0:512], ALU.mult))
                    next_rstd()
                    stt(x[:, m, :], nrm[:, m, :], rs_post[:, m:m + 1], x[:, m, :], ALU.mult, ALU.add)\
                        .then_inc(S("x_new"), 1)

                def pre_tile(m, g):
                    next_rstd()
                    if m == 0:
                        dve.wait_ge(S(f"gain{g % 4}"), 16 * (g // 4 + 1))
                    stt(nrm[:, m, :], x[:, m, :], rs_pre[:, m:m + 1], gain[g % 4][:, :], ALU.mult, ALU.mult)\
                        .then_inc(S("normed"), 1)

                def low_tile(m, bank):
                    for j in range(2):
                        his[0] += 1
                        dve.wait_ge(S("act_hi"), his[0])
                        k = slice(4 * j, 4 * j + 4)
                        tt(act_hl[:, k, T + m * P:T + (m + 1) * P], turned_tile(bank, m, j),
                           act_hl[:, k, m * P:(m + 1) * P].bitcast(F32), ALU.subtract).then_inc(S("act_lo"), 1)

                def boundary(s, last):
                    lo_until(last + 2)
                    post_tile(0, last)
                    pre_tile(0, norms[0] + 1)
                    post_tile(1, last)
                    low_tile(0, TURN_BANK[s])
                    if s == 4:
                        lo_until(last + 3)
                    pre_tile(1, norms[0] + 1)
                    if s == 4:
                        lo_until(last + 4)
                    low_tile(1, TURN_BANK[s])
                    norms[0] += 2
                    dve.sem_inc(S("gain_used"), 2)

                def rope(dst, src, cos, sin, ta, tb, half):
                    idx = (slice(None),) * (len(dst.shape) - 1)
                    first, second = idx + (slice(0, half),), idx + (slice(half, 2 * half),)
                    link(tt(ta, src, cos, ALU.mult))
                    link(tt(tb[first], src[second], sin[first], ALU.mult))
                    link(tt(tb[second], src[first], sin[second], ALU.mult))
                    return tt(dst, ta, tb, ALU.add)

                pre_tile(0, 0)
                pre_tile(1, 0)
                ssqs[0] = 2
                low_tile(0, ACC)
                lo_until(1)
                low_tile(1, ACC)
                norms[0] = 1
                dve.sem_inc(S("gain_used"), 1)
                dve.wait_ge(S("cols"), 1)
                link(dve.tensor_copy(col[:, 0, 0:VROWS], ps[:, ACC + 3, 0:VROWS]))
                tsc(col[:, 1:3, 0:DROWS], ps[:, ACC + 3, P:3 * P].rearrange("p (i r) -> p i r", i=2)[:, :, 0:DROWS],
                    0.5, None, ALU.mult).then_inc(S("cols_read"), 1)
                dve.wait_ge(S("cols_read"), 1)
                lo_until(3)
                dve.wait_ge(S("small"), 16 * 11)
                posf, ang = rt[:, 0, 0:2], rt[:, 1:2, 0:32].rearrange("p o (m f) -> p (o m) f", m=2)
                link(dve.tensor_copy(posf, posi[:, :]))
                for m in range(M):
                    link(tsc(ang[:, m, :], cst[:, C_FREQ:C_FREQ + 16], posf[:, m:m + 1], None, ALU.mult))
                for i, quarter in enumerate((0.25, 0.0)):
                    turns = rt[:, 2 + i:3 + i, 0:32].rearrange("p o (m f) -> p (o m) f", m=2)
                    red = rt[:, 4 + i:5 + i, 0:32].rearrange("p o (m f) -> p (o m) f", m=2)
                    link(tsc(turns, ang, 1.0 / (2 * float(np.pi)), quarter, ALU.mult, ALU.add))
                    link(tsc(turns, turns, ROUND, -ROUND, ALU.add, ALU.add))
                    link(stt(red, turns, -TWO_PI[0], ang, ALU.mult, ALU.add))
                    link(stt(red, turns, -TWO_PI[1], red, ALU.mult, ALU.add))
                    link(stt(red, turns, -TWO_PI[2], red, ALU.mult, ALU.add))
                    link(tsc(red, red, float(np.pi) / 2 if i == 0 else 0.0, 3.1415925, ALU.add, ALU.min))
                    tsc(red, red, -3.1415925, None, ALU.max).then_inc(S("angles"), 1)
                dve.wait_ge(S("sines"), 2)
                link(dve.tensor_copy(cs1[:, 0, :, 16:32], cs1[:, 0, :, 0:16]))
                link(tsc(cs1[:, 1, :, 0:16], cs1[:, 1, :, 16:32], -1.0, None, ALU.mult))
                link(stt(rt[:, 6:8, :].rearrange("p a b -> p (a b)"), bc[:, 768:832], 1.0, bc[:, 832:896],
                         ALU.mult, ALU.mult, accum_out=lam4[:, 0:1]))
                stt(rt[:, 6:8, :].rearrange("p a b -> p (a b)"), bc[:, 896:960], 1.0, bc[:, 960:1024],
                    ALU.mult, ALU.mult, accum_out=lam4[:, 1:2]).then_inc(S("lam_sums"), 1)
                dve.wait_ge(S("lam_exp"), 1)
                link(tt(lamn[:, :], lam4[:, 3:4], lam4[:, 2:3], ALU.subtract))
                link(tsc(lamn[:, :], lamn[:, :], -LAM_INIT, None, ALU.add))
                link(dve.memset(cx[:, :, 0:1], 0.0))
                link(dve.memset(cx[:, :, T + 1:T + 2], 0.0))

                def halves(bank):
                    return ps[:, bank:bank + 4, 0:T]

                for b, dst in enumerate((gate_b, gate_c, None)):
                    n = FIRST["w_in_wide"] + 2 * b + 1
                    lo_until(n + 3)
                    dve.wait_ge(S("half_copied"), b + 1)
                    bank = (UP, ACC, UP)[b]
                    if b < 2:
                        tt(dst, halves(bank), ctmp, ALU.add).then_inc(S("wide_read"), 1)
                    else:
                        dve.wait_ge(S("wide_read"), 2)
                        link(tt(cx[:, :, 1:T + 1], halves(bank), ctmp, ALU.add))
                        link(tt(cx[:, :, 1:T + 1], cx[:, :, 1:T + 1], gate_c, ALU.mult))
                        dve.sem_inc(S("wide_read"), 1)
                for t in range(3):
                    for c in range(4):
                        w = vcol("sc", 4 * t + c)
                        if t == 0:
                            ins = tsc(gate_c[:, c, :], cx[:, c, 0:T], w, None, ALU.mult)
                        else:
                            ins = stt(gate_c[:, c, :], cx[:, c, t:t + T], w, gate_c[:, c, :], ALU.mult, ALU.add)
                    link(ins)
                tt(gate_b, gate_b, gate_c, ALU.mult).then_inc(S("ya"), 1)
                lo_until(FIRST["w_uq"] - 1 + 3)
                dve.wait_ge(S("lat_rstd"), 1)
                for m in range(M):
                    tall = tall_out(ACC, m)
                    stt(lat[:, m, 0:QR], tall[:, 0:QR], rs4[:, m:m + 1], bc[:, 0:QR], ALU.mult, ALU.mult)
                    stt(lat[:, m, QR:QR + KVR], tall[:, QR:QR + KVR], rs4[:, 2 + m:3 + m],
                        bc[:, QR:QR + KVR], ALU.mult, ALU.mult).then_inc(S("lat_normed"), 1)
                kr = ps[:, ACC:ACC + 4, :].rearrange("p (m b) n -> p m (b n)", m=2)[:, :, QR + KVR:A_COLS]
                link(rope(rt2, kr, cs1[:, 0], cs1[:, 1], rt[:, 0:2, :], rt[:, 2:4, :], ROPE // 2))
                for m in range(M):
                    ins = dve.tensor_copy(kf[:, m, :, NOPE:QKD], rt2[:, m, :].unsqueeze(1).to_broadcast([P, NH, ROPE]))
                ins.then_inc(S("kpe"), 1)
                for i, (k, n) in enumerate(((0, 2), (2, 2), (4, 1))):
                    dve.wait_ge(S("lat_hi"), i + 1)
                    tt(hl2[:, k:k + n, T:2 * T], turned(UP, k, n), hl2[:, k:k + n, 0:T].bitcast(F32),
                       ALU.subtract).then_inc(S("lat_lo"), 1)
                his[0] += 1
                act_lo(gate_b, 0, 4, his[0])
                lo_until(FIRST["w_uq"] + 1 + 3)
                piece_done(FIRST["w_uq"] + 1)
                for m in range(M):
                    src = tall_out(ACC, m, NH * QKD).rearrange("p (h d) -> p h d", h=NH)[:, :, NOPE:QKD]
                    cos, sin = (cs1[:, i, m, :].unsqueeze(1).to_broadcast([P, NH, ROPE]) for i in range(2))
                    ta = AR(4104, NH, ROPE)
                    tb = AR(4360, NH, ROPE)
                    dve.wait_ge(S("q_nope"), m + 1)
                    rope(qf[:, m, :, NOPE:QKD], src, cos, sin, ta, tb, ROPE // 2).then_inc(S("q_rope"), 1)
                    dve.wait_ge(S("q_rope"), m + 1)
                lo_until(FIRST["w_out"] - 1 + 3)
                for j in range(4):
                    dve.wait_ge(S("k_turned"), j + 1)
                    dve.tensor_copy(kT1[0:QKD, 2 * j:2 * j + 2, :],
                                    ps[0:QKD, UP + j, :].rearrange("p (h t) -> p h t", h=2)).then_inc(S("kT"), 1)
                lo_until(FIRST["w_out"] + 3)
                for t in range(NH + 3):
                    if t < NH:
                        b = t % 2
                        dve.wait_ge(S("scores"), t + 1)
                        if t >= 2:
                            dve.wait_ge(S("probs_exp"), t - 1)
                        dve.tensor_reduce(nmx[b][:, 0:2], ps[:, b, :].rearrange("p (m t) -> p m t", m=2), AX, ALU.max,
                                          negate=True).then_inc(S("row_max"), 1)
                    if 1 <= t <= NH:
                        h = t - 1
                        b = h % 2
                        dve.wait_ge(S("probs_exp"), h + 1)
                        link(dve.reciprocal(rinv[b][:, 0:2], rsum[b][:, 0:2]))
                        for m in range(M):
                            tsc(prob[b][:, m, :], prob[b][:, m, :], rinv[b][:, m:m + 1], None, ALU.mult)\
                                .then_inc(S("probs"), 1)
                    if t >= 4 and t % 2 == 0:
                        h = t - 4
                        his[0] += 1
                        act_lo(ps[:, 4 + (h // 2) % 2, 0:T].unsqueeze(1), 4 + h // 2, 1, his[0])
                boundary(1, FIRST["mlp0"] - 1)

                def mlp(n0, s):
                    blocks = MLP_BLOCKS * s

                    def square(i):
                        for j in range(2):
                            dve.wait_ge(S("half_copied"), 3 + 2 * blocks + 2 * i + j + 1)
                            c = slice(2 * j, 2 * j + 2)
                            link(tt(htmp[:, c, :], ps[:, UP + 2 * j:UP + 2 * j + 2, 0:T], htmp[:, c, :], ALU.add))
                            stt(hb[:, c, :], htmp[:, c, :], 0.0, htmp[:, c, :], ALU.max, ALU.mult)\
                                .then_inc(S("hidden"), 1)

                    def hidden_lo(i):
                        for j in range(2):
                            dve.wait_ge(S("hid_hi"), 2 * blocks + 2 * i + j + 1)
                            c = slice(2 * j, 2 * j + 2)
                            tt(hl2[:, c, T:2 * T], hb[:, c, :], hl2[:, c, 0:T].bitcast(F32), ALU.subtract)\
                                .then_inc(S("hid_lo"), 1)

                    lo_until(n0 + 3)
                    square(0)
                    hidden_lo(0)
                    with dve.Fori(0, MLP_BLOCKS - 1) as i:
                        me.enter(i, 2)
                        lo(n0 + 4, i, 4)
                        lo(n0 + 5, i, 4)
                        square(i + 1)
                        lo(n0 + 6, i, 4)
                        lo(n0 + 7, i, 4)
                        hidden_lo(i + 1)
                    me.leave(MLP_BLOCKS - 1)
                    cursor[0] = n0 + 4 * MLP_BLOCKS
                    boundary(2 * s + 2, n0 + 4 * MLP_BLOCKS - 1)

                mlp(FIRST["mlp0"], 0)

                def convolve(c, t):
                    if t == 0:
                        return tsc(cv[:, c, :], upad[:, c, t:t + T], dwcol(t, c), vcol("b_dw", c), ALU.mult, ALU.add)
                    return stt(cv[:, c, :], upad[:, c, t:t + T], dwcol(t, c), cv[:, c, :], ALU.mult, ALU.add)

                early = [0]

                def ahead(n):
                    for t in range(early[0], early[0] + n):
                        link(convolve(DVE_TILES[0], t))
                    early[0] += n

                link(dve.memset(upad[:, :, 0:CONV_PAD], 0.0))
                link(dve.memset(upad[:, :, CONV_PAD + T:UW], 0.0))
                for b in range(4):
                    n = FIRST["pw1"] + 2 * b + 1
                    lo_until(n + 2)
                    if b:
                        ahead(4)
                    if b < 3:
                        lo_until(n + 3)
                    if 0 < b < 3:
                        ahead(3)
                    bank = (UP, ACC)[b % 2]
                    dve.wait_ge(S("pw_half"), b + 1)
                    for c in range(4):
                        bias = vcol("b_pw1", 2 * b + c if c < 2 else 8 + 2 * b + c - 2)
                        stt(ag[:, c, :], ps[:, bank + c, 0:T], bias, ptmp[:, c, :], ALU.add, ALU.add)\
                            .then_inc(S("ag"), 1)
                    dve.wait_ge(S("gate_tanh"), b + 1)
                    stt(upad[:, 2 * b:2 * b + 2, CONV_PAD:CONV_PAD + T], eg, 1.0, ag[:, 0:2, :], ALU.add, ALU.mult)\
                        .then_inc(S("u"), 1)
                    dve.wait_ge(S("u"), b + 1)
                for t in range(TAPS):
                    if early[0] < TAPS:
                        convolve(DVE_TILES[0], early[0])
                        early[0] += 1
                    if t == SHARED_TAPS:
                        dve.wait_ge(S("conv_act"), 1)
                    for c in DVE_TILES[1:] if t >= SHARED_TAPS else DVE_TILES[1:-1]:
                        ins = convolve(c, t)
                    if t < TAPS - 1:
                        link(ins)
                ins.then_inc(S("conv_dve"), 1)
                for m in range(M):
                    dve.wait_ge(S("cv_turned"), m + 1)
                    for h in range(2):
                        ins = dve.bn_stats(bns[:, m, h, :], ps[:, ACC + 2 * m + h, :])
                    link(ins)
                    dve.bn_aggr(mv[:, m, :], bns[:, m, :, :]).then_inc(S("ln_stats"), 1)
                for m in range(M):
                    dve.wait_ge(S("ln_rstd"), m + 1)
                    tsc(nrm[:, m, :], tall_out(ACC, m), mv[:, m, 0:1], rstd[:, m:m + 1], ALU.subtract, ALU.mult)\
                        .then_inc(S("normed"), 1)
                lo_until(FIRST["pw2"] + 3)
                for j in range(5):
                    if j < 4:
                        dve.wait_ge(S("z_tanh"), j + 1)
                        c = slice(2 * j, 2 * j + 2)
                        stt(zb[:, c, :], eb[:, c, :], 1.0, zb[:, c, :], ALU.add, ALU.mult).then_inc(S("silu"), 1)
                    if j:
                        his[0] += 1
                        act_lo(zb[:, 2 * j - 2:2 * j, :], 2 * j - 2, 2, his[0], 0.5)
                boundary(3, FIRST["mlp1"] - 1)
                mlp(FIRST["mlp1"], 1)

                def tab(c, m, *shape):
                    v = cst[:, c + 64 * m:c + 64 * m + 64]
                    for _ in shape:
                        v = v.unsqueeze(1)
                    return v.to_broadcast([P, *shape, 64])

                n = FIRST["w_in_2"]
                for c, (bank, h0, heads) in enumerate(((ACC, 0, 16), (UP, 8, 8))):
                    lo_until(n + 4 * c + 3 + 3)
                    piece_done(n + 4 * c + 3)
                    for m in range(M):
                        src = tall_out(bank, m).rearrange("p (h d) -> p h d", d=HD)[:, h0:h0 + heads, :]
                        dst = tok2.rearrange("p (m h d) -> p m h d", m=2, h=16)[:, m] if c == 0 else \
                            nqt[:, m, :].rearrange("p (h d) -> p h d", d=HD)
                        ta, tb = (t[:, 0:heads * HD].rearrange("p (h d) -> p h d", d=HD) for t in (t1, t2))
                        link(rope(dst, src, tab(C_COS, m, heads), tab(C_SIN, m, heads), ta, tb, HD // 2))
                    dve.sem_inc(S("roped"), 1)
                lo_until(n + 8 + 3 + 3)
                piece_done(n + 11)
                dve.wait_ge(S("dqk_turned"), 1)
                kd = tok2.rearrange("p (m a g u d) -> p m a g u d", m=2, a=4, g=2, u=2)
                for m in range(M):
                    src = tall_out(ACC, m, 768).rearrange("p (a v g d) -> p a v g d", a=3, v=2, g=2)[:, :, 0]
                    ta, tb = (t[:, 0:384].rearrange("p (a g d) -> p a g d", a=3, g=2) for t in (t1, t2))
                    link(rope(kd[:, m, 0:3, :, 0, :], src, tab(C_COS, m, 3, 2), tab(C_SIN, m, 3, 2), ta, tb, HD // 2))
                    ins = tt(kd[:, m, 0:3, :, 1, :], ta, tb, ALU.add)
                    link(ins)
                dve.sem_inc(S("roped"), 1)
                dve.wait_ge(S("gate_e"), 1)
                link(tsc(gates[:, :, :], gates[:, :, :], 1.0, 0.5, ALU.add, ALU.mult))
                dve.wait_ge(S("dqk_turned"), 1)
                for j in range(4):
                    dve.wait_ge(S("kd_turned"), j + 1)
                    dve.tensor_copy(kT2[:, j, :, :], ps[:, ACC + j, :].rearrange("p (g t) -> p g t", g=2))\
                        .then_inc(S("kT2"), 1)
                dve.wait_ge(S("kT2"), 4)
                for a_, kind in enumerate((0, 3)):
                    for par in range(2):
                        p0 = 64 * par
                        for g in range(2):
                            src = kT2[p0:p0 + 64, kind, g, :]
                            pos = vcol("kpos" if a_ == 0 else "vpos", 0, 16)[p0:p0 + 64, :]
                            win = src[:, 0:16 * 15].rearrange("p (n j q) -> p j n q", j=8, q=2)[:, :, :, par]
                            win2 = src[:, 16:256].rearrange("p (n j q) -> p j n q", j=8, q=2)[:, :, :, par]
                            for hh, wv in enumerate((win, win2)):
                                ins = tt(flat[p0:p0 + 64, a_, 8 * hh:8 * hh + 8, 15 * g:15 * g + 15], wv,
                                         pos[:, 8 * hh:8 * hh + 8].unsqueeze(2).to_broadcast([64, 8, 15]), ALU.add)
                link(ins)
                dve.sem_inc(S("flat"), 1)
                f2 = hl2[:, :, :].rearrange("p a b -> p (a b)")[:, 0:1920].rearrange("p (j n) -> p j n", j=32)
                dve.wait_ge(S("flat_hi"), 1)
                tt(f2[:, :, 30:60], flat.rearrange("p a j n -> p (a j) n"), f2[:, :, 0:30].bitcast(F32), ALU.subtract)\
                    .then_inc(S("flat_lo"), 1)
                lo_until(FIRST["w_out_2"] - 1 + 3)

                dve.wait_ge(S("hc_half"), 1)
                for a_ in range(2):
                    ins = tt(hidc[:, a_], ps[:, UP + 2 * a_:UP + 2 * a_ + 2, 0:30], hctmp[:, a_], ALU.add)
                ins.then_inc(S("hc"), 1)
                dve.wait_ge(S("hc_tanh"), 1)
                link(stt(hidc, hce, 1.0, hidc, ALU.add, ALU.mult))
                link(dve.memset(hidrep, 0.0))
                for c in range(2):
                    ins = dve.tensor_copy(
                        hidrep[:, c].rearrange("p (g r) n -> p g r n", g=2)[:, :, :, 0:15],
                        hidc[:, 1, c, :].rearrange("p (g n) -> p g n", g=2).unsqueeze(2).to_broadcast([P, 2, 4, 15]))
                ins.then_inc(S("hidc"), 1)
                HEADS = DH + NH
                pcv = nrm[:, 0, 0:256].rearrange("p (r n) -> p r n", n=16)[:, :, 0:15]
                sq = AR(3072, 8, P)

                def row_max(u):
                    b = u % 2
                    dve.wait_ge(S("att_scores"), u + 1)
                    if u >= 2:
                        dve.wait_ge(S("att_exp"), u - 1)
                    dve.tensor_reduce(nmx[b][:, 0:2], ps[:, 2 * b:2 * b + 2, 0:128], AX, ALU.max, negate=True)
                    dve.tensor_reduce(nmx[b][:, 2:4], ps[:, 2 * b:2 * b + 2, 128:384], AX, ALU.max, negate=True)\
                        .then_inc(S("att_max"), 1)

                def weigh(u):
                    b = u % 2
                    dve.wait_ge(S("att_exp"), u + 1)
                    link(dve.reciprocal(rinv[b], rsum[b]))
                    if u < DH:
                        for m in range(M):
                            ins = tt(cf[b][:, m:m + 1], rinv[b][:, 2 * m + 1:2 * m + 2], lamn[:, :], ALU.mult)
                        link(ins)
                        for m, c in enumerate((slice(0, 128), slice(128, 384))):
                            ins = tsc(p2[b][:, 1, c], p2[b][:, 1, c], cf[b][:, m:m + 1], None, ALU.mult)
                        link(ins)
                        for m, c in enumerate((slice(0, 128), slice(128, 384))):
                            ins = stt(p2[b][:, 0, c], p2[b][:, 0, c], rinv[b][:, 2 * m:2 * m + 1], p2[b][:, 1, c],
                                      ALU.mult, ALU.add)
                    else:
                        h = u - DH
                        gt = gates[:, :, 3 * h + 1:3 * h + 3]
                        link(tt(cf[b].rearrange("p (m a) -> p m a", m=2), rinv[b].rearrange("p (m a) -> p m a", m=2),
                                gt, ALU.mult))
                        for m, c in enumerate((slice(0, 128), slice(128, 384))):
                            for a_ in range(2):
                                ins = tsc(p2[b][:, a_, c], p2[b][:, a_, c], cf[b][:, 2 * m + a_:2 * m + a_ + 1], None,
                                          ALU.mult)
                    ins.then_inc(S("att_probs"), 1)

                def compressed_kv():
                    dve.wait_ge(S("cmp_kv"), 1)
                    tsc(kcT, ps[:, UP + 2, 0:30], 0.5, None, ALU.mult).then_inc(S("kcT"), 1)
                    stt(vsel, ps[:, UP + 3, 0:64].unsqueeze(1).to_broadcast([P, 8, 64]), 0.5,
                        cst[:, C_BLK:C_BLK + 8].unsqueeze(2).to_broadcast([P, 8, 64]), ALU.mult, ALU.mult)\
                        .then_inc(S("vsel"), 1)

                def compressed_shift():
                    dve.wait_ge(S("cscores"), 1)
                    neg = cst[:, C_CNEG:C_CNEG + 32].rearrange("p (m n) -> p m n", m=2)[:, :, 0:15]
                    for par in range(2):
                        ins = tt(pc[:, par, :, :, 0:15],
                                 ps[:, UP + 2 + par, 0:128].rearrange("p (h m n) -> p h m n", h=4, m=2)[:, :, :, 0:15],
                                 neg.unsqueeze(1).to_broadcast([P, 4, 2, 15]), ALU.add)
                    ins.then_inc(S("cscores_read"), 1)
                    dve.wait_ge(S("cscores_read"), 1)
                    link(dve.tensor_reduce(cmx, pcv, AX, ALU.max))
                    tt(pcv, pcv, cmx.unsqueeze(2).to_broadcast([P, 16, 15]), ALU.subtract).then_inc(S("cshift"), 1)

                def compressed_weigh():
                    dve.wait_ge(S("cexp"), 1)
                    link(dve.tensor_reduce(crs, pcv, AX, ALU.add))
                    link(dve.reciprocal(crs, crs))
                    crv = crs.rearrange("p (a h m) -> p a h m", a=2, h=4)
                    gv = gates[:, :, :].rearrange("p m (h a b) -> p a h m b", a=2, b=3)
                    for par in range(2):
                        ins = tt(crv[:, par], crv[:, par], gv[:, par, :, :, 0], ALU.mult)
                    link(ins)
                    link(tt(pcv, pcv, crs.unsqueeze(2).to_broadcast([P, 16, 15]), ALU.mult))
                    link(dve.memset(pcm, 0.0))
                    pmv = pcm.rearrange("p m (h a) n -> p a h m n", a=2)
                    one = cst[:, C_CONE:C_CONE + 32].rearrange("p (m n) -> p m n", m=2)[:, :, 0:15]
                    for par in range(2):
                        ins = tt(pmv[:, par, :, :, 0:15], pc[:, par, :, :, 0:15],
                                 one.unsqueeze(1).to_broadcast([P, 4, 2, 15]), ALU.mult)
                    ins.then_inc(S("pcm"), 1)

                def diff_out(u):
                    dve.wait_ge(S("att_out"), u + 1)
                    dve.tensor_copy(od[:, 2 * u:2 * u + 2, :], ps[:, 6 + u % 2, 0:256].rearrange("p (m e) -> p m e", m=2))\
                        .then_inc(S("od"), 1)

                for t in range(HEADS + 2):
                    if t < HEADS:
                        row_max(t)
                    if t == 0:
                        compressed_kv()
                    if t == 1:
                        compressed_shift()
                    if t == 2:
                        compressed_weigh()
                    if t == DH + 1:
                        dve.wait_ge(S("pcm_turned"), 1)
                        dve.tensor_copy(pcT, ps[:, UP, 0:256]).then_inc(S("pcT"), 1)
                    if 1 <= t <= HEADS:
                        weigh(t - 1)
                    if 2 <= t < 2 + DH:
                        diff_out(t - 2)
                    if t == DH + 2:
                        dve.wait_ge(S("od"), DH)
                        link(tt(sq, od, od, ALU.mult))
                    if t == DH + 3:
                        dve.tensor_reduce(ss8, sq, AX, ALU.add).then_inc(S("diff_ssq"), 1)
                    if t == DH + 4:
                        dve.wait_ge(S("diff_rstd"), 1)
                        link(tt(od, od, rs8.unsqueeze(2).to_broadcast([P, 8, P]), ALU.mult))
                    if t == DH + 5:
                        stt(od, od, 1.0 - LAM_INIT, bc[:, 640:768].unsqueeze(1).to_broadcast([P, 8, P]),
                            ALU.mult, ALU.mult).then_inc(S("o_normed"), 1)
                    if t >= DH + 4 and t % 2 == 0 and t <= HEADS:
                        pair = (t - DH) // 2 - 2
                        his[0] += 1
                        act_lo(ps[:, 6 + pair % 2, 0:T].unsqueeze(1), 4 + pair, 1, his[0])
                for j in range(2):
                    his[0] += 1
                    act_lo(turned(ACC, 2 * j, 2), 2 * j, 2, his[0])
                his[0] += 1
                act_lo(ps[:, 7, 0:T].unsqueeze(1), 7, 1, his[0])
                boundary(5, FIRST["ffn"] - 1)

                f0 = FIRST["ffn"]

                def silu_gate(i):
                    for j in range(2):
                        dve.wait_ge(S("ff_half"), 2 * i + j + 1)
                        dst = (gsum, usum)[j]
                        tt(dst, ps[:, UP + 2 * j:UP + 2 * j + 2, 0:T], htmp[:, 2 * j:2 * j + 2, :], ALU.add)\
                            .then_inc(S("ff_sum"), 1)
                    dve.wait_ge(S("ff_tanh"), i + 1)
                    link(stt(gsum, esum, 1.0, gsum, ALU.add, ALU.mult))
                    tt(hb[:, 0:2, :], gsum, usum, ALU.mult).then_inc(S("ff_hidden"), 1)

                def ff_lo(i):
                    dve.wait_ge(S("ff_hi"), i + 1)
                    stt(hl2[:, 0:2, T:2 * T], hb[:, 0:2, :], 0.5, hl2[:, 0:2, 0:T].bitcast(F32), ALU.mult, ALU.subtract)\
                        .then_inc(S("ff_lo"), 1)

                lo_until(f0 + 2)
                silu_gate(0)
                lo_until(f0 + 3)
                ff_lo(0)
                with dve.Fori(0, FF_BLOCKS - 2) as i:
                    me.enter(i, 1)
                    lo(f0 + 4, i, 3)
                    lo(f0 + 5, i, 3)
                    silu_gate(i + 1)
                    lo(f0 + 6, i, 3)
                    ff_lo(i + 1)
                me.leave(FF_BLOCKS - 2)
                cursor[0] = f0 + 4 + 3 * (FF_BLOCKS - 2)
                lo_until(N_PIECES)
                silu_gate(FF_BLOCKS - 1)
                ff_lo(FF_BLOCKS - 1)
                post_tile(0, N_PIECES - 1)
                post_tile(1, N_PIECES - 1)

            @block.scalar
            def _(act):
                me = Steps(act, S("act_step"))
                link = me.link
                f = act.activation

                def small(dst, src, sem="small"):
                    act.dma_start(dst, src).then_inc(S(sem), 16)

                small(gain[0][:, :], a["sandwich_gains"][0, 0, :].partition_broadcast(P), "gain0")
                small(cst[:, :], a["shape_constants"], "cst_in")
                his = [0]

                def piece_done(n, turn=0, per=0):
                    act.wait_ge(S("pe_piece"), turn * per + n + 1)

                def act_high(src, k0, n, scale=1.0):
                    f(act_hl[:, k0:k0 + n, 0:T], src, ACT.Copy, scale=scale).then_inc(S("act_hi"), 1)

                turns, gained, outs = [0], [0], [0]

                def square(m, src, total, at=0):
                    f(junk[:, m, at:at + src.shape[1]], src, ACT.Square, scale=1.0 / D ** 0.5, accum_out=total)\
                        .then_inc(S("ssq"), 1)

                def post_square(m, last):
                    if m == 0:
                        outs[0] += 1
                        act.wait_ge(S("tile_out"), outs[0])
                    else:
                        piece_done(last)
                    y = tall_out(ACC, m)
                    square(m, y[:, 0:512], ssh[:, 2 * m:2 * m + 1])
                    gained[0] += 1
                    act.wait_ge(S("gained"), gained[0])
                    square(m, y[:, 512:D], ssh[:, 2 * m + 1:2 * m + 2], 512)

                def high_tile(m, bank):
                    for j in range(2):
                        turns[0] += 1
                        act.wait_ge(S("turned"), turns[0])
                        f(act_hl[:, 4 * j:4 * j + 4, m * P:(m + 1) * P], turned_tile(bank, m, j), ACT.Copy)\
                            .then_inc(S("act_hi"), 1)

                def boundary(s, last):
                    post_square(0, last)
                    act.wait_ge(S("x_new"), 2 * (s - 1) + 1)
                    square(0, x[:, 0, :], ssx[:, 0:1])
                    post_square(1, last)
                    high_tile(0, TURN_BANK[s])
                    act.wait_ge(S("x_new"), 2 * (s - 1) + 2)
                    square(1, x[:, 1, :], ssx[:, 1:2])
                    high_tile(1, TURN_BANK[s])

                def high_of_turned(bank, pairs):
                    for j in range(pairs):
                        turns[0] += 1
                        act.wait_ge(S("turned"), turns[0])
                        act_high(turned(bank, 2 * j, 2), 2 * j, 2)

                for m in range(M):
                    act.wait_ge(S(f"x_in{m}"), 16)
                    square(m, x[:, m, :], ssx[:, m:m + 1])
                for m in range(M):
                    high_tile(m, ACC)
                for i in range(2):
                    act.wait_ge(S("angles"), i + 1)
                    red = rt[:, 4 + i:5 + i, 0:32].rearrange("p o (m f) -> p (o m) f", m=2)
                    f(cs1[:, i, :, 16 * i:16 * i + 16], red, ACT.Sin).then_inc(S("sines"), 1)
                act.wait_ge(S("lam_sums"), 1)
                act.wait_ge(S("dve_step"), 1)
                f(lam4[:, 2:4], lam4[:, 0:2], ACT.Exp).then_inc(S("lam_exp"), 1)
                for b in range(3):
                    piece_done(FIRST["w_in_wide"] + 2 * b + 1)
                    if b:
                        act.wait_ge(S("wide_read"), b)
                    bank = (UP, ACC, UP)[b]
                    f(ctmp, ps[:, bank:bank + 4, T:2 * T], ACT.Copy).then_inc(S("half_copied"), 1)
                piece_done(FIRST["w_uq"] - 1)
                for c0, c1, i in ((0, QR, 0), (QR, QR + KVR, 2)):
                    for m in range(M):
                        f(lat[:, m, c0:c1], tall_out(ACC, m)[:, c0:c1], ACT.Square, accum_out=ss4[:, i + m:i + m + 1])\
                            .then_inc(S("lat_ssq"), 1)
                for i, (k, n) in enumerate(((0, 2), (2, 2), (4, 1))):
                    act.wait_ge(S("lat_turned"), i + 1)
                    f(hl2[:, k:k + n, 0:T], turned(UP, k, n), ACT.Copy).then_inc(S("lat_hi"), 1)
                act.wait_ge(S("ya"), 1)
                act_high(gate_b, 0, 4)
                piece_done(FIRST["w_uq"] + 1)
                for m in range(M):
                    src = tall_out(ACC, m, NH * QKD).rearrange("p (h d) -> p h d", h=NH)[:, :, 0:NOPE]
                    f(qf[:, m, :, 0:NOPE], src, ACT.Copy).then_inc(S("q_nope"), 1)
                piece_done(FIRST["w_ukv"])
                for m in range(M):
                    src = tall_out(UP, m).rearrange("p (h d) -> p h d", h=NH)
                    f(kf[:, m, :, 0:NOPE], src[:, :, 0:NOPE], ACT.Copy)
                    f(v1[:, m, :, :], src[:, :, NOPE:NOPE + VD], ACT.Copy).then_inc(S("kv_nope"), 1)
                act.wait_ge(S("act_lo"), 5)
                for j in range(4):
                    act.wait_ge(S("q_turned"), j + 1)
                    f(qT[0:QKD, 2 * j:2 * j + 2, :], ps[0:QKD, ACC + j, :].rearrange("p (h t) -> p h t", h=2),
                      ACT.Copy, scale=float(QKD) ** -0.5).then_inc(S("qT"), 1)

                def pair_out(h, sem, bank, k0):
                    act.wait_ge(S(sem), h + 1)
                    act_high(ps[:, bank, 0:T].unsqueeze(1), k0, 1)

                def prob_turned(h):
                    act.wait_ge(S("probs_turned"), h + 1)
                    if h >= 2:
                        act.wait_ge(S("pv"), h - 1)
                    f(probT[h % 2], ps[:, 2 + h % 2, :].rearrange("p (k t) -> p k t", k=2), ACT.Copy)\
                        .then_inc(S("probT"), 1)

                for h in range(NH):
                    b = h % 2
                    act.wait_ge(S("row_max"), h + 1)
                    if h >= 2:
                        act.wait_ge(S("probs_turned"), h - 1)
                    for m in range(M):
                        ins = f(prob[b][:, m, :], ps[:, b, m * T:(m + 1) * T], ACT.Exp, bias=nmx[b][:, m:m + 1],
                                accum_out=rsum[b][:, m:m + 1])
                    ins.then_inc(S("probs_exp"), 1)
                    if h >= 1:
                        prob_turned(h - 1)
                    if h % 2 == 0 and h >= 4:
                        pair_out(h - 3, "pv", 4 + (h // 2 - 2) % 2, 4 + h // 2 - 2)
                prob_turned(NH - 1)
                pair_out(5, "pv", 4, 6)
                pair_out(7, "pv", 5, 7)
                boundary(1, FIRST["mlp0"] - 1)

                def mlp(n0, s):
                    blocks = MLP_BLOCKS * s

                    def half_copy(i, turn):
                        for j in range(2):
                            if j == 0:
                                act.wait_ge(S("front_out"), blocks + i + 1)
                            else:
                                piece_done(n0 + 1 if turn is None else n0 + 3, 0 if turn is None else turn, 4)
                            if turn is not None:
                                act.wait_ge(S("hidden"), 2 * blocks + 2 * i - 1 + j)
                            f(htmp[:, 2 * j:2 * j + 2, :], ps[:, UP + 2 * j:UP + 2 * j + 2, T:2 * T], ACT.Copy)\
                                .then_inc(S("half_copied"), 1)

                    def hidden_hi(i, turn):
                        for j in range(2):
                            if turn is not None:
                                piece_done(n0 + 4 + j, turn, 4)
                            act.wait_ge(S("hidden"), 2 * blocks + 2 * i + j + 1)
                            f(hl2[:, 2 * j:2 * j + 2, 0:T], hb[:, 2 * j:2 * j + 2, :], ACT.Copy).then_inc(S("hid_hi"), 1)

                    half_copy(0, None)
                    hidden_hi(0, None)
                    with act.Fori(0, MLP_BLOCKS - 1) as i:
                        half_copy(i + 1, i)
                        hidden_hi(i + 1, i)
                    boundary(2 * s + 2, n0 + 4 * MLP_BLOCKS - 1)

                mlp(FIRST["mlp0"], 0)

                def diagonal(i):
                    if i >= DIAGS:
                        act.wait_ge(S("diag_used"), i - DIAGS + 1)
                    f(diag[:, i % DIAGS, :], ident, ACT.Copy, scale=dwcol(PE_TAPS[i][1], PE_TAPS[i][0]))\
                        .then_inc(S("diag"), 1)

                for b in range(4):
                    if b == 3:
                        for i in range(DIAGS):
                            diagonal(i)
                    piece_done(FIRST["pw1"] + 2 * b + 1)
                    if b:
                        act.wait_ge(S("ag"), 4 * b)
                    bank = (UP, ACC)[b % 2]
                    f(ptmp, ps[:, bank:bank + 4, T:2 * T], ACT.Copy).then_inc(S("pw_half"), 1)
                    if b == 3:
                        for i in range(DIAGS, 2 * DIAGS):
                            diagonal(i)
                    act.wait_ge(S("ag"), 4 * b + 4)
                    if b:
                        act.wait_ge(S("u"), b)
                    f(eg, ag[:, 2:4, :], ACT.Tanh, scale=0.5).then_inc(S("gate_tanh"), 1)
                built = 2 * DIAGS
                for q, c in enumerate((4, 5, 6, 7)):
                    used = SHARED_TAPS + q * TAPS
                    for i in range(built, min(used + DIAGS, len(PE_TAPS))):
                        diagonal(i)
                    built = max(built, used + DIAGS)
                    act.wait_ge(S("diag_used"), used)
                    f(cv[:, c, :], ps[:, UP + q, 0:T], ACT.Identity, bias=vcol("b_dw", c)).then_inc(S("conv_act"), 1)

                def silu_high(j):
                    act.wait_ge(S("silu"), j + 1)
                    act_high(zb[:, 2 * j:2 * j + 2, :], 2 * j, 2, 0.5)

                for k in range(KD):
                    act.wait_ge(S("turned"), turns[0] + k // 2 + 1)
                    f(zb[:, k, :], turned(UP, k, 1)[:, 0, :], ACT.Identity, bias=vcol("ln_b", k), scale=vcol("ln_g", k))\
                        .then_inc(S("z"), 1)
                    if k % 2:
                        act.wait_ge(S("z"), k + 1)
                        f(eb[:, k - 1:k + 1, :], zb[:, k - 1:k + 1, :], ACT.Tanh, scale=0.5).then_inc(S("z_tanh"), 1)
                        if k > 1:
                            silu_high(k // 2 - 1)
                silu_high(3)
                turns[0] += 4
                boundary(3, FIRST["mlp1"] - 1)
                mlp(FIRST["mlp1"], 1)

                n = FIRST["w_in_2"]
                piece_done(n + 7)
                for m in range(M):
                    ins = f(dv[:, m, :], tall_out(UP, m)[:, 0:512], ACT.Copy)
                ins.then_inc(S("dv"), 1)
                for j in range(4):
                    act.wait_ge(S("dqk_turned4"), j + 1)
                    f(dqkT[:, 2 * j:2 * j + 2, :], ps[:, UP + j, :].rearrange("p (h t) -> p h t", h=2), ACT.Copy,
                      scale=HD ** -0.5 if j < 2 else 1.0).then_inc(S("dqkT"), 1)
                act.wait_ge(S("roped"), 3)
                for m in range(M):
                    src = tall_out(ACC, m)[:, 0:792]
                    f(vsw[:, m, :, :], src[:, 256:768].rearrange("p (a v n) -> p a v n", a=2, v=2)[:, :, 1, :], ACT.Copy)
                    f(gates[:, m, :], src[:, 768:792], ACT.Tanh, scale=0.5)
                    kd = tok2.rearrange("p (m a g u d) -> p m a g u d", m=2, a=4, g=2, u=2)
                    for u in range(2):
                        ins = f(kd[:, m, 3, :, u, :], src[:, 128:256].rearrange("p (g d) -> p g d", g=2), ACT.Copy)
                ins.then_inc(S("gate_e"), 1)
                for j in range(2):
                    act.wait_ge(S("nq_turned"), j + 1)
                    f(nqT[:, 2 * j:2 * j + 2, :], ps[:, UP + j, :].rearrange("p (h t) -> p h t", h=2), ACT.Copy,
                      scale=HD ** -0.5).then_inc(S("nqT"), 1)
                f2 = hl2[:, :, :].rearrange("p a b -> p (a b)")[:, 0:1920].rearrange("p (j n) -> p j n", j=32)
                act.wait_ge(S("flat"), 1)
                f(f2[:, :, 0:30], flat.rearrange("p a j n -> p (a j) n"), ACT.Copy).then_inc(S("flat_hi"), 1)
                piece_done(FIRST["w_out_2"] - 1)
                for a_ in range(2):
                    ins = f(hctmp[:, a_], ps[:, UP + 2 * a_:UP + 2 * a_ + 2, 30:60], ACT.Copy)
                ins.then_inc(S("hc_half"), 1)
                act.wait_ge(S("hc"), 1)
                f(hce, hidc, ACT.Tanh, scale=0.5).then_inc(S("hc_tanh"), 1)

                HEADS = DH + NH

                def exponentials(u):
                    b = u % 2
                    act.wait_ge(S("att_max"), u + 1)
                    if u >= 2:
                        act.wait_ge(S("att_turned"), u - 1)
                    for m, c in enumerate((slice(0, 128), slice(128, 384))):
                        for j in range(2):
                            k = 2 * m + j
                            ins = f(p2[b][:, j, c], ps[:, 2 * b + j, c], ACT.Exp, bias=nmx[b][:, k:k + 1],
                                    accum_out=rsum[b][:, k:k + 1])
                    ins.then_inc(S("att_exp"), 1)

                def probs_turned(u):
                    act.wait_ge(S("att_turned"), u + 1)
                    if u >= 2:
                        act.wait_ge(S("att_out"), u - 1)
                    if u < DH:
                        f(pt2[u % 2][:, 0, :], ps[:, 4 + u % 2, 0:384], ACT.Copy).then_inc(S("att_pT"), 1)
                    else:
                        f(pt2[u % 2], ps[:, 4:6, 0:384], ACT.Copy).then_inc(S("att_pT"), 1)

                for t in range(HEADS + 1):
                    if t < HEADS:
                        exponentials(t)
                    if t == 1:
                        act.wait_ge(S("cshift"), 1)
                        pcv = nrm[:, 0, 0:256].rearrange("p (r n) -> p r n", n=16)[:, :, 0:15]
                        f(pcv, pcv, ACT.Exp).then_inc(S("cexp"), 1)
                    if t >= 1:
                        probs_turned(t - 1)
                    if t >= DH + 4 and t % 2 == 0:
                        pair = (t - DH) // 2 - 2
                        pair_out(DH + 2 * pair + 1, "att_out", 6 + pair % 2, 4 + pair)
                high_of_turned(ACC, 2)
                pair_out(HEADS - 1, "att_out", 7, 7)
                boundary(5, FIRST["ffn"] - 1)
                f0 = FIRST["ffn"]

                def gate_half(i, turn):
                    for j in range(2):
                        if j == 0:
                            act.wait_ge(S("front_out"), 2 * MLP_BLOCKS + i + 1)
                        else:
                            piece_done(f0 + 1 if turn is None else f0 + 3, 0 if turn is None else turn, 3)
                        if turn is not None:
                            act.wait_ge(S("ff_sum"), 2 * i - 1 + j)
                        f(htmp[:, 2 * j:2 * j + 2, :], ps[:, UP + 2 * j:UP + 2 * j + 2, T:2 * T], ACT.Copy)\
                            .then_inc(S("ff_half"), 1)
                    act.wait_ge(S("ff_sum"), 2 * i + 1)
                    if turn is not None:
                        act.wait_ge(S("ff_hidden"), i)
                    f(esum, gsum, ACT.Tanh, scale=0.5).then_inc(S("ff_tanh"), 1)

                def ff_hi(i):
                    act.wait_ge(S("ff_hidden"), i + 1)
                    f(hl2[:, 0:2, 0:T], hb[:, 0:2, :], ACT.Copy, scale=0.5).then_inc(S("ff_hi"), 1)

                gate_half(0, None)
                ff_hi(0)
                with act.Fori(0, FF_BLOCKS - 1) as i:
                    gate_half(i + 1, i)
                    piece_done(f0 + 4, i, 3)
                    ff_hi(i + 1)
                post_square(0, N_PIECES - 1)
                post_square(1, N_PIECES - 1)

            @block.tensor
            def _(pe):
                def mm(o, l, r, start, stop):
                    return pe.matmul(o, l, r, start=start, stop=stop, skip_group_check=True)

                def turn(o, src):
                    return pe.transpose(o, src, ident[0:src.shape[0], 0:src.shape[0]])

                def arrived(n, turn_=0, per=0):
                    pe.wait_ge(S("w_split"), turn_ * per + n + 1)

                def pv_hl(tile, n):
                    return tile[slot_of(n)][:, :].rearrange("p (k n) -> p k n", k=4)

                def wide(n, bank, lhs_k0, moving, first, last, k, cols, turn_=0, per=0, read=None, out=False):
                    arrived(n, turn_, per)
                    wh = w_hi[slot_of(n)][:, 0:k * cols].rearrange("p (k n) -> p k n", k=k)
                    wl = w_lo[slot_of(n)][:, 0:k * cols].rearrange("p (k n) -> p k n", k=k)
                    width = moving.shape[2]
                    for c in range(cols // P):
                        if read and c % 2 == 0:
                            pe.wait_ge(S(read[0]), read[1 + c // 2])
                        for kk in range(k):
                            act_k = moving[:, lhs_k0 + kk, :]
                            s = slice(c * P, (c + 1) * P)
                            mm(ps[:, bank + c, 0:width], wh[:, kk, s], act_k, first and kk == 0, False)
                            ins = mm(ps[:, bank + c, 0:width // 2], wl[:, kk, s], act_k[:, 0:width // 2],
                                     False, last and kk == k - 1)
                        if out and c == 1:
                            ins.then_inc(S("front_out"), 1)
                    ins.then_inc(S("pe_piece"), 1)

                def tall(n, bank, lhs, lhs_k0, first, last, k, cols, turn_=0, per=0, tiles=range(M), free=True):
                    arrived(n, turn_, per)
                    wh = w_hi[slot_of(n)][:, 0:k * cols].rearrange("p (k n) -> p k n", k=k)
                    wl = w_lo[slot_of(n)][:, 0:k * cols].rearrange("p (k n) -> p k n", k=k)
                    for kk in range(k):
                        for m in tiles:
                            h = lhs[:, lhs_k0 + kk, m * P:(m + 1) * P]
                            l = lhs[:, lhs_k0 + kk, T + m * P:T + (m + 1) * P]
                            for part, (lt, w) in enumerate(((h, wh), (h, wl), (l, wh))):
                                for j, c0 in enumerate(range(0, cols, 512)):
                                    c1 = min(cols, c0 + 512)
                                    ins = mm(ps[:, bank + 2 * m + j, 0:c1 - c0], lt, w[:, kk, c0:c1],
                                             first and kk == 0 and part == 0, last and kk == k - 1 and part == 2)
                    if free:
                        ins.then_inc(S("pe_piece"), 1)
                    return ins

                def tall_by_tile(n, count, lhs, lhs_k0, first=False, lows=None):
                    for m in range(M):
                        for j in range(count):
                            if lows and m == 0:
                                pe.wait_ge(S("hid_lo"), lows + j)
                            ins = tall(n + j, ACC, lhs, lhs_k0 + 2 * j, first and j == 0, j == count - 1, 2, 1024,
                                       tiles=(m,), free=m == 1)
                        if m == 0:
                            ins.then_inc(S("tile_out"), 1)

                normed, lows = [0], [0]

                def turn_m(bank, m):
                    normed[0] += 1
                    pe.wait_ge(S("normed"), normed[0])
                    for k in range(KD):
                        ins = turn(turned_tile(bank, m, k // 4)[:, k % 4, :], nrm[:, m, k * P:(k + 1) * P])
                        if k % 4 == 3:
                            ins.then_inc(S("turned"), 1)

                def wide_by_tile(n, turn_bank, between=None, out=False):
                    def by_tile(v, m):
                        return v.rearrange("p (a t) -> p a t", a=2)[:, :, m * P:(m + 1) * P]

                    for m in range(M):
                        if m == 1:
                            turn_m(turn_bank, 1)
                        for h in range(2):
                            need_lows(lows[0] + 2 * m + h + 1)
                            pe.wait_ge(S("w_hi"), n + h + 1)
                            wh = pv_hl(w_hi, n + h)
                            for kk in range(4):
                                for c in range(4):
                                    ins = mm(by_tile(ps[:, UP + c, :], m), wh[:, kk, c * P:(c + 1) * P],
                                             by_tile(act_hl[:, 4 * h + kk, :], m), m == 0 and h == 0 and kk == 0, False)
                    if between:
                        between()
                    arrived(n + 1)
                    for c in range(4):
                        for h in range(2):
                            wl = pv_hl(w_lo, n + h)
                            for kk in range(4):
                                ins = mm(ps[:, UP + c, 0:T], wl[:, kk, c * P:(c + 1) * P],
                                         act_hl[:, 4 * h + kk, 0:T], False, h == 1 and kk == 3)
                            if c == 3:
                                ins.then_inc(S("pe_piece"), 1)
                        if out and c == 1:
                            ins.then_inc(S("front_out"), 1)

                def turn_normed(bank=ACC):
                    for k in range(KD):
                        for m in range(M):
                            pe.wait_ge(S("normed"), normed[0] + m + 1)
                            ins = turn(turned(bank, k, 1)[:, 0, m * P:(m + 1) * P], nrm[:, m, k * P:(k + 1) * P])
                        if k % 2:
                            ins.then_inc(S("turned"), 1)
                    normed[0] += 2

                def need_lows(n):
                    pe.wait_ge(S("act_lo"), n)

                pe.wait_ge(S("cst_in"), 16)
                turn_m(ACC, 0)
                n = FIRST["w_in_wide"]

                def turn_rows():
                    pe.wait_ge(S("rows_in"), 16 * 9)
                    for i in range(3):
                        r = VROWS if i == 0 else DROWS
                        ins = turn(ps[:, ACC + 3, i * P:i * P + r], rows[0:r, i, :])
                    ins.then_inc(S("cols"), 1)

                wide_by_tile(n, ACC, turn_rows)
                pe.wait_ge(S("cols_read"), 1)
                for b in (1, 2):
                    if b == 2:
                        pe.wait_ge(S("wide_read"), 1)
                    for h in range(2):
                        wide(n + 2 * b + h, (UP, ACC, UP)[b], 4 * h, act_hl, h == 0, h == 1, 4, 512)
                lows[0] += 4
                pe.wait_ge(S("wide_read"), 2)
                for j, (k, kn) in enumerate(TALL_K):
                    tall(FIRST["w_in_tall"] + j, ACC, act_hl, k, j == 0, j == 2, kn, A_COLS)
                pe.wait_ge(S("wide_read"), 3)
                for i, (k, kn) in enumerate(((0, 2), (2, 2), (4, 1))):
                    for kk in range(k, k + kn):
                        for m in range(M):
                            pe.wait_ge(S("lat_normed"), m + 1)
                            ins = turn(turned(UP, kk, 1)[:, 0, m * P:(m + 1) * P], lat[:, m, kk * P:(kk + 1) * P])
                    ins.then_inc(S("lat_turned"), 1)
                pe.wait_ge(S("kpe"), 1)
                for j, (k, kn) in enumerate(UQ_K):
                    pe.wait_ge(S("lat_lo"), (1, 2)[j])
                    tall(FIRST["w_uq"] + j, ACC, hl2, k, j == 0, j == 1, kn, NH * QKD)
                pe.wait_ge(S("lat_lo"), 3)
                tall(FIRST["w_ukv"], UP, hl2, 3, True, True, 2, 1024)
                pe.wait_ge(S("q_nope"), 2)
                pe.wait_ge(S("q_rope"), 2)
                for h in range(NH):
                    for m in range(M):
                        ins = turn(ps[0:QKD, ACC + h // 2, (h % 2) * T + m * P:(h % 2) * T + (m + 1) * P], qf[:, m, h, :])
                    if h % 2:
                        ins.then_inc(S("q_turned"), 1)
                pe.wait_ge(S("kv_nope"), 2)
                for h in range(NH):
                    for m in range(M):
                        ins = turn(ps[0:QKD, UP + h // 2, (h % 2) * T + m * P:(h % 2) * T + (m + 1) * P], kf[:, m, h, :])
                    if h % 2:
                        ins.then_inc(S("k_turned"), 1)
                pe.wait_ge(S("qT"), 4)
                def probs_times_v(h):
                    if h == 0:
                        pe.wait_ge(S("kT"), 4)
                    pe.wait_ge(S("probT"), h + 1)
                    if h % 2 == 0 and h >= 4:
                        need_lows(5 + h // 2 - 1)
                    r = 64 * (h % 2)
                    for k in range(M):
                        ins = mm(ps[r:r + 64, 4 + (h // 2) % 2, 0:T], v1[:, k, h, :], probT[h % 2][:, k, :],
                                 k == 0, k == 1)
                    ins.then_inc(S("pv"), 1)

                for t in range(NH + 1):
                    if t < NH:
                        if t % 2 == 0:
                            pe.wait_ge(S("kT"), t // 2 + 1)
                        if t >= 2:
                            pe.wait_ge(S("probs_exp"), t - 1)
                        for m in range(M):
                            ins = mm(ps[:, t % 2, m * T:(m + 1) * T], qT[0:QKD, t, m * P:(m + 1) * P], kT1[0:QKD, t, :],
                                     True, True)
                        ins.then_inc(S("scores"), 1)
                    if t >= 2:
                        probs_times_v(t - 2)
                    if t >= 1:
                        h = t - 1
                        if h >= 2:
                            pe.wait_ge(S("probT"), h - 1)
                        for m in range(M):
                            pe.wait_ge(S("probs"), 2 * h + m + 1)
                            for k in range(M):
                                ins = turn(ps[:, 2 + h % 2, k * T + m * P:k * T + (m + 1) * P],
                                           prob[h % 2][:, m, k * P:(k + 1) * P])
                        ins.then_inc(S("probs_turned"), 1)
                pe.wait_ge(S("probT"), NH)
                tall(FIRST["w_out"], ACC, act_hl, 0, True, False, 2, 1024)
                probs_times_v(NH - 1)
                tall(FIRST["w_out"] + 1, ACC, act_hl, 2, False, False, 2, 1024)
                need_lows(9)
                tall_by_tile(FIRST["w_out"] + 2, 2, act_hl, 4)
                turn_m(ACC, 0)
                lows[0] = 9

                def mlp(n0, s):
                    blocks = MLP_BLOCKS * s
                    wide_by_tile(n0, ACC, out=True)
                    lows[0] += 4

                    def up(n, i, per):
                        free = ("hidden", 2 * blocks + 2 * i + 1, 2 * blocks + 2 * i + 2)
                        for h in range(2):
                            wide(n + h, UP, 4 * h, act_hl, h == 0, h == 1, 4, 512, i, per,
                                 read=free if h == 0 else None, out=h == 1)

                    def down(n, i, per, first):
                        for h in range(2):
                            tall(n + h, ACC, hl2, 2 * h, first and h == 0, False, 2, 1024, i, per)

                    up(n0 + 2, 0, 0)
                    pe.wait_ge(S("hid_lo"), 2 * blocks + 2)
                    down(n0 + 4, 0, 0, True)
                    with pe.Fori(1, MLP_BLOCKS - 1) as i:
                        up(n0 + 2, i, 4)
                        pe.wait_ge(S("hid_lo"), 2 * i + 2 * blocks + 2)
                        down(n0 + 4, i, 4, False)
                    tall_by_tile(n0 + 4 * MLP_BLOCKS - 2, 2, hl2, 0, lows=2 * blocks + 2 * MLP_BLOCKS - 1)
                    turn_m(TURN_BANK[2 * s + 2], 0)

                mlp(FIRST["mlp0"], 0)
                wide_by_tile(FIRST["pw1"], ACC)
                for b in range(1, 4):
                    if b >= 2:
                        pe.wait_ge(S("ag"), 4 * (b - 1))
                    for h in range(2):
                        wide(FIRST["pw1"] + 2 * b + h, (UP, ACC)[b % 2], 4 * h, act_hl, h == 0, h == 1, 4, 512)
                lows[0] += 4
                pe.wait_ge(S("ag"), 12)
                for i, (c, t) in enumerate(PE_TAPS):
                    last = i + 1 == len(PE_TAPS) or PE_TAPS[i + 1][0] != c
                    if t == 0:
                        pe.wait_ge(S("u"), c // 2 + 1)
                    pe.wait_ge(S("diag"), i + 1)
                    mm(ps[:, UP + c - 4, 0:T], diag[:, i % DIAGS, :], upad[:, c, t:t + T], t == 0, last)\
                        .then_inc(S("diag_used"), 1)
                pe.wait_ge(S("ag"), 16)
                pe.wait_ge(S("conv_act"), 4)
                pe.wait_ge(S("conv_dve"), 1)
                pe.wait_ge(S("conv_pool"), 1)
                for m in range(M):
                    for c in range(KD):
                        ins = turn(tall_out(ACC, m)[:, c * P:(c + 1) * P], cv[:, c, m * P:(m + 1) * P])
                    ins.then_inc(S("cv_turned"), 1)
                turn_normed(UP)
                for j in range(4):
                    need_lows(lows[0] + j + 1)
                    if j == 0:
                        pe.wait_ge(S("ones"), 1)
                        pe.wait_ge(S("b_pw2"), 16)
                        for m in range(M):
                            for h in range(2):
                                mm(ps[:, ACC + 2 * m + h, :], ones[:, :], brow[0:1, 512 * h:512 * h + 512],
                                   True, False)
                    if j < 2:
                        tall(FIRST["pw2"] + j, ACC, act_hl, 2 * j, False, False, 2, 1024)
                tall_by_tile(FIRST["pw2"] + 2, 2, act_hl, 4)
                lows[0] += 4
                turn_m(ACC, 0)
                mlp(FIRST["mlp1"], 1)

                n = FIRST["w_in_2"]
                for m in range(M):
                    if m == 1:
                        turn_m(UP, 1)
                    for j in range(4):
                        need_lows(lows[0] + 2 * m + j // 2 + 1)
                        tall(n + j, ACC, act_hl, 2 * j, j == 0, j == 3, 2, 1024, tiles=(m,), free=m == 1)
                for c, (bank, cols) in ((1, (UP, 1024)), (2, (ACC, 792))):
                    if c == 2:
                        pe.wait_ge(S("roped"), 1)
                    for j in range(4):
                        tall(n + 4 * c + j, bank, act_hl, 2 * j, j == 0, j == 3, 2, cols)
                lows[0] += 4
                pe.wait_ge(S("roped"), 2)
                pe.wait_ge(S("dv"), 1)
                tk = tok2.rearrange("p (m h d) -> p m h d", m=2, h=8)
                for h in range(8):
                    for m in range(M):
                        ins = turn(ps[:, UP + h // 2, (h % 2) * T + m * P:(h % 2) * T + (m + 1) * P], tk[:, m, h, :])
                    if h % 2:
                        ins.then_inc(S("dqk_turned4"), 1)
                for h in range(4):
                    if h % 2 == 0:
                        pe.wait_ge(S("dqkT"), h // 2 + 1)
                    for m in range(M):
                        ins = turn(ps[:, UP + h // 2, (h % 2) * T + m * P:(h % 2) * T + (m + 1) * P],
                                   nqt[:, m, h * P:(h + 1) * P])
                    if h == 0:
                        ins.then_inc(S("dqk_turned"), 1)
                    elif h % 2:
                        ins.then_inc(S("nq_turned"), 1)
                pe.wait_ge(S("roped"), 3)
                pe.wait_ge(S("gate_e"), 1)
                kd = tok2.rearrange("p (m a n) -> p m a n", m=2, a=8)
                for q in range(8):
                    for m in range(M):
                        ins = turn(ps[:, ACC + q // 2, (q % 2) * T + m * P:(q % 2) * T + (m + 1) * P], kd[:, m, q, :])
                    if q % 2:
                        ins.then_inc(S("kd_turned"), 1)
                f2 = hl2[:, :, :].rearrange("p a b -> p (a b)")[:, 0:1920].rearrange("p (j n) -> p j n", j=32)
                pe.wait_ge(S("flat_lo"), 1)
                pe.wait_ge(S("dqkT"), 4)
                pe.wait_ge(S("nqT"), 2)
                for a_ in range(2):
                    for h in range(2):
                        wide(FIRST["cmp"] + 2 * a_ + h, UP + 2 * a_, 16 * a_ + 8 * h, f2, h == 0, h == 1, 8, 256)

                spans = ((0, 128), (128, 256))

                def causal_scores(bank, q, key):
                    for m, (c0, w) in enumerate(spans):
                        mm(ps[:, bank, c0:c0 + w], q[:, m * P:(m + 1) * P], key[:, 0:w], True, False)
                        ins = mm(ps[:, bank, c0 + w - P:c0 + w], ident, causal, False, True)
                    return ins

                def turn_probs(bank, p):
                    turn(ps[:, bank, 0:128], p[:, 0:128])
                    turn(ps[:, bank, 128:256], p[:, 128:256])
                    return turn(ps[:, bank, 256:384], p[:, 256:384])

                def scores_of(u):
                    if u == 0:
                        pe.wait_ge(S("kT2"), 4)
                    if u >= 2:
                        pe.wait_ge(S("att_exp"), u - 1)
                    for j in range(2):
                        if u < DH:
                            q, key = dqkT[64 * j:64 * j + 64, u, :], dqkT[64 * j:64 * j + 64, 4 + u, :]
                        else:
                            h = u - DH
                            r = 64 * (h % 2)
                            q, key = nqT[r:r + 64, h // 2, :], kT2[r:r + 64, 1 + j, h // 4, :]
                        ins = causal_scores(2 * (u % 2) + j, q, key)
                    ins.then_inc(S("att_scores"), 1)

                def turn_of(u):
                    pe.wait_ge(S("att_probs"), u + 1)
                    if u < DH:
                        if u >= 2:
                            pe.wait_ge(S("att_pT"), u - 1)
                        ins = turn_probs(4 + u % 2, p2[u % 2][:, 0, :])
                    else:
                        pe.wait_ge(S("att_pT"), u)
                        if u == DH:
                            pe.wait_ge(S("pcT"), 1)
                        for j in range(2):
                            ins = turn_probs(4 + j, p2[u % 2][:, j, :])
                    ins.then_inc(S("att_turned"), 1)

                def out_of(u):
                    pe.wait_ge(S("att_pT"), u + 1)
                    if u < DH:
                        if u == 0:
                            pe.wait_ge(S("cscores_read"), 1)
                        if u >= 2:
                            pe.wait_ge(S("od"), u - 1)
                        pt = pt2[u % 2][:, 0, :]
                        o = ps[:, 6 + u % 2, :]
                        mm(o[:, 0:128], pt[:, 0:128], dv[:, 0, u * P:(u + 1) * P], True, True)
                        mm(o[:, 128:256], pt[:, 128:256], dv[:, 0, u * P:(u + 1) * P], True, False)
                        ins = mm(o[:, 128:256], pt[:, 256:384], dv[:, 1, u * P:(u + 1) * P], False, True)
                    else:
                        h = u - DH
                        if h in (0, 2):
                            pe.wait_ge(S("od"), 3 + h // 2)
                        if h % 2 == 0 and h >= 4:
                            need_lows(lows[0] + h // 2 - 1)
                        r, g = 64 * (h % 2), h // 4
                        o = ps[r:r + 64, 6 + (h // 2) % 2, :]
                        mm(o[:, 0:T], vsel[:, h, :], pcT, True, False)
                        for j in range(2):
                            pt = pt2[h % 2][:, j, :]
                            mm(o[:, 0:T], vsw[:, 0, j, 64 * g:64 * g + 64], pt[:, 0:256], False, False)
                            ins = mm(o[:, P:T], vsw[:, 1, j, 64 * g:64 * g + 64], pt[:, 256:384], False, j == 1)
                    ins.then_inc(S("att_out"), 1)

                def compressed_kv():
                    pe.wait_ge(S("hidc"), 1)
                    pe.wait_ge(S("small"), 16 * 11)
                    for c in range(2):
                        mm(ps[:, UP + 2, 0:30], w2k[:, c, :, :].rearrange("p u d -> p (u d)"), hidc[:, 0, c, :],
                           c == 0, c == 1)
                    for c in range(2):
                        ins = mm(ps[:, UP + 3, 0:64], hidrep[:, c].rearrange("p h n -> p (h n)"), w2v[:, c, :],
                                 c == 0, c == 1)
                    ins.then_inc(S("cmp_kv"), 1)

                def compressed_scores():
                    pe.wait_ge(S("kcT"), 1)
                    pe.wait_ge(S("vsel"), 1)
                    for h in range(NH):
                        r, g = 64 * (h % 2), h // 4
                        for m in range(M):
                            c = (h // 2) * 32 + m * 16
                            ins = mm(ps[:, UP + 2 + h % 2, c:c + 15], nqT[r:r + 64, h // 2, m * P:(m + 1) * P],
                                     kcT[r:r + 64, 15 * g:15 * g + 15], True, True)
                    ins.then_inc(S("cscores"), 1)

                for t in range(DH + NH + 1):
                    if t < DH + NH:
                        scores_of(t)
                    if t == 0:
                        compressed_kv()
                    if t == 1:
                        compressed_scores()
                    if t == DH + NH:
                        pe.wait_ge(S("o_normed"), 1)
                        pe.wait_ge(S("att_exp"), t - 1)
                        for h in range(DH):
                            for m in range(M):
                                ins = turn(turned(ACC, h, 1)[:, 0, m * P:(m + 1) * P], od[:, 2 * h + m, :])
                            if h % 2:
                                ins.then_inc(S("turned"), 1)
                    if t >= 2:
                        out_of(t - 2)
                    if t >= 1:
                        turn_of(t - 1)
                    if t == DH:
                        pe.wait_ge(S("pcm"), 1)
                        for m in range(M):
                            ins = turn(ps[:, UP, m * P:(m + 1) * P], pcm[:, m].rearrange("p h n -> p (h n)"))
                        ins.then_inc(S("pcm_turned"), 1)
                need_lows(lows[0] + 5)
                tall(FIRST["w_out_2"], ACC, act_hl, 0, True, False, 2, 1024)
                out_of(DH + NH - 1)
                tall(FIRST["w_out_2"] + 1, ACC, act_hl, 2, False, False, 2, 1024)
                lows[0] += 6
                need_lows(lows[0])
                tall_by_tile(FIRST["w_out_2"] + 2, 2, act_hl, 4)
                turn_m(ACC, 0)

                f0 = FIRST["ffn"]

                def gate_up(n, i, per):
                    free = ("ff_sum", 2 * i + 1, 2 * i + 2)
                    for h in range(2):
                        wide(n + h, UP, 4 * h, act_hl, h == 0, h == 1, 4, 512, i, per,
                             read=free if h == 0 else None, out=h == 1)

                wide_by_tile(f0, ACC, out=True)
                gate_up(f0 + 2, 0, 0)
                pe.wait_ge(S("ff_lo"), 1)
                tall(f0 + 4, ACC, hl2, 0, True, False, 2, 1024)
                with pe.Fori(1, FF_BLOCKS - 1) as i:
                    gate_up(f0 + 2, i, 3)
                    pe.wait_ge(S("ff_lo"), i + 1)
                    tall(f0 + 4, ACC, hl2, 0, False, False, 2, 1024, i, 3)
                pe.wait_ge(S("ff_lo"), FF_BLOCKS)
                tall_by_tile(N_PIECES - 1, 1, hl2, 0)


def kernel(**inputs):
    import numpy as _np
    import concourse.bacc as _bacc
    from concourse import mybir as _mybir
    from concourse.bass_utils import run_bass_kernel_spmd as _run

    nc = _bacc.Bacc("TRN2", target_bir_lowering=False, num_devices=1)
    arrays = {name: _np.ascontiguousarray(v) for name, v in inputs.items()}
    arrays["shape_constants"] = shape_constants()
    aps = {name: nc.dram_tensor(f"in_{name}", v.shape, _mybir.dt.from_np(v.dtype), kind="ExternalInput").ap()
           for name, v in arrays.items()}
    result = nc.dram_tensor("result", (1, T, D), _mybir.dt.float32, kind="ExternalOutput").ap()
    two_blocks(nc, aps, result)
    r = _run(nc, [{f"in_{name}": v for name, v in arrays.items()}], core_ids=[0])
    return r.results[0]["result"]
```

```python
from contextlib import ExitStack

import numpy as np

import concourse.bass as bass
from concourse import mybir

F32 = mybir.dt.float32
F32R = mybir.dt.float32r
I32 = mybir.dt.int32
ALU = mybir.AluOpType
ACT = mybir.ActivationFunctionType
AX = mybir.AxisListType.X
ds = bass.ds

P = 128
T = 256
M = T // P
D = 1024
KD = D // P
EPS = 1e-6
NEG = -1e30

SCW = 512
QR, KVR, ROPE = 384, 256, 32
NOPE, VD, NH = 64, 64, 8
QKD = NOPE + ROPE
A_COLS = QR + KVR + ROPE
MLP_BLOCKS = 4096 // 512
TAPS = 31
CONV_PAD = TAPS // 2
POOL_TILE = 0
DVE_TILES = (1, 2, 3, 4)
EARLY_TAPS = 21
SHARED_TAPS = 10
PE_TAPS = [(4, t) for t in range(SHARED_TAPS)] + [(c, t) for c in (5, 6, 7) for t in range(31)]
DIAGS = 6

HD = 64
DH = 4
LAM_INIT = 0.8 - 0.6 * float(np.exp(-0.3 * 0))
FF = 2816
FF_BLOCKS = FF // 256

PIECE = 2048
RING = 4
FF_RING = 3

C_ID, C_CAUSAL = 0, 128
C_COS, C_SIN = 256, 384
C_CNEG, C_CONE = 512, 544
C_BLK, C_FREQ = 576, 584
C_END = 600

TWO_PI = (6.28125, 0.0019350051879882812, 2 * float(np.pi) - 6.28125 - 0.0019350051879882812)
ROUND = 1.5 * 2.0 ** 23


def shape_constants():
    c = np.zeros((P, C_END), np.float32)
    c[:, C_ID:C_ID + P] = np.eye(P)
    q = np.arange(P)
    c[:, C_CAUSAL:C_CAUSAL + P] = np.where(q[None, :] <= q[:, None], 0.0, NEG)
    inv = (1.0 / (np.float32(10000.0) ** (np.arange(0, HD, 2, dtype=np.float32) / np.float32(HD)))).astype(np.float32)
    for m in range(M):
        tok = np.arange(m * P, (m + 1) * P)
        ang = tok.astype(np.float32)[:, None] * inv[None, :]
        cos, sin = np.cos(ang), np.sin(ang)
        c[:, C_COS + 64 * m:C_COS + 64 * m + 64] = np.concatenate([cos, cos], 1)
        c[:, C_SIN + 64 * m:C_SIN + 64 * m + 64] = np.concatenate([-sin, sin], 1)
        seen = (np.arange(16) * 16 + 31)[None, :] <= tok[:, None]
        c[:, C_CNEG + 16 * m:C_CNEG + 16 * m + 16] = np.where(seen, 0.0, NEG)
        c[:, C_CONE + 16 * m:C_CONE + 16 * m + 16] = seen
    c[:, C_BLK:C_BLK + 8] = (q[:, None] // 16 == np.arange(8)[None, :])
    c[:, C_FREQ:C_FREQ + 16] = 1.0 / (np.float32(10000.0) ** (np.arange(16, dtype=np.float32) / np.float32(16)))
    return c


STAGES = [("w_in_gate", 2), ("w_in_tall", 3), ("w_in_conv", 4), ("w_uq", 2), ("w_ukv", 1), ("w_out", 4),
          ("mlp0", 4 * MLP_BLOCKS), ("pw1", 8), ("pw2", 4), ("mlp1", 4 * MLP_BLOCKS),
          ("w_in_2", 12), ("cmp", 4), ("w_out_2", 4), ("ffn", 3 * FF_BLOCKS)]
FIRST = {}
_n = 0
for _name, _count in STAGES:
    FIRST[_name] = _n
    _n += _count
W_IN_WIDE = (FIRST["w_in_gate"], FIRST["w_in_conv"], FIRST["w_in_conv"] + 2)
N_PIECES = _n
assert FIRST["ffn"] % RING == 0


class Steps:

    def __init__(self, eng, sem):
        self.eng, self.sem, self.count, self.turn, self.per = eng, sem, 0, None, 0

    def link(self, ins):
        self.count += 1
        ins.then_inc(self.sem, 1)
        self.eng.wait_ge(self.sem, self.count if self.turn is None else self.turn * self.per + self.count)

    def enter(self, turn, per):
        self.turn, self.per, self.at = turn, per, self.count

    def leave(self, turns):
        assert self.count - self.at == self.per, (self.count - self.at, self.per)
        self.count = self.at + turns * self.per
        self.turn = None


def two_blocks(nc, a, out):
    with ExitStack() as ctx:
        def sb(name, shape, dt=F32):
            return ctx.enter_context(nc.sbuf_tensor(name, shape, dt))

        sems = {}

        def S(name):
            if name not in sems:
                sems[name] = ctx.enter_context(nc.semaphore(name))
            return sems[name]

        raw = [sb(f"raw{i}", [P, PIECE]) for i in range(RING)]
        w_hi = [sb(f"w_hi{i}", [P, PIECE], F32R) for i in range(RING)]
        w_lo = [sb(f"w_lo{i}", [P, PIECE], F32R) for i in range(RING)]
        x = sb("x_res", [P, M, D])
        act_hl = sb("act_hl", [P, KD, 2 * T], F32R)
        hl2 = sb("hl2", [P, 5, 2 * T], F32R)
        nrm = sb("nrm", [P, M, D])
        gain = [sb(f"gain{i}", [P, D]) for i in range(4)]
        cst = sb("cst", [P, C_END])
        col = sb("col", [P, 3, P])
        bc = sb("bc", [P, 1024])
        ones = sb("ones", [1, P])
        st = sb("st", [P, 192])
        arena = sb("arena", [P, 10752])
        brow = arena[0:1, 9712:9712 + D]

        ident = cst[:, C_ID:C_ID + P]
        causal = cst[:, C_CAUSAL:C_CAUSAL + P]

        def AR(at, *dims, p=P, p0=0):
            n = int(np.prod(dims))
            v = arena[p0:p0 + p, at:at + n]
            if len(dims) == 2:
                return v.rearrange("p (a b) -> p a b", a=dims[0])
            if len(dims) == 3:
                return v.rearrange("p (a b c) -> p a b c", a=dims[0], b=dims[1])
            if len(dims) == 4:
                return v.rearrange("p (a b c d) -> p a b c d", a=dims[0], b=dims[1], c=dims[2])
            return v

        hb = AR(0, 4, T)
        htmp = AR(1024, 4, T)
        gsum, usum = AR(2048, 2, T), AR(2560, 2, T)
        esum = AR(3072, 2, T)
        gate_b, gate_c = AR(0, 4, T), AR(1024, 4, T)
        cx = AR(2048, 4, T + 2)
        ctmp = AR(3080, 4, T)
        qT, kT1 = nrm[:, :, :].rearrange("p m (h t) -> p (m h) t", h=4), AR(2048, NH, T)
        lat = AR(4104, M, QR + KVR)
        prob = [AR(at, M, T) for at in (4104, 4616, 1536)]
        probT = [AR(5128 + 512 * i, M, T) for i in range(2)]
        qf, kf = AR(6152, M, NH, QKD), AR(7688, M, NH, QKD)
        v1 = AR(9224, M, NH, VD)
        rows = AR(9224, 3, P)
        rt = AR(10248, NH, ROPE)
        rt2 = AR(10504, M, ROPE)
        UW = T + 2 * CONV_PAD
        upad = AR(0, 8, UW)
        cv = AR(2288, 8, T)
        ag = AR(4336, 4, T)
        ptmp = AR(5360, 4, T)
        diag = AR(6384, DIAGS, P)
        tap = AR(8944, T)
        zb = AR(0, 8, T)
        eb = AR(7152, 8, T)
        eg = AR(9200, 2, T)
        tok2 = AR(0, 2048)
        nqt = AR(2048, M, 8 * HD)
        p2 = [AR(768 * i, 2, 384) for i in range(2)]
        pt2 = [AR(1536 + 768 * i, 2, 384) for i in range(2)]
        dqkT = AR(3072, 8, T)
        nqT = AR(5120, 4, T)
        kT2 = AR(6144, 4, 2, T)
        dv = AR(8192, M, 512)
        vsw = AR(9216, M, 2, 128)
        od = AR(9728, 8, P)
        t1, t2 = nrm[:, 0, :], nrm[:, 1, :]
        flat = nrm[:, 0, 0:960].rearrange("p (a j n) -> p a j n", a=2, j=16)
        vsel = nrm[:, 1, 0:512].rearrange("p (h d) -> p h d", h=8)
        pcT = nrm[:, 1, 512:768]
        pcm = nrm[:, 1, 768:1024].rearrange("p (m h n) -> p m h n", m=2, h=8)
        pc = nrm[:, 0, 0:256].rearrange("p (a h m n) -> p a h m n", a=2, h=4, m=2)
        hidrep = nrm[:, 0, 256:512].rearrange("p (c h n) -> p c h n", c=2, h=8)
        hidc = nrm[:, 0, 512:572].rearrange("p (c n) -> p c n", c=2)
        hce = nrm[0:30, 1, 0:512].rearrange("p (a n) -> p a n", a=2)
        hid = nrm[0:30, 1, 512:1024].rearrange("p (a n) -> p a n", a=2)
        kcT = nrm[:, 0, 896:926]
        w2k = sb("w2k", [P, 2, 2, HD])
        w2v = sb("w2v", [P, 2, HD])
        gates = sb("gates", [P, M, 24])
        cs1 = sb("cs1", [P, 2, M, ROPE])
        posi = sb("posi", [P, M], I32)
        lamn = sb("lamn", [P, 1])

        ssh = st[:, 144:148]
        ssx = st[:, 148:150]
        rs_post, rs_pre = st[:, 150:152], st[:, 152:154]
        junk = AR(0, M, D)
        ss = st[:, 0:2]
        rstd = st[:, 2:4]
        mhalf = st[:, 4:12]
        ss4, rs4 = st[:, 12:16], st[:, 16:20]
        mv = st[:, 20:24].rearrange("p (m c) -> p m c", m=2)
        bns = st[:, 24:48].rearrange("p (m h c) -> p m h c", m=2, h=2)
        ss8, rs8 = st[:, 48:56], st[:, 56:64]
        nmx = [st[:, 72 + 4 * i:76 + 4 * i] for i in range(2)]
        rsum = [st[:, 80 + 4 * i:84 + 4 * i] for i in range(2)]
        rinv = [st[:, 88 + 4 * i:92 + 4 * i] for i in range(2)]
        cf = [st[:, 96 + 4 * i:100 + 4 * i] for i in range(2)]
        lam4 = st[:, 106:110]
        cmx = st[:, 112:128]
        crs = st[:, 128:144]

        VC = {}
        r = 0
        for name, n in (("b_pw1", 16), ("b_dw", 8), ("ln_g", 8), ("ln_b", 8), ("sc", 12), ("kpos", 16), ("vpos", 16)):
            VC[name] = r
            r += n
        VROWS = r
        DROWS = 4 * TAPS

        def vcol(name, i, n=1):
            return col[:, 0, VC[name] + i:VC[name] + i + n]

        def dwcol(t, c):
            r = t * 8 + c
            return col[:, 1 + r // DROWS, r % DROWS:r % DROWS + 1]

        ps = ctx.enter_context(nc.psum_tensor("ps", [P, 8, 512], F32))
        ACC, UP = 0, 4
        TURN_BANK = (ACC, ACC, ACC, ACC, UP, ACC)

        def tall_out(bank, m, width=1024):
            return ps[:, bank + 2 * m:bank + 2 * m + 2, :].rearrange("p b n -> p (b n)")[:, 0:width]

        def turned(bank, k0, n):
            v = ps[:, bank:bank + 4, :].rearrange("p b (h t) -> p (b h) t", h=2)
            return v[:, k0:k0 + n, :]

        def turned_tile(bank, m, j):
            return ps[:, bank + 2 * m + j, :].rearrange("p (k t) -> p k t", k=4)

        def view_k(w):
            return w.rearrange("(k p) n -> p k n", p=P)

        w_in = view_k(a["even_w_in"][0])
        w_uq, w_ukv = view_k(a["even_w_uq"][0]), view_k(a["even_w_ukv"][0])
        w_out = view_k(a["even_w_out"][0])
        pw1 = a["odd_w_pw1"][0].rearrange("(k p) (h n) -> p k h n", p=P, h=2)
        pw2 = view_k(a["odd_w_pw2"][0])
        mlp1 = [view_k(a["mlp_w1"][i]) for i in range(2)]
        mlp2 = [view_k(a["mlp_w2"][i]) for i in range(2)]
        w_in_2, w_out_2 = view_k(a["w_in_2"][0]), view_k(a["w_out_2"][0])
        cmp1 = [view_k(a["k_cmp_w1_2"][0]), view_k(a["v_cmp_w1_2"][0])]
        w_gate, w_up, w_down = view_k(a["w_gate_2"][0]), view_k(a["w_up_2"][0]), view_k(a["w_down_2"][0])

        piece = {}
        for b in range(3):
            for h in range(2):
                piece[W_IN_WIDE[b] + h] = (4, 512, [w_in[:, 4 * h:4 * h + 4, 512 * b:512 * b + 512]])
        TALL_K = [(0, 3), (3, 3), (6, 2)]
        for j, (k, n) in enumerate(TALL_K):
            piece[FIRST["w_in_tall"] + j] = (n, A_COLS, [w_in[:, k:k + n, 3 * SCW:3 * SCW + A_COLS]])
        UQ_K = [(0, 2), (2, 1)]
        for j, (k, n) in enumerate(UQ_K):
            piece[FIRST["w_uq"] + j] = (n, NH * QKD, [w_uq[:, k:k + n, :]])
        piece[FIRST["w_ukv"]] = (2, 1024, [w_ukv])
        for name, w in (("w_out", w_out), ("pw2", pw2), ("w_out_2", w_out_2)):
            for j in range(4):
                piece[FIRST[name] + j] = (2, 1024, [w[:, 2 * j:2 * j + 2, :]])
        for b in range(4):
            for h in range(2):
                piece[FIRST["pw1"] + 2 * b + h] = (4, 512, [
                    pw1[:, 4 * h:4 * h + 4, g, 256 * b:256 * b + 256] for g in range(2)])
        W2C = [(2048, 792), (0, 1024), (1024, 1024)]
        for c, (n0, n) in enumerate(W2C):
            for j in range(4):
                piece[FIRST["w_in_2"] + 4 * c + j] = (2, n, [w_in_2[:, 2 * j:2 * j + 2, n0:n0 + n]])
        for a_ in range(2):
            for h in range(2):
                piece[FIRST["cmp"] + 2 * a_ + h] = (8, 256, [cmp1[a_][:, 8 * h:8 * h + 8, :]])

        def slot_of(n):
            return n % RING if n < FIRST["ffn"] else (n - FIRST["ffn"]) % FF_RING

        def back(n):
            return RING if n < FIRST["ffn"] + FF_RING else FF_RING

        def width_of(n):
            return piece[n][0] * piece[n][1] if n in piece else PIECE

        def parts_of(n):
            if n in piece:
                return len(piece[n][2])
            if n < FIRST["ffn"]:
                return 1
            q = n - FIRST["ffn"]
            return 2 if q < 2 or (q < 2 + 3 * (FF_BLOCKS - 1) and (q - 2) % 3 < 2) else 1

        def landed_at(n):
            return 16 * sum(parts_of(q) for q in range(n + 1) if slot_of(q) == slot_of(n))

        def pv(tile, n):
            k, w = piece[n][0:2]
            return tile[slot_of(n)][:, 0:k * w].rearrange("p (k n) -> p k n", k=k)

        with nc.Block() as block:
            @block.sync
            def _(sp):
                def load(n):
                    k, w, srcs = piece[n]
                    if n >= back(n):
                        sp.wait_ge(S("w_split"), n - back(n) + 1)
                    dst = pv(raw, n)
                    for i, src in enumerate(srcs):
                        part = w // len(srcs)
                        sp.dma_start(dst[:, :, i * part:(i + 1) * part], src).then_inc(S(f"landed{slot_of(n)}"), 16)

                def load_gain(s, src):
                    if s >= 4:
                        sp.wait_ge(S("gain_used"), s - 3)
                    sp.dma_start(gain[s % 4][:, :], src.partition_broadcast(P)).then_inc(S(f"gain{s % 4}"), 16)

                gains = [a["sandwich_gains"][i, j, :] for i in range(2) for j in range(4)] + [
                    a["attn_pre_norm_2"][0, :], a["attn_post_norm_2"][0, :],
                    a["ffn_pre_norm_2"][0, :], a["ffn_post_norm_2"][0, :]]

                for m in range(M):
                    sp.dma_start(x[:, m, :], a["x"][0, m * P:(m + 1) * P, :]).then_inc(S(f"x_in{m}"), 16)
                for n in range(4):
                    load(n)

                def small(dst, src, sem="small"):
                    sp.dma_start(dst, src).then_inc(S(sem), 16)

                small(cst[:, P:C_END], a["shape_constants"][:, P:C_END])
                for name, src in (("b_pw1", a["odd_b_pw1"][0]), ("b_dw", a["odd_b_dw"][0]), ("ln_g", a["odd_ln_g"][0]),
                                  ("ln_b", a["odd_ln_b"][0])):
                    n = src.shape[0] // P
                    small(rows[VC[name]:VC[name] + n, 0, :], src.rearrange("(k p) -> k p", p=P), "rows_in")
                small(rows[VC["sc"]:VC["sc"] + 12, 0, :], a["even_sc_kernel"][0].rearrange("t (c p) -> (t c) p", p=P),
                      "rows_in")
                for name, src in (("kpos", a["k_cmp_pos_2"][0]), ("vpos", a["v_cmp_pos_2"][0])):
                    small(rows[VC[name]:VC[name] + 16, 0, :], src.rearrange("(j q) d -> j (q d)", q=2), "rows_in")
                dw = a["odd_w_dw"][0].rearrange("t (c p) -> (t c) p", p=P)
                for i in range(2):
                    small(rows[0:DROWS, 1 + i, :], dw[DROWS * i:DROWS * (i + 1), :], "rows_in")
                sp.dma_start(posi[:, :], a["positions"][0].rearrange("(m p) -> p m", p=P),
                              allow_slow_non_contiguous=True).then_inc(S("small"), 16)
                at = 0
                for src in (a["even_q_norm"][0], a["even_kv_norm"][0], a["diff_subln_2"][0], a["lambda_q1_2"][0],
                            a["lambda_k1_2"][0], a["lambda_q2_2"][0], a["lambda_k2_2"][0]):
                    n = src.shape[0]
                    small(bc[:, at:at + n], src.partition_broadcast(P))
                    at += n
                for u in range(2):
                    small(w2k[:, :, u, :], view_k(a["k_cmp_w2_2"][0]))
                small(w2v[:, :, :], view_k(a["v_cmp_w2_2"][0]))
                for s in range(1, 4):
                    load_gain(s, gains[s])
                for n in range(4, FIRST["mlp0"]):
                    load(n)
                load_gain(4, gains[4])

                def load_in_loop(n, i, per, src, cols=None):
                    slot = n % RING if per == 4 else (n - FIRST["ffn"]) % FF_RING
                    sp.wait_ge(S("w_split"), i * per + (n - (RING if per == 4 else FF_RING) + 1))
                    dst = raw[slot][:, :].rearrange("p (k n) -> p k n", k=src.shape[1])
                    if cols is not None:
                        dst = dst[:, :, cols[0]:cols[1]]
                    sp.dma_start(dst, src).then_inc(S(f"landed{slot}"), 16)

                def load_mlp(layer, n0):
                    def up(n, i, turn):
                        for h in range(2):
                            load_in_loop(n + h, turn, 4, mlp1[layer][:, 4 * h:4 * h + 4, ds(i * 512, 512)])

                    def down(n, i, turn):
                        for h in range(2):
                            load_in_loop(n + h, turn, 4, mlp2[layer][:, ds(i * 4 + 2 * h, 2), :])

                    up(n0, 0, 0)
                    with sp.Fori(1, MLP_BLOCKS) as i:
                        up(n0 + 2 - 4, i, i)
                        down(n0 + 4 - 4, i - 1, i)
                    down(n0 + 4 * MLP_BLOCKS - 2, MLP_BLOCKS - 1, 0)

                load_mlp(0, FIRST["mlp0"])
                sp.dma_start(brow, a["odd_b_pw2"]).then_inc(S("b_pw2"), 16)
                load_gain(5, gains[5])
                load_gain(6, gains[6])
                for n in range(FIRST["pw1"], FIRST["mlp1"]):
                    load(n)
                load_gain(7, gains[7])
                load_gain(8, gains[8])
                load_mlp(1, FIRST["mlp1"])
                load_gain(9, gains[9])
                load_gain(10, gains[10])
                for n in range(FIRST["w_in_2"], FIRST["ffn"]):
                    load(n)
                load_gain(11, gains[11])

                f0 = FIRST["ffn"]

                def gate_up(n, i, turn):
                    for h in range(2):
                        for g, w in enumerate((w_gate, w_up)):
                            load_in_loop(n + h, turn, 3, w[:, 4 * h:4 * h + 4, ds(i * 256, 256)], (256 * g, 256 * g + 256))

                gate_up(f0, 0, 0)
                with sp.Fori(1, FF_BLOCKS) as i:
                    gate_up(f0 - 1, i, i)
                    load_in_loop(f0 + 1, i, 3, w_down[:, ds((i - 1) * 2, 2), :])
                n = N_PIECES - 1
                sp.wait_ge(S("w_split"), n - FF_RING + 1)
                sp.dma_start(raw[slot_of(n)][:, :].rearrange("p (k n) -> p k n", k=2),
                             w_down[:, 2 * FF_BLOCKS - 2:2 * FF_BLOCKS, :]).then_inc(S(f"landed{slot_of(n)}"), 16)
                for m in range(M):
                    sp.wait_ge(S("x_new"), 2 * 5 + m + 1)
                    sp.dma_start(out[0, m * P:(m + 1) * P, :], x[:, m, :]).then_inc(S("stored"), 16)
                sp.wait_ge(S("stored"), 16 * M)

            @block.gpsimd
            def _(gp):
                me = Steps(gp, S("pool_step"))
                cursor = [0]

                def hi(n):
                    gp.wait_ge(S(f"landed{slot_of(n)}"), landed_at(n))
                    if n >= back(n):
                        gp.wait_ge(S("pe_piece"), n - back(n) + 1)
                    w = width_of(n)
                    gp.tensor_scalar(w_hi[slot_of(n)][:, 0:w], raw[slot_of(n)][:, 0:w], 1.0, 0.0,
                                     ALU.mult, ALU.add).then_inc(S("w_hi"), 1)

                def hi_until(n):
                    while cursor[0] <= min(n, N_PIECES - 1):
                        hi(cursor[0])
                        cursor[0] += 1

                def hi_in_loop(n, turn, per):
                    each = landed_at(n + per) - landed_at(n)
                    gp.wait_ge(S(f"landed{slot_of(n)}"), turn * each + landed_at(n))
                    gp.wait_ge(S("pe_piece"), turn * per + (n - back(n) + 1))
                    gp.sem_inc(S("pool_turn"), 1)
                    gp.tensor_scalar(w_hi[slot_of(n)][:, :], raw[slot_of(n)][:, :], 1.0, 0.0,
                                     ALU.mult, ALU.add).then_inc(S("w_hi"), 1)

                def rsqrt(dst, src, parts, sem):
                    for c0, c1, scale in parts:
                        me.link(gp.tensor_scalar(src[:, c0:c1], src[:, c0:c1], scale, EPS, ALU.mult, ALU.add))
                    n = parts[-1][1]
                    gp.tensor_tensor(dst[:, 0:n], src[:, 0:n], mhalf[:, 0:n], ALU.pow).then_inc(sem, 1)

                me.link(gp.memset(mhalf, -0.5))
                gp.memset(ones[:, :], 1.0).then_inc(S("ones"), 1)
                squares = [0]

                def post_rsqrt(m):
                    squares[0] += 2
                    gp.wait_ge(S("ssq"), squares[0])
                    h = ssh[:, 2 * m:2 * m + 1]
                    me.link(gp.tensor_scalar(h, h, ssh[:, 2 * m + 1:2 * m + 2], EPS, ALU.add, ALU.add))
                    gp.tensor_tensor(rs_post[:, m:m + 1], h, mhalf[:, 0:1], ALU.pow).then_inc(S("rstd"), 1)

                def pre_rsqrt(m):
                    squares[0] += 1
                    gp.wait_ge(S("ssq"), squares[0])
                    h = ssx[:, m:m + 1]
                    me.link(gp.tensor_scalar(h, h, EPS, None, ALU.add))
                    gp.tensor_tensor(rs_pre[:, m:m + 1], h, mhalf[:, 0:1], ALU.pow).then_inc(S("rstd"), 1)

                def boundary(last):
                    hi_until(last + 1)
                    post_rsqrt(0)
                    hi_until(last + 2)
                    pre_rsqrt(0)
                    hi_until(last + 3)
                    post_rsqrt(1)
                    hi_until(min(last + 4, FIRST["ffn"] + 2))
                    pre_rsqrt(1)

                pre_rsqrt(0)
                pre_rsqrt(1)
                hi_until(FIRST["w_in_conv"] + 2)
                gp.wait_ge(S("lat_ssq"), 4)
                rsqrt(rs4, ss4, [(0, 2, 1.0 / QR), (2, 4, 1.0 / KVR)], S("lat_rstd"))

                def mlp(n0):
                    hi_until(n0 + 3)
                    with gp.Fori(0, MLP_BLOCKS - 1) as i:
                        for j in range(4):
                            hi_in_loop(n0 + 4 + j, i, 4)
                    cursor[0] = n0 + 4 * MLP_BLOCKS
                    boundary(n0 + 4 * MLP_BLOCKS - 1)

                boundary(FIRST["mlp0"] - 1)
                mlp(FIRST["mlp0"])
                taps = [0]

                def convolve(n, c=POOL_TILE):
                    for t in range(taps[0], min(taps[0] + n, TAPS)):
                        src, w = upad[:, c, t:t + T], dwcol(t, c)
                        if t == 0:
                            gp.wait_ge(S("u"), POOL_TILE // 2 + 1)
                            me.link(gp.tensor_scalar(cv[:, POOL_TILE, :], src, w, vcol("b_dw", POOL_TILE),
                                                     ALU.mult, ALU.add))
                        else:
                            me.link(gp.tensor_scalar(tap, src, w, 0.0, ALU.mult, ALU.add))
                            me.link(gp.tensor_tensor(cv[:, c, :], cv[:, c, :], tap, ALU.add))
                    taps[0] = min(taps[0] + n, TAPS)

                hi_until(FIRST["pw1"] + 6)
                for n in range(FIRST["pw1"] + 7, FIRST["pw2"] + 4):
                    convolve(2)
                    hi_until(n)
                convolve(TAPS)
                gp.wait_ge(S("conv_early"), 1)
                taps[0] = EARLY_TAPS
                convolve(TAPS, DVE_TILES[0])
                gp.sem_inc(S("conv_pool"), 1)
                for m in range(M):
                    gp.wait_ge(S("ln_stats"), m + 1)
                    me.link(gp.tensor_scalar(ss[:, m:m + 1], mv[:, m, 1:2], EPS, None, ALU.add))
                    gp.tensor_tensor(rstd[:, m:m + 1], ss[:, m:m + 1], mhalf[:, 0:1], ALU.pow)\
                        .then_inc(S("ln_rstd"), 1)
                boundary(FIRST["mlp1"] - 1)
                mlp(FIRST["mlp1"])
                hi_until(FIRST["w_out_2"] + 3)
                gp.wait_ge(S("diff_ssq"), 1)
                rsqrt(rs8, ss8, [(0, 8, 1.0 / P)], S("diff_rstd"))
                f0 = FIRST["ffn"]
                boundary(f0 - 1)
                with gp.Fori(0, FF_BLOCKS - 2) as i:
                    for j in range(3):
                        q = f0 + 3 + j
                        base = landed_at(q)
                        each = 32 if (q - f0 - 2) % 3 < 2 else 16
                        gp.wait_ge(S(f"landed{slot_of(q)}"), i * each + base)
                        gp.wait_ge(S("pe_piece"), i * 3 + (q - FF_RING + 1))
                        gp.sem_inc(S("pool_turn"), 1)
                        gp.tensor_scalar(w_hi[slot_of(q)][:, :], raw[slot_of(q)][:, :], 1.0, 0.0,
                                         ALU.mult, ALU.add).then_inc(S("w_hi"), 1)
                cursor[0] = f0 + 3 * (FF_BLOCKS - 1)
                hi_until(N_PIECES)
                post_rsqrt(0)
                post_rsqrt(1)

            @block.vector
            def _(dve):
                me = Steps(dve, S("dve_step"))
                link = me.link
                tt, stt, tsc = dve.tensor_tensor, dve.scalar_tensor_tensor, dve.tensor_scalar
                cursor = [0]

                def lo(n, turn=0, per=0):
                    w = width_of(n)
                    dve.wait_ge(S("w_hi"), turn * per + n + 1)
                    tt(w_lo[slot_of(n)][:, 0:w], raw[slot_of(n)][:, 0:w],
                       w_hi[slot_of(n)][:, 0:w].bitcast(F32), ALU.subtract).then_inc(S("w_split"), 1)

                def lo_until(n):
                    while cursor[0] <= min(n, N_PIECES - 1):
                        lo(cursor[0])
                        cursor[0] += 1

                def lo_half(n, half):
                    assert cursor[0] == n
                    w = width_of(n) // 2
                    c = slice(half * w, (half + 1) * w)
                    dve.wait_ge(S("w_hi"), n + 1)
                    ins = tt(w_lo[slot_of(n)][:, c], raw[slot_of(n)][:, c], w_hi[slot_of(n)][:, c].bitcast(F32),
                             ALU.subtract)
                    if half == 0:
                        link(ins)
                    else:
                        ins.then_inc(S("w_split"), 1)
                        cursor[0] = n + 1

                def piece_done(n, turn=0, per=0):
                    dve.wait_ge(S("pe_piece"), turn * per + n + 1)

                def act_lo(src, k0, n, count, scale=1.0):
                    dve.wait_ge(S("act_hi"), count)
                    dst, high = act_hl[:, k0:k0 + n, T:2 * T], act_hl[:, k0:k0 + n, 0:T].bitcast(F32)
                    if scale == 1.0:
                        tt(dst, src, high, ALU.subtract).then_inc(S("act_lo"), 1)
                    else:
                        stt(dst, src, scale, high, ALU.mult, ALU.subtract).then_inc(S("act_lo"), 1)

                norms, rsts, outs, ssqs = [0], [0], [0], [0]
                his = [0]

                def next_rstd():
                    rsts[0] += 1
                    dve.wait_ge(S("rstd"), rsts[0])

                def post_gain(m, last):
                    g = norms[0]
                    y, gn = tall_out(ACC, m), gain[g % 4][:, :]
                    if m == 0:
                        dve.wait_ge(S("tile_out"), outs[0] + 1)
                        dve.wait_ge(S(f"gain{g % 4}"), 16 * (g // 4 + 1))
                        outs[0] += 1
                    else:
                        piece_done(last)
                    tt(nrm[:, m, 512:D], y[:, 512:D], gn[:, 512:D], ALU.mult).then_inc(S("gained"), 1)
                    dve.wait_ge(S("ssq"), ssqs[0] + 1)
                    ssqs[0] += 3
                    link(tt(nrm[:, m, 0:512], y[:, 0:512], gn[:, 0:512], ALU.mult))

                def post_add(m):
                    next_rstd()
                    stt(x[:, m, :], nrm[:, m, :], rs_post[:, m:m + 1], x[:, m, :], ALU.mult, ALU.add)\
                        .then_inc(S("x_new"), 1)

                def pre_tile(m, g):
                    next_rstd()
                    if m == 0:
                        dve.wait_ge(S(f"gain{g % 4}"), 16 * (g // 4 + 1))
                    stt(nrm[:, m, :], x[:, m, :], rs_pre[:, m:m + 1], gain[g % 4][:, :], ALU.mult, ALU.mult)\
                        .then_inc(S("normed"), 1)

                def low_tile(m, bank, halves=(0, 1)):
                    for j in halves:
                        his[0] += 1
                        dve.wait_ge(S("act_hi"), his[0])
                        k = slice(4 * j, 4 * j + 4)
                        tt(act_hl[:, k, T + m * P:T + (m + 1) * P], turned_tile(bank, m, j),
                           act_hl[:, k, m * P:(m + 1) * P].bitcast(F32), ALU.subtract).then_inc(S("act_lo"), 1)

                def boundary(s, last):
                    g = norms[0]
                    lo_until(last + 1)
                    post_gain(0, last)
                    post_add(0)
                    pre_tile(0, g + 1)
                    if s == 4:
                        lo_until(last + 2)
                    post_gain(1, last)
                    low_tile(0, TURN_BANK[s])
                    post_add(1)
                    if s == 4:
                        lo_until(last + 3)
                    pre_tile(1, g + 1)
                    if s == 4:
                        lo_until(last + 4)
                    else:
                        lo_half(last + 2, 0)
                    low_tile(1, TURN_BANK[s])
                    if s != 4:
                        lo_half(last + 2, 1)
                    norms[0] += 2
                    dve.sem_inc(S("gain_used"), 2)

                def rope(dst, src, cos, sin, ta, tb, half):
                    idx = (slice(None),) * (len(dst.shape) - 1)
                    first, second = idx + (slice(0, half),), idx + (slice(half, 2 * half),)
                    link(tt(ta, src, cos, ALU.mult))
                    link(tt(tb[first], src[second], sin[first], ALU.mult))
                    link(tt(tb[second], src[first], sin[second], ALU.mult))
                    return tt(dst, ta, tb, ALU.add)

                pre_tile(0, 0)
                pre_tile(1, 0)
                ssqs[0] = 2
                low_tile(0, ACC)
                lo_until(1)
                low_tile(1, ACC)
                norms[0] = 1
                dve.sem_inc(S("gain_used"), 1)
                dve.wait_ge(S("cols"), 1)
                link(dve.tensor_copy(col[:, 0, 0:VROWS], ps[:, ACC + 3, 0:VROWS]))
                tsc(col[:, 1:3, 0:DROWS], ps[:, ACC + 3, P:3 * P].rearrange("p (i r) -> p i r", i=2)[:, :, 0:DROWS],
                    0.5, None, ALU.mult).then_inc(S("cols_read"), 1)
                dve.wait_ge(S("cols_read"), 1)
                lo_until(3)
                dve.wait_ge(S("small"), 16 * 12)
                posf, ang = rt[:, 0, 0:2], rt[:, 1:2, 0:32].rearrange("p o (m f) -> p (o m) f", m=2)
                link(dve.tensor_copy(posf, posi[:, :]))
                for m in range(M):
                    link(tsc(ang[:, m, :], cst[:, C_FREQ:C_FREQ + 16], posf[:, m:m + 1], None, ALU.mult))
                for i, quarter in enumerate((0.25, 0.0)):
                    turns = rt[:, 2 + i:3 + i, 0:32].rearrange("p o (m f) -> p (o m) f", m=2)
                    red = rt[:, 4 + i:5 + i, 0:32].rearrange("p o (m f) -> p (o m) f", m=2)
                    link(tsc(turns, ang, 1.0 / (2 * float(np.pi)), quarter, ALU.mult, ALU.add))
                    link(tsc(turns, turns, ROUND, -ROUND, ALU.add, ALU.add))
                    link(stt(red, turns, -TWO_PI[0], ang, ALU.mult, ALU.add))
                    link(stt(red, turns, -TWO_PI[1], red, ALU.mult, ALU.add))
                    link(stt(red, turns, -TWO_PI[2], red, ALU.mult, ALU.add))
                    link(tsc(red, red, float(np.pi) / 2 if i == 0 else 0.0, 3.1415925, ALU.add, ALU.min))
                    tsc(red, red, -3.1415925, None, ALU.max).then_inc(S("angles"), 1)
                dve.wait_ge(S("sines"), 2)
                link(dve.tensor_copy(cs1[:, 0, :, 16:32], cs1[:, 0, :, 0:16]))
                link(tsc(cs1[:, 1, :, 0:16], cs1[:, 1, :, 16:32], -1.0, None, ALU.mult))
                link(stt(rt[:, 6:8, :].rearrange("p a b -> p (a b)"), bc[:, 768:832], 1.0, bc[:, 832:896],
                         ALU.mult, ALU.mult, accum_out=lam4[:, 0:1]))
                stt(rt[:, 6:8, :].rearrange("p a b -> p (a b)"), bc[:, 896:960], 1.0, bc[:, 960:1024],
                    ALU.mult, ALU.mult, accum_out=lam4[:, 1:2]).then_inc(S("lam_sums"), 1)
                dve.wait_ge(S("lam_exp"), 1)
                link(tt(lamn[:, :], lam4[:, 3:4], lam4[:, 2:3], ALU.subtract))
                link(tsc(lamn[:, :], lamn[:, :], -LAM_INIT, None, ALU.add))
                link(dve.memset(cx[:, :, 0:1], 0.0))
                link(dve.memset(cx[:, :, T + 1:T + 2], 0.0))

                def halves(bank):
                    return ps[:, bank:bank + 4, 0:T]

                def wide_sum(b, dst):
                    lo_until(W_IN_WIDE[b] + 4)
                    dve.wait_ge(S("half_copied"), b + 1)
                    return tt(dst, halves(UP), ctmp, ALU.add)

                wide_sum(0, gate_b).then_inc(S("wide_read"), 1)
                lo_until(FIRST["w_in_conv"] + 2)
                dve.wait_ge(S("lat_rstd"), 1)
                for m in range(M):
                    tall = tall_out(ACC, m)
                    stt(lat[:, m, 0:QR], tall[:, 0:QR], rs4[:, m:m + 1], bc[:, 0:QR], ALU.mult, ALU.mult)
                    stt(lat[:, m, QR:QR + KVR], tall[:, QR:QR + KVR], rs4[:, 2 + m:3 + m],
                        bc[:, QR:QR + KVR], ALU.mult, ALU.mult).then_inc(S("lat_normed"), 1)
                kr = ps[:, ACC:ACC + 4, :].rearrange("p (m b) n -> p m (b n)", m=2)[:, :, QR + KVR:A_COLS]
                link(rope(rt2, kr, cs1[:, 0], cs1[:, 1], rt[:, 0:2, :], rt[:, 2:4, :], ROPE // 2))
                for m in range(M):
                    ins = dve.tensor_copy(kf[:, m, :, NOPE:QKD], rt2[:, m, :].unsqueeze(1).to_broadcast([P, NH, ROPE]))
                ins.then_inc(S("kpe"), 1)
                wide_sum(1, gate_c).then_inc(S("wide_read"), 1)
                for i, (k, n) in enumerate(((0, 2), (2, 2), (4, 1))):
                    dve.wait_ge(S("lat_hi"), i + 1)
                    tt(hl2[:, k:k + n, T:2 * T], turned(ACC, k, n), hl2[:, k:k + n, 0:T].bitcast(F32),
                       ALU.subtract).then_inc(S("lat_lo"), 1)
                xs_sum = wide_sum(2, cx[:, :, 1:T + 1])
                link(xs_sum)
                dve.sem_inc(S("wide_read"), 1)
                link(tt(cx[:, :, 1:T + 1], cx[:, :, 1:T + 1], gate_c, ALU.mult))
                def rope_queries():
                    piece_done(FIRST["w_uq"] + 1)
                    for m in range(M):
                        src = tall_out(ACC, m, NH * QKD).rearrange("p (h d) -> p h d", h=NH)[:, :, NOPE:QKD]
                        cos, sin = (cs1[:, i, m, :].unsqueeze(1).to_broadcast([P, NH, ROPE]) for i in range(2))
                        ta = AR(4104, NH, ROPE)
                        tb = AR(4360, NH, ROPE)
                        dve.wait_ge(S("q_nope"), m + 1)
                        rope(qf[:, m, :, NOPE:QKD], src, cos, sin, ta, tb, ROPE // 2).then_inc(S("q_rope"), 1)
                        dve.wait_ge(S("q_rope"), m + 1)

                for t in range(3):
                    if t == 2:
                        lo_until(FIRST["w_ukv"])
                        rope_queries()
                    for c in range(4):
                        w = vcol("sc", 4 * t + c)
                        if t == 0:
                            ins = tsc(gate_c[:, c, :], cx[:, c, 0:T], w, None, ALU.mult)
                        else:
                            ins = stt(gate_c[:, c, :], cx[:, c, t:t + T], w, gate_c[:, c, :], ALU.mult, ALU.add)
                    link(ins)
                tt(gate_b, gate_b, gate_c, ALU.mult).then_inc(S("ya"), 1)
                for j in range(4):
                    dve.wait_ge(S("k_turned"), j + 1)
                    dve.tensor_copy(kT1[0:QKD, 2 * j:2 * j + 2, :],
                                    ps[0:QKD, UP + j, :].rearrange("p (h t) -> p h t", h=2)).then_inc(S("kT"), 1)
                for t in range(NH + 4):
                    if 1 <= t <= NH:
                        h = t - 1
                        b = h % 2
                        dve.wait_ge(S("probs_exp"), h + 1)
                        link(dve.reciprocal(rinv[b][:, 0:2], rsum[b][:, 0:2]))
                        for m in range(M):
                            tsc(prob[h % 3][:, m, :], prob[h % 3][:, m, :], rinv[b][:, m:m + 1], None, ALU.mult)\
                                .then_inc(S("probs"), 1)
                    if t < NH:
                        b = t % 2
                        dve.wait_ge(S("scores"), t + 1)
                        if t >= 2:
                            dve.wait_ge(S("probs_exp"), t - 1)
                        dve.tensor_reduce(nmx[b][:, 0:2], ps[:, b, :].rearrange("p (m t) -> p m t", m=2), AX, ALU.max,
                                          negate=True).then_inc(S("row_max"), 1)
                    if t == 0:
                        his[0] += 1
                        act_lo(gate_b, 0, 4, his[0])
                    if t < NH:
                        lo_half(FIRST["w_out"] + t // 2, t % 2)
                    if t >= 5 and t % 2 == 1:
                        h = t - 5
                        his[0] += 1
                        act_lo(ps[:, 4 + (h // 2) % 2, 0:T].unsqueeze(1), 4 + h // 2, 1, his[0])
                boundary(1, FIRST["mlp0"] - 1)

                def mlp(n0, s):
                    blocks = MLP_BLOCKS * s

                    def square(i):
                        for j in range(2):
                            dve.wait_ge(S("half_copied"), 3 + 2 * blocks + 2 * i + j + 1)
                            c = slice(2 * j, 2 * j + 2)
                            link(tt(htmp[:, c, :], ps[:, UP + 2 * j:UP + 2 * j + 2, 0:T], htmp[:, c, :], ALU.add))
                            stt(hb[:, c, :], htmp[:, c, :], 0.0, htmp[:, c, :], ALU.max, ALU.mult)\
                                .then_inc(S("hidden"), 1)

                    def hidden_lo(i, dst=hl2):
                        for j in range(2):
                            dve.wait_ge(S("hid_hi"), 2 * blocks + 2 * i + j + 1)
                            c = slice(2 * j, 2 * j + 2)
                            tt(dst[:, c, T:2 * T], hb[:, c, :], dst[:, c, 0:T].bitcast(F32), ALU.subtract)\
                                .then_inc(S("hid_lo"), 1)

                    lo_until(n0 + 3)
                    square(0)
                    hidden_lo(0)
                    with dve.Fori(0, MLP_BLOCKS - 2) as i:
                        me.enter(i, 2)
                        lo(n0 + 4, i, 4)
                        lo(n0 + 5, i, 4)
                        square(i + 1)
                        lo(n0 + 6, i, 4)
                        lo(n0 + 7, i, 4)
                        hidden_lo(i + 1)
                    me.leave(MLP_BLOCKS - 2)
                    cursor[0] = n0 + 4 * MLP_BLOCKS - 4
                    lo_until(n0 + 4 * MLP_BLOCKS - 3)
                    square(MLP_BLOCKS - 1)
                    hidden_lo(MLP_BLOCKS - 1, act_hl)
                    lo_until(n0 + 4 * MLP_BLOCKS - 1)
                    boundary(2 * s + 2, n0 + 4 * MLP_BLOCKS - 1)

                mlp(FIRST["mlp0"], 0)

                def convolve(c, t):
                    if t == 0:
                        return tsc(cv[:, c, :], upad[:, c, t:t + T], dwcol(t, c), vcol("b_dw", c), ALU.mult, ALU.add)
                    return stt(cv[:, c, :], upad[:, c, t:t + T], dwcol(t, c), cv[:, c, :], ALU.mult, ALU.add)

                early = [0]

                def ahead(n):
                    for t in range(early[0], early[0] + n):
                        link(convolve(DVE_TILES[0], t))
                    early[0] += n

                link(dve.memset(upad[:, :, 0:CONV_PAD], 0.0))
                link(dve.memset(upad[:, :, CONV_PAD + T:UW], 0.0))
                for b in range(4):
                    n = FIRST["pw1"] + 2 * b + 1
                    lo_until(n + 2)
                    if b:
                        ahead(4)
                    if b < 3:
                        lo_until(n + 3)
                    if 0 < b < 3:
                        ahead(3)
                    bank = (UP, ACC)[b % 2]
                    dve.wait_ge(S("pw_half"), b + 1)
                    for c in range(4):
                        bias = vcol("b_pw1", 2 * b + c if c < 2 else 8 + 2 * b + c - 2)
                        stt(ag[:, c, :], ps[:, bank + c, 0:T], bias, ptmp[:, c, :], ALU.add, ALU.add)\
                            .then_inc(S("ag"), 1)
                    dve.wait_ge(S("gate_tanh"), b + 1)
                    stt(upad[:, 2 * b:2 * b + 2, CONV_PAD:CONV_PAD + T], eg, 1.0, ag[:, 0:2, :], ALU.add, ALU.mult)\
                        .then_inc(S("u"), 1)
                    dve.wait_ge(S("u"), b + 1)
                ahead(EARLY_TAPS - early[0])
                dve.sem_inc(S("conv_early"), 1)
                for t in range(TAPS):
                    if t == SHARED_TAPS:
                        dve.wait_ge(S("conv_act"), 1)
                    for c in DVE_TILES[1:] if t >= SHARED_TAPS else DVE_TILES[1:-1]:
                        ins = convolve(c, t)
                    if t < TAPS - 1:
                        link(ins)
                ins.then_inc(S("conv_dve"), 1)
                for m in range(M):
                    dve.wait_ge(S("cv_turned"), m + 1)
                    for h in range(2):
                        ins = dve.bn_stats(bns[:, m, h, :], ps[:, ACC + 2 * m + h, :])
                    link(ins)
                    dve.bn_aggr(mv[:, m, :], bns[:, m, :, :]).then_inc(S("ln_stats"), 1)
                for m in range(M):
                    dve.wait_ge(S("ln_rstd"), m + 1)
                    tsc(nrm[:, m, :], tall_out(ACC, m), mv[:, m, 0:1], rstd[:, m:m + 1], ALU.subtract, ALU.mult)\
                        .then_inc(S("normed"), 1)
                lo_until(FIRST["pw2"] + 3)
                for j in range(5):
                    if j < 4:
                        dve.wait_ge(S("z_tanh"), j + 1)
                        c = slice(2 * j, 2 * j + 2)
                        stt(zb[:, c, :], eb[:, c, :], 1.0, zb[:, c, :], ALU.add, ALU.mult).then_inc(S("silu"), 1)
                    if j:
                        his[0] += 1
                        act_lo(zb[:, 2 * j - 2:2 * j, :], 2 * j - 2, 2, his[0], 0.5)
                boundary(3, FIRST["mlp1"] - 1)
                mlp(FIRST["mlp1"], 1)

                def tab(c, m, *shape):
                    v = cst[:, c + 64 * m:c + 64 * m + 64]
                    for _ in shape:
                        v = v.unsqueeze(1)
                    return v.to_broadcast([P, *shape, 64])

                n = FIRST["w_in_2"]
                lo_until(n + 6)
                piece_done(n + 3)
                kd = tok2.rearrange("p (m a g u d) -> p m a g u d", m=2, a=4, g=2, u=2)
                for m in range(M):
                    src = tall_out(ACC, m, 768).rearrange("p (a v g d) -> p a v g d", a=3, v=2, g=2)[:, :, 0]
                    ta, tb = (t[:, 0:384].rearrange("p (a g d) -> p a g d", a=3, g=2) for t in (t1, t2))
                    link(rope(kd[:, m, 0:3, :, 0, :], src, tab(C_COS, m, 3, 2), tab(C_SIN, m, 3, 2), ta, tb, HD // 2))
                    link(tt(kd[:, m, 0:3, :, 1, :], ta, tb, ALU.add))
                dve.sem_inc(S("roped"), 1)
                lo_until(n + 7)
                dve.wait_ge(S("gate_e"), 1)
                link(tsc(gates[:, :, :], gates[:, :, :], 1.0, 0.5, ALU.add, ALU.mult))
                lo_until(n + 10)
                for j in range(4):
                    dve.wait_ge(S("kd_turned"), j + 1)
                    dve.tensor_copy(kT2[:, j, :, :], ps[:, ACC + j, :].rearrange("p (g t) -> p g t", g=2))\
                        .then_inc(S("kT2"), 1)
                dve.wait_ge(S("kT2"), 4)
                for a_, kind in enumerate((0, 3)):
                    for par in range(2):
                        p0 = 64 * par
                        for g in range(2):
                            src = kT2[p0:p0 + 64, kind, g, :]
                            pos = vcol("kpos" if a_ == 0 else "vpos", 0, 16)[p0:p0 + 64, :]
                            win = src[:, 0:16 * 15].rearrange("p (n j q) -> p j n q", j=8, q=2)[:, :, :, par]
                            win2 = src[:, 16:256].rearrange("p (n j q) -> p j n q", j=8, q=2)[:, :, :, par]
                            for hh, wv in enumerate((win, win2)):
                                ins = tt(flat[p0:p0 + 64, a_, 8 * hh:8 * hh + 8, 15 * g:15 * g + 15], wv,
                                         pos[:, 8 * hh:8 * hh + 8].unsqueeze(2).to_broadcast([64, 8, 15]), ALU.add)
                link(ins)
                dve.sem_inc(S("flat"), 1)
                f2 = hl2[:, :, :].rearrange("p a b -> p (a b)")[:, 0:1920].rearrange("p (j n) -> p j n", j=32)
                dve.wait_ge(S("flat_hi"), 1)
                tt(f2[:, :, 30:60], flat.rearrange("p a j n -> p (a j) n"), f2[:, :, 0:30].bitcast(F32), ALU.subtract)\
                    .then_inc(S("flat_lo"), 1)

                def rope_heads(bank, m, h0, heads, dst):
                    src = tall_out(bank, m).rearrange("p (h d) -> p h d", d=HD)[:, h0:h0 + heads, :]
                    ta, tb = (t[:, 0:heads * HD].rearrange("p (h d) -> p h d", d=HD) for t in (t1, t2))
                    link(rope(dst, src, tab(C_COS, m, heads), tab(C_SIN, m, heads), ta, tb, HD // 2))

                lo_until(n + 11)
                dve.wait_ge(S("flat_lo"), 1)
                piece_done(n + 7)
                dqk = tok2.rearrange("p (m h d) -> p m h d", m=2, h=16)
                rope_heads(UP, 0, 0, 16, dqk[:, 0])
                rope_heads(UP, 1, 0, 16, dqk[:, 1])
                dve.sem_inc(S("roped"), 1)
                for m in range(M):
                    if m == 0:
                        dve.wait_ge(S("dv_nq_tile"), 1)
                    else:
                        lo_until(n + 13)
                        piece_done(n + 11)
                    rope_heads(ACC, m, 8, 8, nqt[:, m, :].rearrange("p (h d) -> p h d", d=HD))
                    dve.sem_inc(S("nq_roped"), 1)
                lo_until(FIRST["w_out_2"] - 1)

                for a_ in range(2):
                    dve.wait_ge(S("hc_tanh"), a_ + 1)
                    stt(hid[:, a_, :], hce[:, a_, :], 1.0, ps[0:30, ACC + 2 * a_, 0:256], ALU.add, ALU.mult)\
                        .then_inc(S("hid"), 1)
                link(dve.memset(hidrep, 0.0))
                dve.wait_ge(S("hid_turned"), 1)
                hT = ps[:, ACC + 3, 0:120].rearrange("p (a c n) -> p a c n", a=2, c=2)
                dve.tensor_copy(hidc, hT[:, 0])
                for c in range(2):
                    ins = dve.tensor_copy(
                        hidrep[:, c].rearrange("p (g r) n -> p g r n", g=2)[:, :, :, 0:15],
                        hT[:, 1, c, :].rearrange("p (g n) -> p g n", g=2).unsqueeze(2).to_broadcast([P, 2, 4, 15]))
                ins.then_inc(S("hidc"), 1)
                HEADS = DH + NH
                pcv = nrm[:, 0, 0:256].rearrange("p (r n) -> p r n", n=16)[:, :, 0:15]
                sq = AR(3072, 8, P)

                def row_max(u):
                    b = u % 2
                    dve.wait_ge(S("att_scores"), u + 1)
                    if u >= 2:
                        dve.wait_ge(S("att_exp"), u - 1)
                    dve.tensor_reduce(nmx[b][:, 0:2], ps[:, 2 * b:2 * b + 2, 0:128], AX, ALU.max, negate=True)
                    dve.tensor_reduce(nmx[b][:, 2:4], ps[:, 2 * b:2 * b + 2, 128:384], AX, ALU.max, negate=True)\
                        .then_inc(S("att_max"), 1)

                def weigh(u):
                    b = u % 2
                    dve.wait_ge(S("att_exp"), u + 1)
                    link(dve.reciprocal(rinv[b], rsum[b]))
                    if u < DH:
                        for m in range(M):
                            ins = tt(cf[b][:, m:m + 1], rinv[b][:, 2 * m + 1:2 * m + 2], lamn[:, :], ALU.mult)
                        link(ins)
                        for m, c in enumerate((slice(0, 128), slice(128, 384))):
                            ins = tsc(p2[b][:, 1, c], p2[b][:, 1, c], cf[b][:, m:m + 1], None, ALU.mult)
                        link(ins)
                        for m, c in enumerate((slice(0, 128), slice(128, 384))):
                            ins = stt(p2[b][:, 0, c], p2[b][:, 0, c], rinv[b][:, 2 * m:2 * m + 1], p2[b][:, 1, c],
                                      ALU.mult, ALU.add)
                    else:
                        h = u - DH
                        gt = gates[:, :, 3 * h + 1:3 * h + 3]
                        link(tt(cf[b].rearrange("p (m a) -> p m a", m=2), rinv[b].rearrange("p (m a) -> p m a", m=2),
                                gt, ALU.mult))
                        for m, c in enumerate((slice(0, 128), slice(128, 384))):
                            for a_ in range(2):
                                ins = tsc(p2[b][:, a_, c], p2[b][:, a_, c], cf[b][:, 2 * m + a_:2 * m + a_ + 1], None,
                                          ALU.mult)
                    ins.then_inc(S("att_probs"), 1)

                def compressed_kv():
                    dve.wait_ge(S("cmp_kv"), 1)
                    tsc(kcT, ps[:, UP + 2, 0:30], 0.5, None, ALU.mult).then_inc(S("kcT"), 1)
                    stt(vsel, ps[:, UP + 3, 0:64].unsqueeze(1).to_broadcast([P, 8, 64]), 0.5,
                        cst[:, C_BLK:C_BLK + 8].unsqueeze(2).to_broadcast([P, 8, 64]), ALU.mult, ALU.mult)\
                        .then_inc(S("vsel"), 1)

                def compressed_shift():
                    dve.wait_ge(S("cscores"), 1)
                    neg = cst[:, C_CNEG:C_CNEG + 32].rearrange("p (m n) -> p m n", m=2)[:, :, 0:15]
                    for par in range(2):
                        ins = tt(pc[:, par, :, :, 0:15],
                                 ps[:, UP + 2 + par, 0:128].rearrange("p (h m n) -> p h m n", h=4, m=2)[:, :, :, 0:15],
                                 neg.unsqueeze(1).to_broadcast([P, 4, 2, 15]), ALU.add)
                    ins.then_inc(S("cscores_read"), 1)
                    dve.wait_ge(S("cscores_read"), 1)
                    link(dve.tensor_reduce(cmx, pcv, AX, ALU.max))
                    tt(pcv, pcv, cmx.unsqueeze(2).to_broadcast([P, 16, 15]), ALU.subtract).then_inc(S("cshift"), 1)

                def compressed_weigh():
                    dve.wait_ge(S("cexp"), 1)
                    link(dve.tensor_reduce(crs, pcv, AX, ALU.add))
                    link(dve.reciprocal(crs, crs))
                    crv = crs.rearrange("p (a h m) -> p a h m", a=2, h=4)
                    gv = gates[:, :, :].rearrange("p m (h a b) -> p a h m b", a=2, b=3)
                    for par in range(2):
                        ins = tt(crv[:, par], crv[:, par], gv[:, par, :, :, 0], ALU.mult)
                    link(ins)
                    link(tt(pcv, pcv, crs.unsqueeze(2).to_broadcast([P, 16, 15]), ALU.mult))
                    link(dve.memset(pcm, 0.0))
                    pmv = pcm.rearrange("p m (h a) n -> p a h m n", a=2)
                    one = cst[:, C_CONE:C_CONE + 32].rearrange("p (m n) -> p m n", m=2)[:, :, 0:15]
                    for par in range(2):
                        ins = tt(pmv[:, par, :, :, 0:15], pc[:, par, :, :, 0:15],
                                 one.unsqueeze(1).to_broadcast([P, 4, 2, 15]), ALU.mult)
                    ins.then_inc(S("pcm"), 1)

                def diff_out(u):
                    dve.wait_ge(S("att_out"), u + 1)
                    dve.tensor_copy(od[:, 2 * u:2 * u + 2, :], ps[:, 6 + u % 2, 0:256].rearrange("p (m e) -> p m e", m=2))\
                        .then_inc(S("od"), 1)

                for t in range(HEADS + 2):
                    if t == DH + 1:
                        dve.wait_ge(S("pcm_turned"), 1)
                        dve.tensor_copy(pcT, ps[:, UP, 0:256]).then_inc(S("pcT"), 1)
                    if 1 <= t <= HEADS:
                        weigh(t - 1)
                    if t < HEADS:
                        row_max(t)
                    if t == 0:
                        compressed_kv()
                    if t == 1:
                        compressed_shift()
                    if t == 2:
                        compressed_weigh()
                    if 2 <= t < 2 + DH:
                        diff_out(t - 2)
                    if 1 <= t <= 8:
                        lo_half(FIRST["w_out_2"] + (t - 1) // 2, (t - 1) % 2)
                    if t == DH + 2:
                        dve.wait_ge(S("od"), DH)
                        link(tt(sq, od, od, ALU.mult))
                    if t == DH + 3:
                        dve.tensor_reduce(ss8, sq, AX, ALU.add).then_inc(S("diff_ssq"), 1)
                    if t == DH + 4:
                        dve.wait_ge(S("diff_rstd"), 1)
                        link(tt(od, od, rs8.unsqueeze(2).to_broadcast([P, 8, P]), ALU.mult))
                    if t == DH + 5:
                        stt(od, od, 1.0 - LAM_INIT, bc[:, 640:768].unsqueeze(1).to_broadcast([P, 8, P]),
                            ALU.mult, ALU.mult).then_inc(S("o_normed"), 1)
                    if t >= DH + 4 and t % 2 == 0 and t <= HEADS:
                        pair = (t - DH) // 2 - 2
                        his[0] += 1
                        act_lo(ps[:, 6 + pair % 2, 0:T].unsqueeze(1), 4 + pair, 1, his[0])
                for j in range(2):
                    his[0] += 1
                    act_lo(turned(ACC, 2 * j, 2), 2 * j, 2, his[0])
                his[0] += 1
                act_lo(ps[:, 7, 0:T].unsqueeze(1), 7, 1, his[0])
                boundary(5, FIRST["ffn"] - 1)

                f0 = FIRST["ffn"]

                def silu_gate(i):
                    for j in range(2):
                        dve.wait_ge(S("ff_half"), 2 * i + j + 1)
                        dst = (gsum, usum)[j]
                        tt(dst, ps[:, UP + 2 * j:UP + 2 * j + 2, 0:T], htmp[:, 2 * j:2 * j + 2, :], ALU.add)\
                            .then_inc(S("ff_sum"), 1)
                    dve.wait_ge(S("ff_tanh"), i + 1)
                    link(stt(gsum, esum, 1.0, gsum, ALU.add, ALU.mult))
                    tt(hb[:, 0:2, :], gsum, usum, ALU.mult).then_inc(S("ff_hidden"), 1)

                def ff_lo(i, dst=hl2):
                    dve.wait_ge(S("ff_hi"), i + 1)
                    stt(dst[:, 0:2, T:2 * T], hb[:, 0:2, :], 0.5, dst[:, 0:2, 0:T].bitcast(F32), ALU.mult, ALU.subtract)\
                        .then_inc(S("ff_lo"), 1)

                lo_until(f0 + 2)
                silu_gate(0)
                lo_until(f0 + 3)
                ff_lo(0)
                with dve.Fori(0, FF_BLOCKS - 2) as i:
                    me.enter(i, 1)
                    lo(f0 + 4, i, 3)
                    lo(f0 + 5, i, 3)
                    silu_gate(i + 1)
                    lo(f0 + 6, i, 3)
                    ff_lo(i + 1)
                me.leave(FF_BLOCKS - 2)
                cursor[0] = f0 + 4 + 3 * (FF_BLOCKS - 2)
                lo_until(N_PIECES - 2)
                silu_gate(FF_BLOCKS - 1)
                ff_lo(FF_BLOCKS - 1, act_hl)
                lo_until(N_PIECES)
                for m in range(M):
                    post_gain(m, N_PIECES - 1)
                    post_add(m)

            @block.scalar
            def _(act):
                me = Steps(act, S("act_step"))
                link = me.link
                f = act.activation

                def small(dst, src, sem="small"):
                    act.dma_start(dst, src).then_inc(S(sem), 16)

                small(gain[0][:, :], a["sandwich_gains"][0, 0, :].partition_broadcast(P), "gain0")
                small(cst[:, 0:P], a["shape_constants"][:, 0:P], "cst_in")
                his = [0]

                def piece_done(n, turn=0, per=0):
                    act.wait_ge(S("pe_piece"), turn * per + n + 1)

                def act_high(src, k0, n, scale=1.0):
                    f(act_hl[:, k0:k0 + n, 0:T], src, ACT.Copy, scale=scale).then_inc(S("act_hi"), 1)

                turns, gained, outs = [0], [0], [0]

                def square(m, src, total, at=0):
                    f(junk[:, m, at:at + src.shape[1]], src, ACT.Square, scale=1.0 / D ** 0.5, accum_out=total)\
                        .then_inc(S("ssq"), 1)

                def post_square(m, last, between=None):
                    if m == 0:
                        outs[0] += 1
                        act.wait_ge(S("tile_out"), outs[0])
                    else:
                        piece_done(last)
                    y = tall_out(ACC, m)
                    square(m, y[:, 0:512], ssh[:, 2 * m:2 * m + 1])
                    if between:
                        between()
                    gained[0] += 1
                    act.wait_ge(S("gained"), gained[0])
                    square(m, y[:, 512:D], ssh[:, 2 * m + 1:2 * m + 2], 512)

                def high_tile(m, bank, halves=(0, 1)):
                    for j in halves:
                        turns[0] += 1
                        act.wait_ge(S("turned"), turns[0])
                        f(act_hl[:, 4 * j:4 * j + 4, m * P:(m + 1) * P], turned_tile(bank, m, j), ACT.Copy)\
                            .then_inc(S("act_hi"), 1)

                def boundary(s, last):
                    post_square(0, last)
                    act.wait_ge(S("x_new"), 2 * (s - 1) + 1)
                    square(0, x[:, 0, :], ssx[:, 0:1])
                    post_square(1, last, lambda: high_tile(0, TURN_BANK[s], (0,)))
                    high_tile(0, TURN_BANK[s], (1,))
                    act.wait_ge(S("x_new"), 2 * (s - 1) + 2)
                    square(1, x[:, 1, :], ssx[:, 1:2])
                    high_tile(1, TURN_BANK[s])

                def high_of_turned(bank, pairs):
                    for j in range(pairs):
                        turns[0] += 1
                        act.wait_ge(S("turned"), turns[0])
                        act_high(turned(bank, 2 * j, 2), 2 * j, 2)

                for m in range(M):
                    act.wait_ge(S(f"x_in{m}"), 16)
                    square(m, x[:, m, :], ssx[:, m:m + 1])
                for m in range(M):
                    high_tile(m, ACC)
                for i in range(2):
                    act.wait_ge(S("angles"), i + 1)
                    red = rt[:, 4 + i:5 + i, 0:32].rearrange("p o (m f) -> p (o m) f", m=2)
                    f(cs1[:, i, :, 16 * i:16 * i + 16], red, ACT.Sin).then_inc(S("sines"), 1)
                act.wait_ge(S("lam_sums"), 1)
                act.wait_ge(S("dve_step"), 1)
                f(lam4[:, 2:4], lam4[:, 0:2], ACT.Exp).then_inc(S("lam_exp"), 1)

                def wide_half(b):
                    piece_done(W_IN_WIDE[b] + 1)
                    if b:
                        act.wait_ge(S("wide_read"), b)
                    f(ctmp, ps[:, UP:UP + 4, T:2 * T], ACT.Copy).then_inc(S("half_copied"), 1)

                wide_half(0)
                piece_done(FIRST["w_in_conv"] - 1)
                for c0, c1, i in ((0, QR, 0), (QR, QR + KVR, 2)):
                    for m in range(M):
                        f(lat[:, m, c0:c1], tall_out(ACC, m)[:, c0:c1], ACT.Square, accum_out=ss4[:, i + m:i + m + 1])\
                            .then_inc(S("lat_ssq"), 1)
                wide_half(1)
                for i, (k, n) in enumerate(((0, 2), (2, 2), (4, 1))):
                    act.wait_ge(S("lat_turned"), i + 1)
                    f(hl2[:, k:k + n, 0:T], turned(ACC, k, n), ACT.Copy).then_inc(S("lat_hi"), 1)
                wide_half(2)
                piece_done(FIRST["w_uq"] + 1)
                for m in range(M):
                    src = tall_out(ACC, m, NH * QKD).rearrange("p (h d) -> p h d", h=NH)[:, :, 0:NOPE]
                    f(qf[:, m, :, 0:NOPE], src, ACT.Copy).then_inc(S("q_nope"), 1)
                piece_done(FIRST["w_ukv"])
                for m in range(M):
                    src = tall_out(UP, m).rearrange("p (h d) -> p h d", h=NH)
                    f(kf[:, m, :, 0:NOPE], src[:, :, 0:NOPE], ACT.Copy)
                    f(v1[:, m, :, :], src[:, :, NOPE:NOPE + VD], ACT.Copy).then_inc(S("kv_nope"), 1)
                for j in range(4):
                    act.wait_ge(S("q_turned"), j + 1)
                    f(qT[0:QKD, 2 * j:2 * j + 2, :], ps[0:QKD, ACC + j, :].rearrange("p (h t) -> p h t", h=2),
                      ACT.Copy, scale=float(QKD) ** -0.5).then_inc(S("qT"), 1)

                def pair_out(h, sem, bank, k0):
                    act.wait_ge(S(sem), h + 1)
                    act_high(ps[:, bank, 0:T].unsqueeze(1), k0, 1)

                act.wait_ge(S("ya"), 1)
                act_high(gate_b, 0, 4)

                def prob_turned(h):
                    act.wait_ge(S("probs_turned"), h + 1)
                    if h >= 2:
                        act.wait_ge(S("pv"), h - 1)
                    f(probT[h % 2], ps[:, 2 + h % 2, :].rearrange("p (k t) -> p k t", k=2), ACT.Copy)\
                        .then_inc(S("probT"), 1)

                for h in range(NH):
                    b = h % 2
                    act.wait_ge(S("row_max"), h + 1)
                    if h >= 3:
                        act.wait_ge(S("probs_turned"), h - 2)
                    for m in range(M):
                        ins = f(prob[h % 3][:, m, :], ps[:, b, m * T:(m + 1) * T], ACT.Exp, bias=nmx[b][:, m:m + 1],
                                accum_out=rsum[b][:, m:m + 1])
                    ins.then_inc(S("probs_exp"), 1)
                    if h >= 2:
                        prob_turned(h - 2)
                    if h % 2 == 1 and h >= 5:
                        pair_out(h - 4, "pv", 4 + (h // 2 - 2) % 2, 4 + h // 2 - 2)
                prob_turned(NH - 2)
                prob_turned(NH - 1)
                pair_out(5, "pv", 4, 6)
                pair_out(7, "pv", 5, 7)
                boundary(1, FIRST["mlp0"] - 1)

                def mlp(n0, s):
                    blocks = MLP_BLOCKS * s

                    def half_copy(i, turn):
                        for j in range(2):
                            if j == 0:
                                act.wait_ge(S("front_out"), blocks + i + 1)
                            else:
                                piece_done(n0 + 1 if turn is None else n0 + 3, 0 if turn is None else turn, 4)
                            if turn is not None:
                                act.wait_ge(S("hidden"), 2 * blocks + 2 * i - 1 + j)
                            f(htmp[:, 2 * j:2 * j + 2, :], ps[:, UP + 2 * j:UP + 2 * j + 2, T:2 * T], ACT.Copy)\
                                .then_inc(S("half_copied"), 1)

                    def hidden_hi(i, turn, dst=hl2):
                        for j in range(2):
                            if turn is not None:
                                piece_done(n0 + 4 + j, turn, 4)
                            act.wait_ge(S("hidden"), 2 * blocks + 2 * i + j + 1)
                            f(dst[:, 2 * j:2 * j + 2, 0:T], hb[:, 2 * j:2 * j + 2, :], ACT.Copy).then_inc(S("hid_hi"), 1)

                    half_copy(0, None)
                    hidden_hi(0, None)
                    with act.Fori(0, MLP_BLOCKS - 2) as i:
                        half_copy(i + 1, i)
                        hidden_hi(i + 1, i)
                    half_copy(MLP_BLOCKS - 1, MLP_BLOCKS - 2)
                    hidden_hi(MLP_BLOCKS - 1, None, act_hl)
                    boundary(2 * s + 2, n0 + 4 * MLP_BLOCKS - 1)

                mlp(FIRST["mlp0"], 0)

                def diagonal(i):
                    if i >= DIAGS:
                        act.wait_ge(S("diag_used"), i - DIAGS + 1)
                    f(diag[:, i % DIAGS, :], ident, ACT.Copy, scale=dwcol(PE_TAPS[i][1], PE_TAPS[i][0]))\
                        .then_inc(S("diag"), 1)

                for b in range(4):
                    if b == 3:
                        for i in range(DIAGS):
                            diagonal(i)
                    piece_done(FIRST["pw1"] + 2 * b + 1)
                    if b:
                        act.wait_ge(S("ag"), 4 * b)
                    bank = (UP, ACC)[b % 2]
                    f(ptmp, ps[:, bank:bank + 4, T:2 * T], ACT.Copy).then_inc(S("pw_half"), 1)
                    if b == 3:
                        for i in range(DIAGS, 2 * DIAGS):
                            diagonal(i)
                    act.wait_ge(S("ag"), 4 * b + 4)
                    if b:
                        act.wait_ge(S("u"), b)
                    f(eg, ag[:, 2:4, :], ACT.Tanh, scale=0.5).then_inc(S("gate_tanh"), 1)
                built = 2 * DIAGS
                for q, c in enumerate((4, 5, 6, 7)):
                    used = SHARED_TAPS + q * TAPS
                    for i in range(built, min(used + DIAGS, len(PE_TAPS))):
                        diagonal(i)
                    built = max(built, used + DIAGS)
                    act.wait_ge(S("diag_used"), used)
                    f(cv[:, c, :], ps[:, UP + q, 0:T], ACT.Identity, bias=vcol("b_dw", c)).then_inc(S("conv_act"), 1)

                def silu_high(j):
                    act.wait_ge(S("silu"), j + 1)
                    act_high(zb[:, 2 * j:2 * j + 2, :], 2 * j, 2, 0.5)

                for k in range(KD):
                    act.wait_ge(S("turned"), turns[0] + k // 2 + 1)
                    f(zb[:, k, :], turned(UP, k, 1)[:, 0, :], ACT.Identity, bias=vcol("ln_b", k), scale=vcol("ln_g", k))\
                        .then_inc(S("z"), 1)
                    if k % 2:
                        act.wait_ge(S("z"), k + 1)
                        f(eb[:, k - 1:k + 1, :], zb[:, k - 1:k + 1, :], ACT.Tanh, scale=0.5).then_inc(S("z_tanh"), 1)
                        if k > 1:
                            silu_high(k // 2 - 1)
                silu_high(3)
                turns[0] += 4
                boundary(3, FIRST["mlp1"] - 1)
                mlp(FIRST["mlp1"], 1)

                n = FIRST["w_in_2"]
                act.wait_ge(S("roped"), 1)
                for m in range(M):
                    src = tall_out(ACC, m)[:, 0:792]
                    f(vsw[:, m, :, :], src[:, 256:768].rearrange("p (a v n) -> p a v n", a=2, v=2)[:, :, 1, :], ACT.Copy)
                    f(gates[:, m, :], src[:, 768:792], ACT.Tanh, scale=0.5)
                    kd = tok2.rearrange("p (m a g u d) -> p m a g u d", m=2, a=4, g=2, u=2)
                    for u in range(2):
                        ins = f(kd[:, m, 3, :, u, :], src[:, 128:256].rearrange("p (g d) -> p g d", g=2), ACT.Copy)
                ins.then_inc(S("gate_e"), 1)
                f2 = hl2[:, :, :].rearrange("p a b -> p (a b)")[:, 0:1920].rearrange("p (j n) -> p j n", j=32)
                act.wait_ge(S("flat"), 1)
                f(f2[:, :, 0:30], flat.rearrange("p a j n -> p (a j) n"), ACT.Copy).then_inc(S("flat_hi"), 1)
                for m in range(M):
                    if m == 0:
                        act.wait_ge(S("dv_nq_tile"), 1)
                    else:
                        piece_done(n + 11)
                    f(dv[:, m, :], tall_out(ACC, m)[:, 0:512], ACT.Copy).then_inc(S("dv"), 1)
                act.wait_ge(S("nq_roped"), 2)
                for a_ in range(2):
                    piece_done(FIRST["cmp"] + 2 * a_ + 1)
                    f(hce[:, a_, :], ps[0:30, ACC + 2 * a_, 0:256], ACT.Tanh, scale=0.5).then_inc(S("hc_tanh"), 1)
                for j in range(4):
                    act.wait_ge(S("dqk_turned"), j + 1)
                    f(dqkT[:, 2 * j:2 * j + 2, :], ps[:, UP + j, :].rearrange("p (h t) -> p h t", h=2), ACT.Copy,
                      scale=HD ** -0.5 if j < 2 else 1.0).then_inc(S("dqkT"), 1)
                for j in range(2):
                    act.wait_ge(S("nq_turned"), j + 1)
                    f(nqT[:, 2 * j:2 * j + 2, :], ps[:, UP + j, :].rearrange("p (h t) -> p h t", h=2), ACT.Copy,
                      scale=HD ** -0.5).then_inc(S("nqT"), 1)

                HEADS = DH + NH

                def exponentials(u):
                    b = u % 2
                    act.wait_ge(S("att_max"), u + 1)
                    if u >= 2:
                        act.wait_ge(S("att_turned"), u - 1)
                    for m, c in enumerate((slice(0, 128), slice(128, 384))):
                        for j in range(2):
                            k = 2 * m + j
                            ins = f(p2[b][:, j, c], ps[:, 2 * b + j, c], ACT.Exp, bias=nmx[b][:, k:k + 1],
                                    accum_out=rsum[b][:, k:k + 1])
                    ins.then_inc(S("att_exp"), 1)

                def probs_turned(u):
                    act.wait_ge(S("att_turned"), u + 1)
                    if u >= 2:
                        act.wait_ge(S("att_out"), u - 1)
                    if u < DH:
                        f(pt2[u % 2][:, 0, :], ps[:, 4 + u % 2, 0:384], ACT.Copy).then_inc(S("att_pT"), 1)
                    else:
                        f(pt2[u % 2], ps[:, 4:6, 0:384], ACT.Copy).then_inc(S("att_pT"), 1)

                for t in range(HEADS + 1):
                    if t < HEADS:
                        exponentials(t)
                    if t == 1:
                        act.wait_ge(S("cshift"), 1)
                        pcv = nrm[:, 0, 0:256].rearrange("p (r n) -> p r n", n=16)[:, :, 0:15]
                        f(pcv, pcv, ACT.Exp).then_inc(S("cexp"), 1)
                    if 1 <= t < HEADS:
                        probs_turned(t - 1)
                    if t >= DH + 4 and t % 2 == 0:
                        pair = (t - DH) // 2 - 2
                        pair_out(DH + 2 * pair + 1, "att_out", 6 + pair % 2, 4 + pair)
                high_of_turned(ACC, 2)
                probs_turned(HEADS - 1)
                pair_out(HEADS - 1, "att_out", 7, 7)
                boundary(5, FIRST["ffn"] - 1)
                f0 = FIRST["ffn"]

                def gate_half(i, turn):
                    for j in range(2):
                        if j == 0:
                            act.wait_ge(S("front_out"), 2 * MLP_BLOCKS + i + 1)
                        else:
                            piece_done(f0 + 1 if turn is None else f0 + 3, 0 if turn is None else turn, 3)
                        if turn is not None:
                            act.wait_ge(S("ff_sum"), 2 * i - 1 + j)
                        f(htmp[:, 2 * j:2 * j + 2, :], ps[:, UP + 2 * j:UP + 2 * j + 2, T:2 * T], ACT.Copy)\
                            .then_inc(S("ff_half"), 1)
                    act.wait_ge(S("ff_sum"), 2 * i + 1)
                    if turn is not None:
                        act.wait_ge(S("ff_hidden"), i)
                    f(esum, gsum, ACT.Tanh, scale=0.5).then_inc(S("ff_tanh"), 1)

                def ff_hi(i, dst=hl2):
                    act.wait_ge(S("ff_hidden"), i + 1)
                    f(dst[:, 0:2, 0:T], hb[:, 0:2, :], ACT.Copy, scale=0.5).then_inc(S("ff_hi"), 1)

                gate_half(0, None)
                ff_hi(0)
                with act.Fori(0, FF_BLOCKS - 2) as i:
                    gate_half(i + 1, i)
                    piece_done(f0 + 4, i, 3)
                    ff_hi(i + 1)
                gate_half(FF_BLOCKS - 1, FF_BLOCKS - 2)
                ff_hi(FF_BLOCKS - 1, act_hl)
                post_square(0, N_PIECES - 1)
                post_square(1, N_PIECES - 1)

            @block.tensor
            def _(pe):
                def mm(o, l, r, start, stop):
                    return pe.matmul(o, l, r, start=start, stop=stop, skip_group_check=True)

                def turn(o, src):
                    return pe.transpose(o, src, ident[0:src.shape[0], 0:src.shape[0]])

                def arrived(n, turn_=0, per=0):
                    pe.wait_ge(S("w_split"), turn_ * per + n + 1)

                def pv_hl(tile, n):
                    return tile[slot_of(n)][:, :].rearrange("p (k n) -> p k n", k=4)

                def piece_of(tile, n):
                    return tile[slot_of(n)][:, :].rearrange("p (k n) -> p k n", k=8)

                def wide(n, bank, lhs_k0, moving, first, last, k, cols, turn_=0, per=0, read=None, out=False):
                    arrived(n, turn_, per)
                    wh = w_hi[slot_of(n)][:, 0:k * cols].rearrange("p (k n) -> p k n", k=k)
                    wl = w_lo[slot_of(n)][:, 0:k * cols].rearrange("p (k n) -> p k n", k=k)
                    width = moving.shape[2]
                    for c in range(cols // P):
                        if read and c % 2 == 0:
                            pe.wait_ge(S(read[0]), read[1 + c // 2])
                        for kk in range(k):
                            act_k = moving[:, lhs_k0 + kk, :]
                            s = slice(c * P, (c + 1) * P)
                            mm(ps[:, bank + c, 0:width], wh[:, kk, s], act_k, first and kk == 0, False)
                            ins = mm(ps[:, bank + c, 0:width // 2], wl[:, kk, s], act_k[:, 0:width // 2],
                                     False, last and kk == k - 1)
                        if out and c == 1:
                            ins.then_inc(S("front_out"), 1)
                    ins.then_inc(S("pe_piece"), 1)

                def tall(n, bank, lhs, lhs_k0, first, last, k, cols, turn_=0, per=0, tiles=range(M), free=True):
                    arrived(n, turn_, per)
                    wh = w_hi[slot_of(n)][:, 0:k * cols].rearrange("p (k n) -> p k n", k=k)
                    wl = w_lo[slot_of(n)][:, 0:k * cols].rearrange("p (k n) -> p k n", k=k)
                    for kk in range(k):
                        for m in tiles:
                            h = lhs[:, lhs_k0 + kk, m * P:(m + 1) * P]
                            l = lhs[:, lhs_k0 + kk, T + m * P:T + (m + 1) * P]
                            for part, (lt, w) in enumerate(((h, wh), (h, wl), (l, wh))):
                                for j, c0 in enumerate(range(0, cols, 512)):
                                    c1 = min(cols, c0 + 512)
                                    ins = mm(ps[:, bank + 2 * m + j, 0:c1 - c0], lt, w[:, kk, c0:c1],
                                             first and kk == 0 and part == 0, last and kk == k - 1 and part == 2)
                    if free:
                        ins.then_inc(S("pe_piece"), 1)
                    return ins

                def tall_by_tile(n, lhs, first=False, waits=None):
                    for m in range(M):
                        for j, (src, k0) in enumerate(lhs):
                            if waits and m == 0 and waits[j]:
                                pe.wait_ge(S(waits[j][0]), waits[j][1])
                            ins = tall(n + j, ACC, src, k0, first and j == 0, j == len(lhs) - 1, 2, 1024,
                                       tiles=(m,), free=m == 1)
                        if m == 0:
                            ins.then_inc(S("tile_out"), 1)

                normed, lows = [0], [0]

                def turn_m(bank, m):
                    normed[0] += 1
                    pe.wait_ge(S("normed"), normed[0])
                    for k in range(KD):
                        ins = turn(turned_tile(bank, m, k // 4)[:, k % 4, :], nrm[:, m, k * P:(k + 1) * P])
                        if k % 4 == 3:
                            ins.then_inc(S("turned"), 1)

                def wide_by_tile(n, turn_bank, between=None, out=False):
                    def by_tile(v, m):
                        return v.rearrange("p (a t) -> p a t", a=2)[:, :, m * P:(m + 1) * P]

                    for m in range(M):
                        if m == 1:
                            turn_m(turn_bank, 1)
                        for h in range(2):
                            need_lows(lows[0] + 2 * m + h + 1)
                            pe.wait_ge(S("w_hi"), n + h + 1)
                            wh = pv_hl(w_hi, n + h)
                            for kk in range(4):
                                for c in range(4):
                                    ins = mm(by_tile(ps[:, UP + c, :], m), wh[:, kk, c * P:(c + 1) * P],
                                             by_tile(act_hl[:, 4 * h + kk, :], m), m == 0 and h == 0 and kk == 0, False)
                    if between:
                        between()
                    arrived(n + 1)
                    for c in range(4):
                        for h in range(2):
                            wl = pv_hl(w_lo, n + h)
                            for kk in range(4):
                                ins = mm(ps[:, UP + c, 0:T], wl[:, kk, c * P:(c + 1) * P],
                                         act_hl[:, 4 * h + kk, 0:T], False, h == 1 and kk == 3)
                            if c == 3:
                                ins.then_inc(S("pe_piece"), 1)
                        if out and c == 1:
                            ins.then_inc(S("front_out"), 1)

                def turn_normed(bank=ACC):
                    for k in range(KD):
                        for m in range(M):
                            pe.wait_ge(S("normed"), normed[0] + m + 1)
                            ins = turn(turned(bank, k, 1)[:, 0, m * P:(m + 1) * P], nrm[:, m, k * P:(k + 1) * P])
                        if k % 2:
                            ins.then_inc(S("turned"), 1)
                    normed[0] += 2

                def need_lows(n):
                    pe.wait_ge(S("act_lo"), n)

                pe.wait_ge(S("cst_in"), 16)
                turn_m(ACC, 0)

                def turn_rows():
                    pe.wait_ge(S("rows_in"), 16 * 9)
                    for i in range(3):
                        r = VROWS if i == 0 else DROWS
                        ins = turn(ps[:, ACC + 3, i * P:i * P + r], rows[0:r, i, :])
                    ins.then_inc(S("cols"), 1)

                wide_by_tile(W_IN_WIDE[0], ACC, turn_rows)
                lows[0] += 4
                pe.wait_ge(S("cols_read"), 1)
                for j, (k, kn) in enumerate(TALL_K):
                    tall(FIRST["w_in_tall"] + j, ACC, act_hl, k, j == 0, j == 2, kn, A_COLS)
                for b in (1, 2):
                    pe.wait_ge(S("wide_read"), b)
                    for h in range(2):
                        wide(W_IN_WIDE[b] + h, UP, 4 * h, act_hl, h == 0, h == 1, 4, 512)
                    if b == 1:
                        pe.wait_ge(S("kpe"), 1)
                        for i, (k, kn) in enumerate(((0, 2), (2, 2), (4, 1))):
                            for kk in range(k, k + kn):
                                for m in range(M):
                                    pe.wait_ge(S("lat_normed"), m + 1)
                                    ins = turn(turned(ACC, kk, 1)[:, 0, m * P:(m + 1) * P],
                                               lat[:, m, kk * P:(kk + 1) * P])
                            ins.then_inc(S("lat_turned"), 1)
                for j, (k, kn) in enumerate(UQ_K):
                    if j == 0:
                        pe.wait_ge(S("lat_lo"), 3)
                    tall(FIRST["w_uq"] + j, ACC, hl2, k, j == 0, j == 1, kn, NH * QKD)
                pe.wait_ge(S("wide_read"), 3)
                tall(FIRST["w_ukv"], UP, hl2, 3, True, True, 2, 1024)
                pe.wait_ge(S("q_nope"), 2)
                pe.wait_ge(S("q_rope"), 2)
                for h in range(NH):
                    for m in range(M):
                        ins = turn(ps[0:QKD, ACC + h // 2, (h % 2) * T + m * P:(h % 2) * T + (m + 1) * P], qf[:, m, h, :])
                    if h % 2:
                        ins.then_inc(S("q_turned"), 1)
                pe.wait_ge(S("kv_nope"), 2)
                for h in range(NH):
                    for m in range(M):
                        ins = turn(ps[0:QKD, UP + h // 2, (h % 2) * T + m * P:(h % 2) * T + (m + 1) * P], kf[:, m, h, :])
                    if h % 2:
                        ins.then_inc(S("k_turned"), 1)
                pe.wait_ge(S("qT"), 4)
                def probs_times_v(h):
                    if h == 0:
                        pe.wait_ge(S("kT"), 4)
                    pe.wait_ge(S("probT"), h + 1)
                    if h % 2 == 0 and h >= 4:
                        need_lows(5 + h // 2 - 1)
                    r = 64 * (h % 2)
                    for k in range(M):
                        ins = mm(ps[r:r + 64, 4 + (h // 2) % 2, 0:T], v1[:, k, h, :], probT[h % 2][:, k, :],
                                 k == 0, k == 1)
                    ins.then_inc(S("pv"), 1)

                for t in range(NH + 2):
                    if t < NH:
                        if t % 2 == 0:
                            pe.wait_ge(S("kT"), t // 2 + 1)
                        if t >= 2:
                            pe.wait_ge(S("probs_exp"), t - 1)
                        for m in range(M):
                            ins = mm(ps[:, t % 2, m * T:(m + 1) * T], qT[0:QKD, t, m * P:(m + 1) * P], kT1[0:QKD, t, :],
                                     True, True)
                        ins.then_inc(S("scores"), 1)
                    if t >= 2:
                        h = t - 2
                        if h >= 2:
                            pe.wait_ge(S("probT"), h - 1)
                        for m in range(M):
                            pe.wait_ge(S("probs"), 2 * h + m + 1)
                            for k in range(M):
                                ins = turn(ps[:, 2 + h % 2, k * T + m * P:k * T + (m + 1) * P],
                                           prob[h % 3][:, m, k * P:(k + 1) * P])
                        ins.then_inc(S("probs_turned"), 1)
                    if t >= 3:
                        probs_times_v(t - 3)
                pe.wait_ge(S("probT"), NH)
                need_lows(5)
                tall(FIRST["w_out"], ACC, act_hl, 0, True, False, 2, 1024)
                probs_times_v(NH - 1)
                tall_by_tile(FIRST["w_out"] + 1, [(act_hl, 2), (act_hl, 4), (act_hl, 6)],
                             waits=[None, ("act_lo", 9), None])
                turn_m(ACC, 0)
                lows[0] = 9

                def mlp(n0, s):
                    blocks = MLP_BLOCKS * s
                    wide_by_tile(n0, ACC, out=True)
                    lows[0] += 4

                    def up(n, i, per, turn_=None):
                        free = ("hidden", 2 * blocks + 2 * i + 1, 2 * blocks + 2 * i + 2)
                        for h in range(2):
                            wide(n + h, UP, 4 * h, act_hl, h == 0, h == 1, 4, 512, i if turn_ is None else turn_, per,
                                 read=free if h == 0 else None, out=h == 1)

                    def down(n, i, per, first):
                        for h in range(2):
                            tall(n + h, ACC, hl2, 2 * h, first and h == 0, False, 2, 1024, i, per)

                    up(n0 + 2, 0, 0)
                    pe.wait_ge(S("hid_lo"), 2 * blocks + 2)
                    down(n0 + 4, 0, 0, True)
                    with pe.Fori(1, MLP_BLOCKS - 2) as i:
                        up(n0 + 2, i, 4)
                        pe.wait_ge(S("hid_lo"), 2 * i + 2 * blocks + 2)
                        down(n0 + 4, i, 4, False)
                    last = MLP_BLOCKS - 1
                    up(n0 + 2 + 4 * (last - 1), last - 1, 0, 0)
                    done = 2 * blocks + 2 * last
                    pe.wait_ge(S("hid_lo"), done)
                    tall(n0 + 4 * last, ACC, hl2, 0, False, False, 2, 1024)
                    tall_by_tile(n0 + 4 * last + 1, [(hl2, 2), (act_hl, 0), (act_hl, 2)],
                                 waits=[None, ("hid_lo", done + 1), ("hid_lo", done + 2)])
                    turn_m(TURN_BANK[2 * s + 2], 0)

                mlp(FIRST["mlp0"], 0)
                wide_by_tile(FIRST["pw1"], ACC)
                for b in range(1, 4):
                    if b >= 2:
                        pe.wait_ge(S("ag"), 4 * (b - 1))
                    for h in range(2):
                        wide(FIRST["pw1"] + 2 * b + h, (UP, ACC)[b % 2], 4 * h, act_hl, h == 0, h == 1, 4, 512)
                lows[0] += 4
                pe.wait_ge(S("ag"), 12)
                for i, (c, t) in enumerate(PE_TAPS):
                    last = i + 1 == len(PE_TAPS) or PE_TAPS[i + 1][0] != c
                    if t == 0:
                        pe.wait_ge(S("u"), c // 2 + 1)
                    pe.wait_ge(S("diag"), i + 1)
                    mm(ps[:, UP + c - 4, 0:T], diag[:, i % DIAGS, :], upad[:, c, t:t + T], t == 0, last)\
                        .then_inc(S("diag_used"), 1)
                pe.wait_ge(S("ag"), 16)
                pe.wait_ge(S("conv_act"), 4)
                pe.wait_ge(S("conv_dve"), 1)
                pe.wait_ge(S("conv_pool"), 1)
                for m in range(M):
                    for c in range(KD):
                        ins = turn(tall_out(ACC, m)[:, c * P:(c + 1) * P], cv[:, c, m * P:(m + 1) * P])
                    ins.then_inc(S("cv_turned"), 1)
                turn_normed(UP)
                pe.wait_ge(S("ones"), 1)
                pe.wait_ge(S("b_pw2"), 16)
                for m in range(M):
                    for h in range(2):
                        mm(ps[:, ACC + 2 * m + h, :], ones[:, :], brow[0:1, 512 * h:512 * h + 512], True, False)
                need_lows(lows[0] + 1)
                tall(FIRST["pw2"], ACC, act_hl, 0, False, False, 2, 1024)
                tall_by_tile(FIRST["pw2"] + 1, [(act_hl, 2), (act_hl, 4), (act_hl, 6)],
                             waits=[("act_lo", lows[0] + j) for j in (2, 3, 4)])
                lows[0] += 4
                turn_m(ACC, 0)
                mlp(FIRST["mlp1"], 1)

                n = FIRST["w_in_2"]
                for m in range(M):
                    if m == 1:
                        turn_m(UP, 1)
                    for j in range(4):
                        need_lows(lows[0] + 2 * m + j // 2 + 1)
                        tall(n + j, ACC, act_hl, 2 * j, j == 0, j == 3, 2, 792, tiles=(m,), free=m == 1)
                lows[0] += 4
                for j in range(4):
                    tall(n + 4 + j, UP, act_hl, 2 * j, j == 0, j == 3, 2, 1024)
                pe.wait_ge(S("roped"), 1)
                pe.wait_ge(S("gate_e"), 1)
                kd = tok2.rearrange("p (m a n) -> p m a n", m=2, a=8)
                for q in range(8):
                    for m in range(M):
                        ins = turn(ps[:, ACC + q // 2, (q % 2) * T + m * P:(q % 2) * T + (m + 1) * P], kd[:, m, q, :])
                    if q % 2:
                        ins.then_inc(S("kd_turned"), 1)
                for m in range(M):
                    pe.wait_ge(S("kT2"), 2 * m + 2)
                    for j in range(4):
                        ins = tall(n + 8 + j, ACC, act_hl, 2 * j, j == 0, j == 3, 2, 1024, tiles=(m,), free=m == 1)
                    if m == 0:
                        ins.then_inc(S("dv_nq_tile"), 1)
                f2 = hl2[:, :, :].rearrange("p a b -> p (a b)")[:, 0:1920].rearrange("p (j n) -> p j n", j=32)
                pe.wait_ge(S("flat_lo"), 1)
                for a_ in range(2):
                    pe.wait_ge(S("nq_roped"), a_ + 1)
                    pe.wait_ge(S("dv"), a_ + 1)
                    for h in range(2):
                        n = FIRST["cmp"] + 2 * a_ + h
                        arrived(n)
                        for kk in range(8):
                            high, low = (f2[:, 16 * a_ + 8 * h + kk, 30 * i:30 * i + 30] for i in range(2))
                            for i, (lt, w) in enumerate(((high, w_hi), (high, w_lo), (low, w_hi))):
                                ins = mm(ps[0:30, ACC + 2 * a_, 0:256], lt, piece_of(w, n)[:, kk, :],
                                         h == 0 and kk == 0 and i == 0, h == 1 and kk == 7 and i == 2)
                        ins.then_inc(S("pe_piece"), 1)
                pe.wait_ge(S("roped"), 2)
                tk = tok2.rearrange("p (m h d) -> p m h d", m=2, h=8)
                for h in range(8):
                    for m in range(M):
                        ins = turn(ps[:, UP + h // 2, (h % 2) * T + m * P:(h % 2) * T + (m + 1) * P], tk[:, m, h, :])
                    if h % 2:
                        ins.then_inc(S("dqk_turned"), 1)
                pe.wait_ge(S("hid"), 2)
                for a_ in range(2):
                    for c in range(2):
                        at = 60 * a_ + 30 * c
                        ins = turn(ps[:, ACC + 3, at:at + 30], hid[:, a_, c * P:(c + 1) * P])
                ins.then_inc(S("hid_turned"), 1)
                for h in range(4):
                    if h % 2 == 0:
                        pe.wait_ge(S("dqkT"), h // 2 + 1)
                    for m in range(M):
                        ins = turn(ps[:, UP + h // 2, (h % 2) * T + m * P:(h % 2) * T + (m + 1) * P],
                                   nqt[:, m, h * P:(h + 1) * P])
                    if h % 2:
                        ins.then_inc(S("nq_turned"), 1)

                spans = ((0, 128), (128, 256))

                def causal_scores(bank, q, key):
                    for m, (c0, w) in enumerate(spans):
                        mm(ps[:, bank, c0:c0 + w], q[:, m * P:(m + 1) * P], key[:, 0:w], True, False)
                        ins = mm(ps[:, bank, c0 + w - P:c0 + w], ident, causal, False, True)
                    return ins

                def turn_probs(bank, p):
                    turn(ps[:, bank, 0:128], p[:, 0:128])
                    turn(ps[:, bank, 128:256], p[:, 128:256])
                    return turn(ps[:, bank, 256:384], p[:, 256:384])

                def scores_of(u):
                    if u == 0:
                        pe.wait_ge(S("dqkT"), 4)
                    if u >= 2:
                        pe.wait_ge(S("att_exp"), u - 1)
                    for j in range(2):
                        if u < DH:
                            q, key = dqkT[64 * j:64 * j + 64, u, :], dqkT[64 * j:64 * j + 64, 4 + u, :]
                        else:
                            h = u - DH
                            r = 64 * (h % 2)
                            q, key = nqT[r:r + 64, h // 2, :], kT2[r:r + 64, 1 + j, h // 4, :]
                        ins = causal_scores(2 * (u % 2) + j, q, key)
                    ins.then_inc(S("att_scores"), 1)

                def turn_of(u):
                    pe.wait_ge(S("att_probs"), u + 1)
                    if u < DH:
                        if u >= 2:
                            pe.wait_ge(S("att_pT"), u - 1)
                        ins = turn_probs(4 + u % 2, p2[u % 2][:, 0, :])
                    else:
                        pe.wait_ge(S("att_pT"), u)
                        if u == DH:
                            pe.wait_ge(S("pcT"), 1)
                        for j in range(2):
                            ins = turn_probs(4 + j, p2[u % 2][:, j, :])
                    ins.then_inc(S("att_turned"), 1)

                def out_of(u):
                    pe.wait_ge(S("att_pT"), u + 1)
                    if u < DH:
                        if u == 0:
                            pe.wait_ge(S("cscores_read"), 1)
                        if u >= 2:
                            pe.wait_ge(S("od"), u - 1)
                        pt = pt2[u % 2][:, 0, :]
                        o = ps[:, 6 + u % 2, :]
                        mm(o[:, 0:128], pt[:, 0:128], dv[:, 0, u * P:(u + 1) * P], True, True)
                        mm(o[:, 128:256], pt[:, 128:256], dv[:, 0, u * P:(u + 1) * P], True, False)
                        ins = mm(o[:, 128:256], pt[:, 256:384], dv[:, 1, u * P:(u + 1) * P], False, True)
                    else:
                        h = u - DH
                        if h in (0, 2):
                            pe.wait_ge(S("od"), 3 + h // 2)
                        if h % 2 == 0 and h >= 4:
                            need_lows(lows[0] + h // 2 - 1)
                        r, g = 64 * (h % 2), h // 4
                        o = ps[r:r + 64, 6 + (h // 2) % 2, :]
                        mm(o[:, 0:T], vsel[:, h, :], pcT, True, False)
                        for j in range(2):
                            pt = pt2[h % 2][:, j, :]
                            mm(o[:, 0:T], vsw[:, 0, j, 64 * g:64 * g + 64], pt[:, 0:256], False, False)
                            ins = mm(o[:, P:T], vsw[:, 1, j, 64 * g:64 * g + 64], pt[:, 256:384], False, j == 1)
                    ins.then_inc(S("att_out"), 1)

                def compressed_kv():
                    pe.wait_ge(S("hidc"), 1)
                    pe.wait_ge(S("small"), 16 * 12)
                    for c in range(2):
                        mm(ps[:, UP + 2, 0:30], w2k[:, c, :, :].rearrange("p u d -> p (u d)"), hidc[:, c, :],
                           c == 0, c == 1)
                    for c in range(2):
                        ins = mm(ps[:, UP + 3, 0:64], hidrep[:, c].rearrange("p h n -> p (h n)"), w2v[:, c, :],
                                 c == 0, c == 1)
                    ins.then_inc(S("cmp_kv"), 1)

                def compressed_scores():
                    pe.wait_ge(S("kcT"), 1)
                    pe.wait_ge(S("vsel"), 1)
                    pe.wait_ge(S("nqT"), 2)
                    for h in range(NH):
                        r, g = 64 * (h % 2), h // 4
                        for m in range(M):
                            c = (h // 2) * 32 + m * 16
                            ins = mm(ps[:, UP + 2 + h % 2, c:c + 15], nqT[r:r + 64, h // 2, m * P:(m + 1) * P],
                                     kcT[r:r + 64, 15 * g:15 * g + 15], True, True)
                    ins.then_inc(S("cscores"), 1)

                for t in range(DH + NH + 1):
                    if t < DH + NH:
                        scores_of(t)
                    if t == 0:
                        compressed_kv()
                    if t == 1:
                        compressed_scores()
                    if t == DH + NH:
                        pe.wait_ge(S("o_normed"), 1)
                        pe.wait_ge(S("att_exp"), t - 1)
                        for h in range(DH):
                            for m in range(M):
                                ins = turn(turned(ACC, h, 1)[:, 0, m * P:(m + 1) * P], od[:, 2 * h + m, :])
                            if h % 2:
                                ins.then_inc(S("turned"), 1)
                    if t >= 2:
                        out_of(t - 2)
                    if t >= 1:
                        turn_of(t - 1)
                    if t == DH:
                        pe.wait_ge(S("pcm"), 1)
                        for m in range(M):
                            ins = turn(ps[:, UP, m * P:(m + 1) * P], pcm[:, m].rearrange("p h n -> p (h n)"))
                        ins.then_inc(S("pcm_turned"), 1)
                need_lows(lows[0] + 5)
                tall(FIRST["w_out_2"], ACC, act_hl, 0, True, False, 2, 1024)
                out_of(DH + NH - 1)
                lows[0] += 6
                tall_by_tile(FIRST["w_out_2"] + 1, [(act_hl, 2), (act_hl, 4), (act_hl, 6)],
                             waits=[None, ("act_lo", lows[0]), None])
                turn_m(ACC, 0)

                f0 = FIRST["ffn"]

                def gate_up(n, i, per):
                    free = ("ff_sum", 2 * i + 1, 2 * i + 2)
                    for h in range(2):
                        wide(n + h, UP, 4 * h, act_hl, h == 0, h == 1, 4, 512, i, per,
                             read=free if h == 0 else None, out=h == 1)

                wide_by_tile(f0, ACC, out=True)
                gate_up(f0 + 2, 0, 0)
                pe.wait_ge(S("ff_lo"), 1)
                tall(f0 + 4, ACC, hl2, 0, True, False, 2, 1024)
                with pe.Fori(1, FF_BLOCKS - 1) as i:
                    gate_up(f0 + 2, i, 3)
                    pe.wait_ge(S("ff_lo"), i + 1)
                    tall(f0 + 4, ACC, hl2, 0, False, False, 2, 1024, i, 3)
                pe.wait_ge(S("ff_lo"), FF_BLOCKS)
                tall_by_tile(N_PIECES - 1, [(act_hl, 0)])


def kernel(**inputs):
    import numpy as _np
    import concourse.bacc as _bacc
    from concourse import mybir as _mybir
    from concourse.bass_utils import run_bass_kernel_spmd as _run

    nc = _bacc.Bacc("TRN2", target_bir_lowering=False, num_devices=1)
    arrays = {name: _np.ascontiguousarray(v) for name, v in inputs.items()}
    arrays["shape_constants"] = shape_constants()
    aps = {name: nc.dram_tensor(f"in_{name}", v.shape, _mybir.dt.from_np(v.dtype), kind="ExternalInput").ap()
           for name, v in arrays.items()}
    result = nc.dram_tensor("result", (1, T, D), _mybir.dt.float32, kind="ExternalOutput").ap()
    two_blocks(nc, aps, result)
    r = _run(nc, [{f"in_{name}": v for name, v in arrays.items()}], core_ids=[0])
    return r.results[0]["result"]
```
